# Optimizing a Trainium2 kernel written in Bass

```python
import jax, jax.numpy as jnp
from jax import lax
import numpy as np

D_MODEL = 1024
BATCH = 1
SEQ = 2048
DEPTH = 1
DEC_BATCH = 8
DEC_SEQ = 4
PAST_LEN = 2048
PAGE_SIZE = 128

D_MIX = 1024
N_HEADS = 8
NOPE_DIM = 64
ROPE_DIM = 32
V_DIM = 64
Q_RANK = 256
KV_RANK = 128
ATT_W = N_HEADS * V_DIM
POOL_WINDOWS = (2, 4, 8, 16)
POOL_GROUPS = len(POOL_WINDOWS)
POOL_W = 256
POOL_GW = POOL_W // POOL_GROUPS
POOL_HIST = max(POOL_WINDOWS) - 1
CONV_W = D_MIX - ATT_W - POOL_W
CONV_K = 31
CONV_HIST = CONV_K - 1
IN_COLS = Q_RANK + KV_RANK + ROPE_DIM + POOL_W + 2 * CONV_W + D_MIX
SPLIT_AT = (Q_RANK,
            Q_RANK + KV_RANK,
            Q_RANK + KV_RANK + ROPE_DIM,
            Q_RANK + KV_RANK + ROPE_DIM + POOL_W,
            Q_RANK + KV_RANK + ROPE_DIM + POOL_W + 2 * CONV_W)
ATT_SCALE = (NOPE_DIM + ROPE_DIM) ** -0.5
ROPE_THETA = 10000.0
Q_BLOCK = 128
EPS = 1e-6

kernel_name = 'hymba_mla_pool_conformer_decode_step'

def rms_norm(x, g):
    xf = x.astype(jnp.float32)
    y = xf * lax.rsqrt(jnp.mean(xf * xf, axis=-1, keepdims=True) + EPS)
    return (y * g.astype(jnp.float32)).astype(x.dtype)

def rope_tables(pos):
    inv = ROPE_THETA ** (-jnp.arange(0, ROPE_DIM, 2, dtype=jnp.float32) / ROPE_DIM)
    ang = pos.astype(jnp.float32)[:, None] * inv[None, :]
    return jnp.cos(ang), jnp.sin(ang)

def apply_rope(x, cos, sin):
    xf = x.astype(jnp.float32)
    x1, x2 = jnp.split(xf, 2, axis=-1)
    return jnp.concatenate([x1 * cos - x2 * sin, x1 * sin + x2 * cos], axis=-1).astype(x.dtype)

def mla_scores(q_abs, q_rope, ckv, krope):
    s = (jnp.einsum('bqhr,bkr->bhqk', q_abs, ckv, preferred_element_type=jnp.float32)
         + jnp.einsum('bqhd,bkd->bhqk', q_rope, krope, preferred_element_type=jnp.float32))
    return s * ATT_SCALE

def attend_prompt(q_abs, q_rope, ckv, krope, pos):
    B, L = q_abs.shape[:2]
    nb = L // Q_BLOCK
    qa = q_abs.reshape(B, nb, Q_BLOCK, N_HEADS, KV_RANK).swapaxes(0, 1)
    qr = q_rope.reshape(B, nb, Q_BLOCK, N_HEADS, ROPE_DIM).swapaxes(0, 1)
    qp = pos.reshape(nb, Q_BLOCK)

    def block(args):
        qa_b, qr_b, qp_b = args
        s = mla_scores(qa_b, qr_b, ckv, krope)
        s = jnp.where(pos[None, :] <= qp_b[:, None], s, -jnp.inf)
        p = jax.nn.softmax(s, axis=-1).astype(ckv.dtype)
        return jnp.einsum('bhqk,bkr->bqhr', p, ckv)

    o = lax.map(block, (qa, qr, qp))
    return o.swapaxes(0, 1).reshape(B, L, N_HEADS, KV_RANK)

def attend_sample(q_abs, q_rope, ckv_past, krope_past, ckv_new, krope_new):
    L = q_abs.shape[1]
    s_past = mla_scores(q_abs, q_rope, ckv_past, krope_past)
    s_new = mla_scores(q_abs, q_rope, ckv_new, krope_new)
    causal = jnp.arange(L)[None, :] <= jnp.arange(L)[:, None]
    s_new = jnp.where(causal, s_new, -jnp.inf)
    p = jax.nn.softmax(jnp.concatenate([s_past, s_new], axis=-1), axis=-1).astype(ckv_new.dtype)
    P = s_past.shape[-1]
    return (jnp.einsum('bhqk,bkr->bqhr', p[..., :P], ckv_past)
            + jnp.einsum('bhqk,bkr->bqhr', p[..., P:], ckv_new))

def pool_mix(u_ext, pos, pool_w, pool_scale):
    B, T, C = u_ext.shape
    L = T - POOL_HIST
    uf = u_ext.astype(jnp.float32).reshape(B, T, POOL_GROUPS, POOL_GW)
    cs = jnp.concatenate([jnp.zeros((B, 1, POOL_GROUPS, POOL_GW), jnp.float32),
                          jnp.cumsum(uf, axis=1)], axis=1)
    cur = uf[:, POOL_HIST:]
    end = cs[:, POOL_HIST + 1:]
    outs = []
    for gi, w in enumerate(POOL_WINDOWS):
        start = cs[:, POOL_HIST + 1 - w: POOL_HIST + 1 - w + L, gi]
        cnt = jnp.minimum(pos + 1, w).astype(jnp.float32)[None, :, None]
        outs.append((end[:, :, gi] - start) / cnt - cur[:, :, gi])
    d = jnp.stack(outs, axis=2)
    y = jnp.einsum('blgc,gcd->blgd', d, pool_w.astype(jnp.float32)).reshape(B, L, C)
    return (y * pool_scale.astype(jnp.float32)).astype(u_ext.dtype)

def conv_module(a_ext, dw, db, ln_g, ln_b, pw):
    C = a_ext.shape[-1]
    y = lax.conv_general_dilated(a_ext, dw[:, None, :], window_strides=(1,), padding='VALID',
                                 dimension_numbers=('NWC', 'WIO', 'NWC'),
                                 feature_group_count=C) + db
    yf = y.astype(jnp.float32)
    mu = jnp.mean(yf, axis=-1, keepdims=True)
    var = jnp.mean(jnp.square(yf - mu), axis=-1, keepdims=True)
    yn = (yf - mu) * lax.rsqrt(var + EPS) * ln_g.astype(jnp.float32) + ln_b.astype(jnp.float32)
    return jax.nn.silu(yn).astype(a_ext.dtype) @ pw

def layer(x, pos, p, attend, pool_prev, conv_prev):
    B, L, _ = x.shape
    h = rms_norm(x, p['norm_pre'])
    z = h @ p['w_in']
    c_q, c_kv, k_r, u_pool, u_conv, gate = jnp.split(z, SPLIT_AT, axis=-1)
    cos, sin = rope_tables(pos)
    c_q = rms_norm(c_q, p['q_norm'])
    q = (c_q @ p['w_uq']).reshape(B, L, N_HEADS, NOPE_DIM + ROPE_DIM)
    q_nope = q[..., :NOPE_DIM]
    q_rope = apply_rope(q[..., NOPE_DIM:], cos[:, None, :], sin[:, None, :])
    c_kv = rms_norm(c_kv, p['kv_norm'])
    k_r = apply_rope(k_r, cos, sin)
    q_abs = jnp.einsum('blhd,rhd->blhr', q_nope, p['w_uk'])
    o_lat = attend(q_abs, q_rope, c_kv, k_r)
    o_att = jnp.einsum('blhr,rhd->blhd', o_lat, p['w_uv']).reshape(B, L, ATT_W)
    pool_ext = jnp.concatenate([pool_prev, u_pool], axis=1)
    y_pool = pool_mix(pool_ext, pos, p['pool_w'], p['pool_scale'])
    a = u_conv[..., :CONV_W] * jax.nn.sigmoid(u_conv[..., CONV_W:])
    conv_ext = jnp.concatenate([conv_prev, a], axis=1)
    y_conv = conv_module(conv_ext, p['conv_dw'], p['conv_b'], p['conv_ln_g'], p['conv_ln_b'], p['conv_pw'])
    mixed = jnp.concatenate([o_att, y_pool, y_conv], axis=-1) * jax.nn.silu(gate)
    out = rms_norm(mixed @ p['w_out'], p['norm_post'])
    return (x + out, c_kv, k_r, pool_ext[:, -POOL_HIST:], conv_ext[:, -CONV_HIST:])

def setup_inputs(seed: int = 0) -> dict:
    key = jax.random.key(seed)
    ks = jax.random.split(key, 32)
    f32 = jnp.float32
    n_pages = PAST_LEN // PAGE_SIZE
    n_used = DEC_BATCH * n_pages
    n_phys = n_used + max(1, n_used // 4)

    def nrm(k, shape, scale=1.0):
        return scale * jax.random.normal(k, shape, f32)

    def gain(k, shape):
        return 1.0 + 0.1 * jax.random.normal(k, shape, f32)

    page_table = jax.random.permutation(ks[4], n_phys)[:n_used].reshape(DEC_BATCH, n_pages).astype(jnp.int32)
    return {
        'x_prompt': nrm(ks[0], (BATCH, SEQ, D_MODEL)),
        'x_sample': nrm(ks[1], (DEC_BATCH, DEC_SEQ, D_MODEL)),
        'cache_ckv': nrm(ks[2], (DEPTH, n_phys, PAGE_SIZE, KV_RANK)),
        'cache_krope': nrm(ks[3], (DEPTH, n_phys, PAGE_SIZE, ROPE_DIM)),
        'page_table': page_table,
        'state_pool': nrm(ks[5], (DEPTH, DEC_BATCH, POOL_HIST, POOL_W)),
        'state_conv': nrm(ks[6], (DEPTH, DEC_BATCH, CONV_HIST, CONV_W), 0.5),
        'norm_pre': gain(ks[7], (DEPTH, D_MODEL)),
        'w_in': nrm(ks[8], (DEPTH, D_MODEL, IN_COLS), D_MODEL ** -0.5),
        'q_norm': gain(ks[9], (DEPTH, Q_RANK)),
        'w_uq': nrm(ks[10], (DEPTH, Q_RANK, N_HEADS * (NOPE_DIM + ROPE_DIM)), Q_RANK ** -0.5),
        'kv_norm': gain(ks[11], (DEPTH, KV_RANK)),
        'w_uk': nrm(ks[12], (DEPTH, KV_RANK, N_HEADS, NOPE_DIM), KV_RANK ** -0.5),
        'w_uv': nrm(ks[13], (DEPTH, KV_RANK, N_HEADS, V_DIM), KV_RANK ** -0.5),
        'pool_w': nrm(ks[14], (DEPTH, POOL_GROUPS, POOL_GW, POOL_GW), POOL_GW ** -0.5),
        'pool_scale': gain(ks[15], (DEPTH, POOL_W)),
        'conv_dw': nrm(ks[16], (DEPTH, CONV_K, CONV_W), CONV_K ** -0.5),
        'conv_b': nrm(ks[17], (DEPTH, CONV_W), 0.02),
        'conv_ln_g': gain(ks[18], (DEPTH, CONV_W)),
        'conv_ln_b': nrm(ks[19], (DEPTH, CONV_W), 0.02),
        'conv_pw': nrm(ks[20], (DEPTH, CONV_W, CONV_W), CONV_W ** -0.5),
        'w_out': nrm(ks[21], (DEPTH, D_MIX, D_MODEL), D_MIX ** -0.5),
        'norm_post': gain(ks[22], (DEPTH, D_MODEL)),
    }

def reference(x_prompt, x_sample, cache_ckv, cache_krope, page_table, state_pool, state_conv,
              norm_pre, w_in, q_norm, w_uq, kv_norm, w_uk, w_uv, pool_w, pool_scale,
              conv_dw, conv_b, conv_ln_g, conv_ln_b, conv_pw, w_out, norm_post):
    Bp, Lp, _ = x_prompt.shape
    Bs, Ls, _ = x_sample.shape
    past = page_table.shape[1] * PAGE_SIZE
    pos_p = jnp.arange(Lp, dtype=jnp.int32)
    pos_s = past + jnp.arange(Ls, dtype=jnp.int32)
    hp, hs = x_prompt, x_sample
    ckv_p, kr_p, pool_p, conv_p = [], [], [], []
    ckv_s, kr_s, pool_s, conv_s = [], [], [], []
    for l in range(DEPTH):
        p = {'norm_pre': norm_pre[l], 'w_in': w_in[l], 'q_norm': q_norm[l], 'w_uq': w_uq[l],
             'kv_norm': kv_norm[l], 'w_uk': w_uk[l], 'w_uv': w_uv[l], 'pool_w': pool_w[l],
             'pool_scale': pool_scale[l], 'conv_dw': conv_dw[l], 'conv_b': conv_b[l],
             'conv_ln_g': conv_ln_g[l], 'conv_ln_b': conv_ln_b[l], 'conv_pw': conv_pw[l],
             'w_out': w_out[l], 'norm_post': norm_post[l]}
        pool0 = jnp.zeros((Bp, POOL_HIST, POOL_W), x_prompt.dtype)
        conv0 = jnp.zeros((Bp, CONV_HIST, CONV_W), x_prompt.dtype)
        attend_p = lambda qa, qr, ck, kr: attend_prompt(qa, qr, ck, kr, pos_p)
        hp, a1, a2, a3, a4 = layer(hp, pos_p, p, attend_p, pool0, conv0)
        ckv_p.append(a1); kr_p.append(a2); pool_p.append(a3); conv_p.append(a4)
        ckv_past = cache_ckv[l][page_table].reshape(Bs, past, KV_RANK)
        kr_past = cache_krope[l][page_table].reshape(Bs, past, ROPE_DIM)
        attend_s = lambda qa, qr, ck, kr: attend_sample(qa, qr, ckv_past, kr_past, ck, kr)
        hs, b1, b2, b3, b4 = layer(hs, pos_s, p, attend_s, state_pool[l], state_conv[l])
        ckv_s.append(b1); kr_s.append(b2); pool_s.append(b3); conv_s.append(b4)
    return (hp, hs,
            jnp.stack(ckv_p), jnp.stack(kr_p), jnp.stack(pool_p), jnp.stack(conv_p),
            jnp.stack(ckv_s), jnp.stack(kr_s), jnp.stack(pool_s), jnp.stack(conv_s))


_drawn_inputs = setup_inputs


def setup_inputs(seed=0):
    import zlib

    import numpy as np

    out = dict(_drawn_inputs(seed))
    spreads = {}
    factors = {'cache_krope': 3.063, 'q_norm': 5.24, 'conv_b': 3.694, 'conv_ln_b': 6.494}
    for name, (base, spread) in spreads.items():
        noise = np.random.default_rng([zlib.crc32(name.encode()), seed]).standard_normal(out[name].shape)
        drawn = base * np.exp(spread * noise) if base else spread * noise
        out[name] = __import__('jax').numpy.asarray(drawn.astype(out[name].dtype))
    for name, factor in factors.items():
        out[name] = (out[name] * factor).astype(out[name].dtype)
    return out
```

```python
from contextlib import ExitStack

import concourse.bass as bass
from concourse import mybir
from concourse.alu_op_type import AluOpType as ALU

F32 = mybir.dt.float32
F32R = mybir.dt.float32r
BF16 = mybir.dt.bfloat16
I32 = mybir.dt.int32
ACT = mybir.ActivationFunctionType
AXX = mybir.AxisListType.X

P = 128
D_MODEL, D_MIX = 1024, 1024
SEQ, DEC_BATCH, DEC_SEQ = 2048, 8, 4
SAMPLES = DEC_BATCH * DEC_SEQ
HEADS, NOPE, ROPE, VDIM = 8, 64, 32, 64
HALF = ROPE // 2
Q_RANK, KV_RANK = 256, 128
POOL_W, CONV_W = 256, 256
POOL_HIST, CONV_K = 15, 31
CONV_HIST = CONV_K - 1
ATT_W = HEADS * VDIM
PAGE, N_PAGES = 128, 16
EPS = 1e-6

GROUP = 512
TILES = GROUP // P
GROUPS = SEQ // GROUP
KC = D_MODEL // P
TOK_COLS = Q_RANK + KV_RANK + ROPE
IN1 = TOK_COLS + 2 * CONV_W + POOL_W
QC, CC = Q_RANK // P, CONV_W // P
UH = POOL_HIST + 1
PASSES = ((0, 0), (1, 0), (0, 1))
N_COLS = 10 + 10 + CC * CONV_K


def f32(ap):
    return ap.bitcast(F32)


def spread(col, ap):
    if len(ap.shape) == 3:
        col = col.rearrange("p (a b) -> p a b", a=1)
    if len(ap.shape) == 4:
        col = col.rearrange("p (a b c) -> p a b c", a=1, b=1)
    return col.broadcast_to(list(ap.shape))


class Banks:

    def __init__(self, sem, name, tensors, per_group):
        self.t, self.n = tensors, len(tensors)
        self.per = per_group // self.n
        self.done = [sem(f"{name}_done{b}") for b in range(self.n)]
        self.free = [sem(f"{name}_free{b}") for b in range(self.n)]

    def count(self, it, job):
        return it * self.per + job // self.n + 1

    def wait_free(self, eng, it, job):
        eng.wait_ge(self.free[job % self.n], self.count(it, job))
        return self.t[job % self.n]

    def wait_done(self, eng, it, job):
        eng.wait_ge(self.done[job % self.n], self.count(it, job))
        return self.t[job % self.n]


def stage1(nc, a, keep):
    ctx = ExitStack()
    with ctx:
        def sb(name, shape, dt=F32):
            return ctx.enter_context(nc.sbuf_tensor(name, shape, dt))

        def sem(name):
            sems.append(nc.alloc_semaphore("s1_" + name))
            return sems[-1]

        sems = keep["stage1_sems"] = []
        ident, rstd_all = keep["ident"], keep["rstd_all"]
        w_in = sb("w_in", [P, 2, KC, IN1], F32R)
        w_uq = sb("w_uq", [P, 2, QC, HEADS * P], F32R)
        w_uk = sb("w_uk", [P, 2, HEADS * NOPE], F32R)
        w_uv = sb("w_uv", [P, 2, HEADS * VDIM], F32R)
        cols = sb("cols", [P, N_COLS])
        g_pre, g_q = cols[:, 0:8], cols[:, 8:10]
        pool_s, ln_g, ln_b = cols[:, 10:12], cols[:, 12:14], cols[:, 14:16]
        conv_b, inv_w = cols[:, 16:18], cols[:, 18:20]
        dw = cols[:, 20:].rearrange("p (c k) -> p c k", c=CC)
        g_kv = sb("g_kv", [P, KV_RANK])
        half, eps = sb("half", [P, 2 * TILES]), sb("eps", [P, 2 * TILES])
        zero, inv_rank = sb("zero", [P, 1]), sb("inv_rank", [P, 2 * TILES])

        load, w_hi, w_lo = sem("load"), sem("w_hi"), sem("w_lo")
        staged = [sem(f"staged{i}") for i in range(2)]
        parts = [(a["w_in"][k * P:(k + 1) * P, :], w_in[:, 0, k, :], w_in[:, 1, k, :], g_pre[:, k:k + 1])
                 for k in range(KC)]
        parts += [(a["w_uq"][k * P:(k + 1) * P, :], w_uq[:, 0, k, :], w_uq[:, 1, k, :], g_q[:, k:k + 1])
                  for k in range(QC)]
        parts += [(a["w_uk"], w_uk[:, 0, :], w_uk[:, 1, :], 1.0), (a["w_uv"], w_uv[:, 0, :], w_uv[:, 1, :], 1.0)]
        with nc.sbuf_tensor("stage", [P, 2, IN1], F32) as stage, nc.Block() as block:
            @block.sync
            def _(sp):
                sp.dma_start(cols[:, :], a["cols"]).then_inc(load, 16)
                sp.dma_start(g_kv[:, :], a["kv_norm"].broadcast_to([P, KV_RANK])).then_inc(load, 16)
                sp.dma_start(ident[:, :], a["ident"]).then_inc(load, 16)
                for n, (src, _, _, _) in enumerate(parts):
                    if n >= 2:
                        sp.wait_ge(w_lo, n - 1)
                    sp.dma_start(stage[:, n % 2, 0:src.shape[1]], src).then_inc(staged[n % 2], 16)

            @block.scalar
            def _(act):
                act.wait_ge(load, 48)
                for n, (src, hi, _, g) in enumerate(parts):
                    act.wait_ge(staged[n % 2], 16 * (n // 2) + 16)
                    act.activation(hi, stage[:, n % 2, 0:src.shape[1]], ACT.Copy, scale=g).then_inc(w_hi, 1)

            @block.vector
            def _(dve):
                dve.memset(half[:, :], -0.5)
                dve.memset(eps[:, :], EPS)
                dve.memset(zero[:, :], 0.0)
                dve.memset(inv_rank[:, 0:TILES], 1.0 / Q_RANK)
                dve.memset(inv_rank[:, TILES:], 1.0 / KV_RANK)
                dve.wait_ge(load, 48)
                for n, (src, hi, lo, g) in enumerate(parts):
                    dve.wait_ge(staged[n % 2], 16 * (n // 2) + 16)
                    dve.wait_ge(w_hi, n + 1)
                    dve.scalar_tensor_tensor(lo, stage[:, n % 2, 0:src.shape[1]], g, f32(hi),
                                             ALU.mult, ALU.subtract).then_inc(w_lo, 1)

        xT = sb("xT", [P, 2, GROUP])
        hT = sb("hT", [P, 2, KC, GROUP], F32R)
        xtok = sb("xtok", [P, D_MODEL])
        junk = sb("junk", [P, Q_RANK], BF16)
        ssx, rx = sb("ssx", [P, TILES]), sb("rx", [P, TILES])
        ssq, rq = sb("ssq", [P, 2 * TILES]), sb("rq", [P, 2 * TILES])
        rb = sb("rb", [P, GROUP])
        zt = sb("zt", [P, TILES, TOK_COLS])
        krd = sb("krd", [P, TILES, P])
        rope4 = sb("rope4", [P, 4, TILES, HALF])
        cq = sb("cq", [P, 2, QC, GROUP], F32R)
        ckv = sb("ckv", [P, 2, GROUP], F32R)
        cs = sb("cs", [P, GROUP])
        cst = sb("cst", [P, TILES, ROPE])
        sg = sb("sg", [P, GROUP])
        krt = sg
        aT = sb("aT", [P, CC, CONV_HIST + GROUP])
        uT = sb("uT", [P, CC, UH + GROUP])
        icnt = sb("icnt", [P, GROUPS, CC, UH])
        sA, sB = sb("sA", [P, CC, UH + GROUP]), sb("sB", [P, CC, UH + GROUP])
        y = sb("y", [P, CC, GROUP])
        yn = sb("yn", [P, TILES, CONV_W])
        st6, mv, ry = sb("st6", [P, TILES, 6]), sb("mv", [P, TILES, 2]), sb("ry", [P, TILES])
        qst, kst = sb("qst", [P, 2, GROUP]), sb("kst", [P, 2, GROUP])
        aS = sb("aS", [P, CC, DEC_BATCH, CONV_HIST + DEC_SEQ])
        uS = sb("uS", [P, CC, DEC_BATCH, UH + DEC_SEQ])
        pw, plw = sb("pw", [P, CC, CONV_W]), sb("plw", [P, CC, P])
        mm = Banks(sem, "mm", [ctx.enter_context(nc.psum_tensor(f"mm{i}", [P, GROUP], F32)) for i in range(5)], 30)
        tr = Banks(sem, "tr", [ctx.enter_context(nc.psum_tensor(f"tr{i}", [P, GROUP], F32)) for i in range(3)], 9)

        s = {n: sem(n) for n in (
            "const", "split", "hT_free", "xtok_ld", "xtok_free", "rx", "rx_free", "rb", "u_ld",
            "sgate", "sig", "aval", "glu", "a_free", "upool", "u_free", "conv", "z", "zt_free", "ckv_out",
            "ssq", "rq", "nrm", "kr", "krd_free", "kr_out", "hi", "pair", "krt", "krt_out", "cs_ld", "cst_ld", "cs_free",
            "qst", "kst", "d", "pool", "mv", "ry", "yn", "act", "prep", "tail_out", "rmid", "stats")}
        xt_ld = [sem(f"xt_ld{i}") for i in range(2)]
        q_out, k_out = ([sem(f"{n}{i}") for i in range(2)] for n in ("q_out", "k_out"))

        T0, TOK0, Q0, K0, V0, PL0, CV0 = 0, 6, 10, 18, 22, 26, 28
        T_R, T_CQ, T_CKV, T_KR, T_YF, T_YB = 0, 1, 3, 4, 5, 7
        KST = 12
        POOL_OPS, CONV_OPS = 18, CC * CONV_K

        class Group:

            def __init__(self, it, smp):
                self.it, self.smp = it, smp
                self.n, self.tiles, self.rows = (SAMPLES, 1, SAMPLES) if smp else (GROUP, TILES, P)

            def wait(self, eng, name, per, n):
                eng.wait_ge(s[name] if isinstance(name, str) else name, self.it * per + n)

            def bl(self, ap):
                return ap.rearrange("p (b l) -> p b l", l=DEC_SEQ) if self.smp else ap

        def over_groups(eng, group):
            with eng.Fori(0, GROUPS) as it:
                group(Group(it, False))
            group(Group(GROUPS, True))

        with nc.Block() as block:
            @block.sync
            def _(sp):
                def load_xtok(first, j, n_before):
                    if n_before is not None:
                        sp.wait_ge(s["xtok_free"], n_before)
                    sp.dma_start(xtok[:, :], a["x"][bass.ds(first + j * P, P), :]).then_inc(s["xtok_ld"], 16)

                for j in range(TILES):
                    load_xtok(0, j, j if j else None)
                sp.dma_start(icnt[:, :, :, :], a["icnt"]).then_inc(s["const"], 16)
                sp.dma_start(pw[:, :, :], a["conv_pw"].rearrange("(c p) n -> p c n", p=P)).then_inc(s["const"], 16)
                sp.dma_start(plw[:, :, :], a["pool_w"]).then_inc(s["const"], 16)
                sp.dma_start(aS[:, :, :, 0:CONV_HIST], a["state_conv"]).then_inc(s["const"], 16)
                sp.dma_start(uS[:, :, :, 1:UH], a["state_pool"]).then_inc(s["const"], 16)

                def group(G):
                    it = G.it
                    first = SEQ if G.smp else it * GROUP
                    rows = bass.ds(first, G.n)
                    G.wait(sp, "cs_free", 1, 1)
                    sp.dma_start(cs[:, 0:G.n], a["cs_T"][:, rows]).then_inc(s["cs_ld"], 16)
                    G.wait(sp, "kr", 1, 1)
                    sp.dma_start(cst[:, :, :], a["cs_tok"][bass.ds(GROUPS if G.smp else it, 1), :, :, :].rearrange("o p j n -> (o p) j n")).then_inc(s["cst_ld"], 16)
                    if not G.smp:
                        for j in range(TILES):
                            load_xtok((it + 1) * GROUP, j, it * TILES + TILES + j)
                    G.wait(sp, "nrm", 2 * TILES, 2 * G.tiles)
                    lat = zt[0:G.rows, 0:G.tiles, Q_RANK:Q_RANK + KV_RANK]
                    rot = krd[0:G.rows, 0:G.tiles, NOPE:NOPE + ROPE]
                    if G.smp:
                        sp.dma_start(a["ckv_s"], lat[:, 0, :]).then_inc(s["ckv_out"], 16)
                        G.wait(sp, "kr", 1, 2)
                        sp.dma_start(a["krope_s"], rot[:, 0, :]).then_inc(s["kr_out"], 16)
                    else:
                        sp.dma_start(a["ckv_p"][rows, :].rearrange("(j p) n -> p j n", p=P), lat).then_inc(s["ckv_out"], 16)
                        G.wait(sp, "kr", 1, 2)
                        sp.dma_start(a["krope_p"][rows, :].rearrange("(j p) n -> p j n", p=P), rot).then_inc(s["kr_out"], 16)
                    G.wait(sp, "krt", 1, 1)
                    sp.dma_start(a["KRT"][:, rows], krt[NOPE:P, 0:G.n]).then_inc(s["krt_out"], 16)
                    for h in range(HEADS):
                        G.wait(sp, "qst", HEADS, h + 1)
                        sp.dma_start(a["QT"][h * P:(h + 1) * P, rows], qst[:, h % 2, 0:G.n]).then_inc(q_out[h % 2], 16)
                    for n in range(KST):
                        G.wait(sp, "kst", KST, n + 1)
                        src = kst[:, n % 2, 0:G.n]
                        if n < 4:
                            dst = a["KT"][n * P:(n + 1) * P, rows]
                        elif n < 8:
                            if G.smp:
                                src = kst[0:SAMPLES, n % 2, :]
                                dst = a["V"][SEQ + (n - 4) * SAMPLES:SEQ + (n - 3) * SAMPLES, :]
                            else:
                                src = kst[:, n % 2, :]
                                dst = a["V"][bass.ds(it * GROUP + (n - 4) * P, P), :]
                        else:
                            dst = a["Y"][ATT_W + (n - 8) * P:ATT_W + (n - 7) * P, rows]
                        sp.dma_start(dst, src).then_inc(k_out[n % 2], 16)

                with sp.Fori(0, GROUPS) as it:
                    group(Group(it, False))
                sp.wait_ge(s["u_free"], GROUPS + 1)
                sp.dma_start(a["pool_p"].rearrange("(c p) n -> p c n", p=P), uT[:, :, 1:UH]).then_inc(s["tail_out"], 16)
                sp.wait_ge(s["a_free"], GROUPS + 1)
                sp.dma_start(a["conv_p"].rearrange("(c p) n -> p c n", p=P), aT[:, :, 0:CONV_HIST]).then_inc(s["tail_out"], 16)
                group(Group(GROUPS, True))
                sp.dma_start(a["pool_s"], uS[:, :, :, DEC_SEQ + 1:]).then_inc(s["tail_out"], 16)
                sp.dma_start(a["conv_s"], aS[:, :, :, DEC_SEQ:]).then_inc(s["tail_out"], 16)
                sp.wait_ge(s["tail_out"], 64)
                for name in ("ckv_out", "kr_out", "krt_out"):
                    sp.wait_ge(s[name], 16 * (GROUPS + 2))
                for i in range(2):
                    sp.wait_ge(q_out[i], 16 * (HEADS // 2 * (GROUPS + 1) + 1))
                    sp.wait_ge(k_out[i], 16 * (KST // 2 * (GROUPS + 1) + 1))

            @block.gpsimd
            def _(pool):
                for name in ("hT_free", "rx_free", "a_free", "u_free", "krd_free", "zt_free", "cs_free", "kr"):
                    pool.sem_inc(s[name], 1)
                for sm in (s["ckv_out"], s["kr_out"], s["krt_out"], *q_out, *k_out):
                    pool.sem_inc(sm, 16)
                for b in (*mm.free, *tr.free):
                    pool.sem_inc(b, 1)

                def load_chunk(first, k):
                    pool.dma_start(xT[:, k % 2, :], a["xT"][k * P:(k + 1) * P, bass.ds(first, GROUP)]).then_inc(xt_ld[k % 2], 16)

                load_chunk(0, 0)
                load_chunk(0, 1)
                pool.memset(krd[:, :, :], 0.0).then_inc(s["prep"], 1)
                pool.memset(aT[:, :, 0:CONV_HIST], 0.0).then_inc(s["prep"], 1)
                pool.memset(uT[:, :, 0:UH], 0.0).then_inc(s["prep"], 1)
                pool.memset(uS[:, :, :, 0:1], 0.0).then_inc(s["prep"], 1)
                pool.memset(rstd_all[:, :], 0.0).then_inc(s["prep"], 1)
                pool.wait_ge(s["prep"], 5)
                pool.wait_ge(s["const"], 80)

                def rms_x(value):
                    pool.tensor_tensor(ssx[:, :], ssx[:, :], eps[:, 0:TILES], ALU.add).then_inc(s["rmid"], 1)
                    pool.wait_ge(s["rmid"], value)
                    pool.tensor_tensor(rx[:, :], ssx[:, :], half[:, 0:TILES], ALU.pow).then_inc(s["rx"], 1)

                pool.wait_ge(s["xtok_free"], TILES)
                rms_x(1)

                def copy(dst, src):
                    return pool.tensor_tensor(dst, src, spread(zero[dst.shape[0] == 64 and 64 or 0:dst.shape[0] == 64 and P or dst.shape[0], :], dst), ALU.add)

                def group(G):
                    it, n, nt, rows = G.it, G.n, G.tiles, G.rows
                    done = [0]

                    def step(ins):
                        ins.then_inc(s["pool"], 1)
                        done[0] += 1
                        G.wait(pool, "pool", POOL_OPS, done[0])

                    G.wait(pool, "hT_free", 1, 1)
                    for k in range(KC):
                        G.wait(pool, xt_ld[k % 2], 8 * KC, 16 * (k // 2 + 1))
                        copy(hT[:, 0, k, 0:n], xT[:, k % 2, 0:n]).then_inc(s["split"], 1)
                        G.wait(pool, "split", 2 * KC, 2 * k + 1)
                        pool.tensor_tensor(hT[:, 1, k, 0:n], xT[:, k % 2, 0:n], f32(hT[:, 0, k, 0:n]), ALU.subtract).then_inc(s["split"], 1)
                        G.wait(pool, "split", 2 * KC, 2 * k + 2)
                        if k + 2 < KC:
                            load_chunk(SEQ if G.smp else it * GROUP, k + 2)
                        elif not G.smp:
                            load_chunk(it * GROUP + GROUP, k + 2 - KC)
                    G.wait(pool, "rx", 1, 1)
                    step(copy(rstd_all[0:rows, bass.ds(GROUPS * TILES if G.smp else it * TILES, nt)], rx[0:rows, 0:nt]))
                    for c in range(CC):
                        G.wait(pool, "sig", CC, c + 1)
                        G.wait(pool, "aval", CC, c + 1)
                        v = aS[:, c, :, CONV_HIST:] if G.smp else aT[:, c, CONV_HIST:]
                        pool.tensor_tensor(v, v, G.bl(sg[:, 0:n]), ALU.mult).then_inc(s["glu"], 1)
                    G.wait(pool, "upool", CC, CC)
                    L = UH + (DEC_SEQ if G.smp else GROUP)

                    def cut(t, c0, c1, p0, lo, hi):
                        if not G.smp:
                            return t[p0:P, c0:c1, lo:hi]
                        if t is uS:
                            return t[p0:P, c0:c1, :, lo:hi]
                        v = t[p0:P, :, :].rearrange("p c n -> p (c n)")[:, 0:CC * DEC_BATCH * L]
                        return v.rearrange("p (c b n) -> p c b n", c=CC, b=DEC_BATCH)[:, c0:c1, :, lo:hi]

                    def both(c0, c1, f):
                        if not G.smp:
                            return [f(c0, c1)]
                        return [f(c, c + 1) for c in range(c0, c1)]

                    def add(dst, src, c0, c1, p0, lo, w):
                        if G.smp:
                            for c in range(c0, c1):
                                last = pool.tensor_tensor(cut(dst, c, c + 1, p0, lo, L), cut(src, c, c + 1, p0, lo, L),
                                                          cut(src, c, c + 1, p0, lo - w, L - w), ALU.add)
                                step(last)
                        else:
                            step(pool.tensor_tensor(cut(dst, c0, c1, p0, lo, L), cut(src, c0, c1, p0, lo, L),
                                                    cut(src, c0, c1, p0, lo - w, L - w), ALU.add))

                    u = uS if G.smp else uT
                    add(sA, u, 0, 2, 0, 1, 1)
                    add(sB, sA, 0, 2, 0, 3, 2)
                    step(copy(cut(sA, 0, 1, 64, UH, L), cut(sB, 0, 1, 64, UH, L)))
                    add(sA, sB, 1, 2, 0, 7, 4)
                    add(sB, sA, 1, 2, 64, 15, 8)
                    step(copy(cut(sA, 1, 2, 64, UH, L), cut(sB, 1, 2, 64, UH, L)))
                    for c in range(CC):
                        if G.smp:
                            part = sA[:, :, :].rearrange("p c n -> p (c n)")[:, c * DEC_BATCH * L:(c + 1) * DEC_BATCH * L].rearrange("p (b n) -> p b n", b=DEC_BATCH)[:, :, UH:]
                            last = pool.tensor_tensor(part, part, spread(inv_w[:, c:c + 1], part), ALU.mult)
                        else:
                            step(pool.tensor_tensor(sA[:, c, UH:2 * UH], sA[:, c, UH:2 * UH],
                                                    icnt[:, bass.ds(it, 1), c, :].rearrange("p o n -> p (o n)"), ALU.mult))
                            last = pool.tensor_tensor(sA[:, c, 2 * UH:L], sA[:, c, 2 * UH:L], spread(inv_w[:, c:c + 1], sA[:, c, 2 * UH:L]), ALU.mult)
                        step(last)
                    for c in range(CC):
                        pool.tensor_tensor(cut(sA, c, c + 1, 0, UH, L), cut(sA, c, c + 1, 0, UH, L), cut(u, c, c + 1, 0, UH, L),
                                           ALU.subtract).then_inc(s["d"], 1)
                    G.wait(pool, "d", CC, CC)
                    if not G.smp:
                        copy(uT[:, :, 1:UH], uT[:, :, GROUP + 1:]).then_inc(s["u_free"], 1)
                    G.wait(pool, "ssq", 2 * TILES, 2 * nt)
                    step(pool.tensor_tensor(ssq[0:rows, :], ssq[0:rows, :], inv_rank[0:rows, :], ALU.mult))
                    step(pool.tensor_tensor(ssq[0:rows, :], ssq[0:rows, :], eps[0:rows, :], ALU.add))
                    pool.tensor_tensor(rq[0:rows, :], ssq[0:rows, :], half[0:rows, :], ALU.pow).then_inc(s["rq"], 1)
                    G.wait(pool, "krd_free", 1, 1)
                    G.wait(pool, "kr_out", 16, 16)
                    x1, x2 = (zt[0:rows, 0:nt, TOK_COLS - ROPE + o:TOK_COLS - ROPE + o + HALF] for o in (0, HALF))
                    G.wait(pool, "cst_ld", 16, 16)
                    tab = cst[0:rows, 0:nt, :]
                    cos, sin = tab[:, :, 0:HALF], tab[:, :, HALF:]
                    for q, (xx, t) in enumerate(((x1, cos), (x2, sin), (x1, sin), (x2, cos))):
                        step(pool.tensor_tensor(rope4[0:rows, q, 0:nt, :], xx, t, ALU.mult))
                    for o in (NOPE, NOPE + ROPE):
                        pool.tensor_tensor(krd[0:rows, 0:nt, o:o + HALF], rope4[0:rows, 0, 0:nt, :], rope4[0:rows, 1, 0:nt, :], ALU.subtract)
                        last = pool.tensor_tensor(krd[0:rows, 0:nt, o + HALF:o + ROPE], rope4[0:rows, 2, 0:nt, :], rope4[0:rows, 3, 0:nt, :], ALU.add)
                    last.then_inc(s["kr"], 1)
                    if not G.smp:
                        G.wait(pool, "xtok_free", TILES, 2 * TILES)
                        G.wait(pool, "rx_free", 1, 1)
                        rms_x(it + 2)
                    G.wait(pool, "mv", TILES, nt)
                    step(pool.tensor_tensor(mv[0:rows, 0:nt, 1], mv[0:rows, 0:nt, 1], eps[0:rows, 0:nt], ALU.add))
                    pool.tensor_tensor(ry[0:rows, 0:nt], mv[0:rows, 0:nt, 1], half[0:rows, 0:nt], ALU.pow).then_inc(s["ry"], 1)
                    assert G.smp or done[0] == POOL_OPS, done

                over_groups(pool, group)

            @block.scalar
            def _(act):
                def square_x(j, value):
                    act.wait_ge(s["xtok_ld"], value)
                    act.activation(xtok[:, :], xtok[:, :], ACT.Square, scale=D_MODEL ** -0.5, accum_out=ssx[:, j:j + 1]).then_inc(s["xtok_free"], 1)

                for j in range(TILES):
                    square_x(j, 16 * (j + 1))
                act.wait_ge(s["const"], 80)

                def group(G):
                    it, n, nt, rows = G.it, G.n, G.tiles, G.rows
                    kuse = [0]

                    def stage_out(job, rows_=P, cols_=None, **scale):
                        u = kuse[0]
                        kuse[0] += 1
                        bank = mm.wait_done(act, it, job)
                        G.wait(act, k_out[u % 2], 16 * KST // 2, 16 * (u // 2 + 1))
                        w = cols_ or n
                        act.activation(kst[0:rows_, u % 2, 0:w], bank[0:rows_, 0:w], ACT.Copy, **scale).then_inc(s["kst"], 1)
                        G.wait(act, "kst", KST, u + 1)
                        act.sem_inc(mm.free[job % mm.n], 1)

                    bank = tr.wait_done(act, it, T_R)
                    act.activation(rb[:, 0:n], bank[:, 0:n], ACT.Copy).then_inc(s["rb"], 1)
                    G.wait(act, "rb", 1, 1)
                    act.sem_inc(tr.free[T_R], 1)
                    for c in range(CC):
                        G.wait(act, "sgate", CC, c + 1)
                        act.activation(sg[:, 0:n], sg[:, 0:n], ACT.Sigmoid).then_inc(s["sig"], 1)
                    G.wait(act, "zt_free", 1, 1)
                    G.wait(act, "ckv_out", 16, 16)
                    for j in range(nt):
                        bank = mm.wait_done(act, it, TOK0 + j)
                        act.activation(zt[0:rows, j, :], bank[0:rows, 0:TOK_COLS], ACT.Copy, scale=rx[0:rows, j:j + 1]).then_inc(s["z"], 1)
                        G.wait(act, "z", TILES, j + 1)
                        act.sem_inc(mm.free[(TOK0 + j) % mm.n], 1)
                        act.activation(junk[0:rows, 0:Q_RANK], zt[0:rows, j, 0:Q_RANK], ACT.Square,
                                       accum_out=ssq[0:rows, j:j + 1]).then_inc(s["ssq"], 1)
                        G.wait(act, "ssq", 2 * TILES, 2 * j + 1)
                        act.activation(junk[0:rows, 0:KV_RANK], zt[0:rows, j, Q_RANK:Q_RANK + KV_RANK], ACT.Square,
                                       accum_out=ssq[0:rows, TILES + j:TILES + j + 1]).then_inc(s["ssq"], 1)
                        G.wait(act, "ssq", 2 * TILES, 2 * j + 2)
                    act.sem_inc(s["rx_free"], 1)
                    if not G.smp:
                        G.wait(act, "rx", 1, 1)
                        for j in range(TILES):
                            square_x(j, (it + 1) * 16 * TILES + 16 * (j + 1))
                    for q in range(3):
                        bank = tr.wait_done(act, it, T_CQ + q)
                        dst = cq[:, 0, q, 0:n] if q < QC else ckv[:, 0, 0:n]
                        act.activation(dst, bank[:, 0:n], ACT.Copy).then_inc(s["hi"], 1)
                    bank = tr.wait_done(act, it, T_KR)
                    G.wait(act, "krt_out", 16, 16)
                    act.activation(krt[NOPE:P, 0:n], bank[NOPE:P, 0:n], ACT.Copy).then_inc(s["krt"], 1)
                    G.wait(act, "krt", 1, 1)
                    act.sem_inc(tr.free[T_KR % tr.n], 1)
                    for q in range(4):
                        stage_out(K0 + q)
                    for j in range(4):
                        stage_out(V0 + j, rows, ATT_W)
                    for c in range(CC):
                        stage_out(PL0 + c, scale=pool_s[:, c:c + 1])
                    for c in range(CC):
                        bank = tr.wait_done(act, it, T_YB + c)
                        act.activation(y[:, c, 0:n], bank[:, 0:n], ACT.Silu, scale=ln_g[:, c:c + 1], bias=ln_b[:, c:c + 1]).then_inc(s["act"], 1)
                        G.wait(act, "act", CC, c + 1)
                        act.sem_inc(tr.free[(T_YB + c) % tr.n], 1)
                    for c in range(CC):
                        stage_out(CV0 + c)

                over_groups(act, group)

            @block.vector
            def _(dve):
                dve.wait_ge(s["prep"], 5)
                dve.wait_ge(s["const"], 80)

                def group(G):
                    it, n, nt, rows = G.it, G.n, G.tiles, G.rows
                    G.wait(dve, "rb", 1, 1)
                    G.wait(dve, "a_free", 1, 1)
                    G.wait(dve, "krt_out", 16, 16)
                    for c in range(CC):
                        bank = mm.wait_done(dve, it, T0 + 2 * c)
                        if c:
                            G.wait(dve, "glu", CC, 1)
                        dve.tensor_tensor(sg[:, 0:n], bank[:, 0:n], rb[:, 0:n], ALU.mult).then_inc(s["sgate"], 1)
                        G.wait(dve, "sgate", CC, c + 1)
                        dve.sem_inc(mm.free[(T0 + 2 * c) % mm.n], 1)
                        bank = mm.wait_done(dve, it, T0 + 2 * c + 1)
                        dst = aS[:, c, :, CONV_HIST:] if G.smp else aT[:, c, CONV_HIST:]
                        dve.tensor_tensor(dst, G.bl(bank[:, 0:n]), G.bl(rb[:, 0:n]), ALU.mult).then_inc(s["aval"], 1)
                        G.wait(dve, "aval", CC, c + 1)
                        dve.sem_inc(mm.free[(T0 + 2 * c + 1) % mm.n], 1)
                    G.wait(dve, "u_free", 1, 1)
                    for c in range(CC):
                        bank = mm.wait_done(dve, it, T0 + 4 + c)
                        dst = uS[:, c, :, UH:] if G.smp else uT[:, c, UH:]
                        dve.tensor_tensor(dst, G.bl(bank[:, 0:n]), G.bl(rb[:, 0:n]), ALU.mult).then_inc(s["upool"], 1)
                        G.wait(dve, "upool", CC, c + 1)
                        dve.sem_inc(mm.free[(T0 + 4 + c) % mm.n], 1)

                    def taps():
                        for c in range(CC):
                            G.wait(dve, "glu", CC, c + 1)
                            for k in range(CONV_K):
                                src = aS[:, c, :, k:k + DEC_SEQ] if G.smp else aT[:, c, k:k + GROUP]
                                out = G.bl(y[:, c, 0:n])
                                if k == 0:
                                    dve.tensor_scalar(out, src, dw[:, c, 0:1], conv_b[:, c:c + 1], ALU.mult, ALU.add).then_inc(s["conv"], 1)
                                else:
                                    G.wait(dve, "conv", CONV_OPS, c * CONV_K + k)
                                    dve.scalar_tensor_tensor(out, src, dw[:, c, k:k + 1], out, ALU.mult, ALU.add).then_inc(s["conv"], 1)
                                yield

                    tap = taps()

                    def run(count):
                        for _ in range(count):
                            next(tap, None)

                    run(6)
                    G.wait(dve, "rq", 1, 1) if G.smp else None
                    run(20)
                    G.wait(dve, "rq", 1, 1)
                    for j in range(nt):
                        G.wait(dve, "z", TILES, j + 1)
                        lat = zt[0:rows, j, 0:Q_RANK]
                        dve.tensor_scalar(lat, lat, rq[0:rows, j:j + 1], None, ALU.mult).then_inc(s["nrm"], 1)
                        lat = zt[0:rows, j, Q_RANK:Q_RANK + KV_RANK]
                        dve.scalar_tensor_tensor(lat, lat, rq[0:rows, TILES + j:TILES + j + 1], g_kv[0:rows, :], ALU.mult, ALU.mult).then_inc(s["nrm"], 1)
                    run(4)
                    for q in range(3):
                        G.wait(dve, "hi", 3, q + 1)
                        bank = tr.t[(T_CQ + q) % tr.n]
                        hi, lo = (cq[:, i, q, 0:n] if q < QC else ckv[:, i, 0:n] for i in range(2))
                        dve.tensor_tensor(lo, bank[:, 0:n], f32(hi), ALU.subtract).then_inc(s["pair"], 1)
                        G.wait(dve, "pair", 3, q + 1)
                        dve.sem_inc(tr.free[(T_CQ + q) % tr.n], 1)
                    G.wait(dve, "cs_ld", 16, 16)
                    for h in range(HEADS):
                        run(2)
                        bank = mm.wait_done(dve, it, Q0 + h)
                        G.wait(dve, q_out[h % 2], 16 * HEADS // 2, 16 * (h // 2 + 1))
                        dve.tensor_tensor(qst[:, h % 2, 0:n], bank[:, 0:n], cs[:, 0:n], ALU.mult).then_inc(s["qst"], 1)
                        G.wait(dve, "qst", HEADS, h + 1)
                        dve.sem_inc(mm.free[(Q0 + h) % mm.n], 1)
                    dve.sem_inc(s["cs_free"], 1)
                    run(CONV_OPS)
                    G.wait(dve, "conv", CONV_OPS, CONV_OPS)
                    if not G.smp:
                        dve.tensor_copy(aT[:, :, 0:CONV_HIST], aT[:, :, GROUP:]).then_inc(s["a_free"], 1)
                    for j in range(nt):
                        bank = tr.wait_done(dve, it, T_YF + j // 2)
                        v = bank[0:rows, (j % 2) * CONV_W:(j % 2 + 1) * CONV_W]
                        dve.bn_stats(st6[0:rows, j, :], v).then_inc(s["yn"], 1)
                        G.wait(dve, "yn", 2 * TILES, j + 1)
                        dve.sem_inc(s["stats"], 1)
                        dve.bn_aggr(mv[0:rows, j, :], st6[0:rows, j, :]).then_inc(s["mv"], 1)
                    G.wait(dve, "ry", 1, 1)
                    for j in range(nt):
                        v = tr.t[(T_YF + j // 2) % tr.n][0:rows, (j % 2) * CONV_W:(j % 2 + 1) * CONV_W]
                        dve.tensor_scalar(yn[0:rows, j, :], v, mv[0:rows, j, 0:1], ry[0:rows, j:j + 1], ALU.subtract, ALU.mult).then_inc(s["yn"], 1)
                    G.wait(dve, "yn", 2 * TILES, 2 * nt)
                    for q in range(2):
                        dve.sem_inc(tr.free[(T_YF + q) % tr.n], 1)

                over_groups(dve, group)

            @block.tensor
            def _(pe):
                pe.wait_ge(s["const"], 80)

                def product(out, pairs):
                    for i, (w, x) in enumerate(pairs):
                        for q, (pw_, px) in enumerate(PASSES):
                            last = pe.matmul(out, w(pw_), x(px), start=(i == 0 and q == 0), stop=(i == len(pairs) - 1 and q == 2))
                    return last

                def group(G):
                    it, n, nt, rows = G.it, G.n, G.tiles, G.rows
                    G.wait(pe, "rx", 1, 1)
                    bank = tr.wait_free(pe, it, T_R)
                    for j in range(nt):
                        last = pe.transpose(bank[:, j * P:j * P + rows], rx[0:rows, j:j + 1].broadcast_to([rows, P]), ident[0:rows, 0:rows])
                    last.then_inc(tr.done[T_R], 1)
                    for b in range(6):
                        bank = mm.wait_free(pe, it, T0 + b)
                        for k in range(KC):
                            if b == 0:
                                G.wait(pe, "split", 2 * KC, 2 * k + 2)
                            c0 = TOK_COLS + b * P
                            for q, (pw_, px) in enumerate(PASSES):
                                last = pe.matmul(bank[:, 0:n], w_in[:, pw_, k, c0:c0 + P], hT[:, px, k, 0:n],
                                                 start=(k == 0 and q == 0), stop=(k == KC - 1 and q == 2))
                        last.then_inc(mm.done[(T0 + b) % mm.n], 1)
                    for j in range(nt):
                        bank = mm.wait_free(pe, it, TOK0 + j)
                        t0 = j * P
                        last = product(bank[0:rows, 0:TOK_COLS], [
                            (lambda i, k=k: hT[:, i, k, t0:t0 + rows], lambda i, k=k: w_in[:, i, k, 0:TOK_COLS]) for k in range(KC)])
                        last.then_inc(mm.done[(TOK0 + j) % mm.n], 1)
                        if j == nt - 1:
                            pe.wait_ge(mm.done[(TOK0 + j) % mm.n], mm.count(it, TOK0 + j))
                            pe.sem_inc(s["hT_free"], 1)
                    for j in range(nt, TILES):
                        mm.wait_free(pe, it, TOK0 + j)
                        pe.sem_inc(mm.done[(TOK0 + j) % mm.n], 1)
                        pe.sem_inc(mm.free[(TOK0 + j) % mm.n], 1)
                    G.wait(pe, "nrm", 2 * TILES, 2 * nt)
                    for q in range(4):
                        if q == 3:
                            G.wait(pe, "kr", 1, 2)
                        bank = tr.wait_free(pe, it, T_CQ + q)
                        for j in range(nt):
                            src = zt[0:rows, j, q * P:(q + 1) * P] if q < 3 else krd[0:rows, j, :]
                            last = pe.transpose(bank[:, j * P:j * P + rows], src, ident[0:rows, 0:rows])
                        last.then_inc(tr.done[(T_CQ + q) % tr.n], 1)
                    pe.wait_ge(tr.done[T_KR % tr.n], tr.count(it, T_KR))
                    pe.sem_inc(s["zt_free"], 1)
                    pe.sem_inc(s["krd_free"], 1)
                    G.wait(pe, "pair", 3, 2)
                    for h in range(HEADS):
                        bank = mm.wait_free(pe, it, Q0 + h)
                        product(bank[:, 0:n], [(lambda i, k=k: w_uq[:, i, k, h * P:(h + 1) * P], lambda i, k=k: cq[:, i, k, 0:n])
                                               for k in range(QC)]).then_inc(mm.done[(Q0 + h) % mm.n], 1)
                    G.wait(pe, "pair", 3, 3)
                    for q in range(4):
                        bank = mm.wait_free(pe, it, K0 + q)
                        product(bank[:, 0:n], [(lambda i: w_uk[:, i, q * P:(q + 1) * P], lambda i: ckv[:, i, 0:n])]).then_inc(mm.done[(K0 + q) % mm.n], 1)
                    for j in range(4):
                        bank = mm.wait_free(pe, it, V0 + j)
                        t0 = 0 if G.smp else j * P
                        product(bank[0:rows, :], [(lambda i: ckv[:, i, t0:t0 + rows], lambda i: w_uv[:, i, :])]).then_inc(mm.done[(V0 + j) % mm.n], 1)
                    G.wait(pe, "d", CC, CC)
                    for c in range(CC):
                        bank = mm.wait_free(pe, it, PL0 + c)
                        if G.smp:
                            L = UH + DEC_SEQ
                            d = sA[:, :, :].rearrange("p c n -> p (c n)")[:, 0:CC * DEC_BATCH * L].rearrange("p (c b n) -> p c b n", c=CC, b=DEC_BATCH)[:, c, :, UH:]
                            out = bank[:, 0:n].rearrange("p (b l) -> p b l", l=DEC_SEQ)
                        else:
                            d, out = sA[:, c, UH:], bank[:, 0:n]
                        pe.matmul(out, plw[:, c, :], d, start=True, stop=True).then_inc(mm.done[(PL0 + c) % mm.n], 1)
                    G.wait(pe, "conv", CONV_OPS, CONV_OPS)
                    for q in range(2):
                        bank = tr.wait_free(pe, it, T_YF + q)
                        for j in (2 * q, 2 * q + 1):
                            if j >= nt:
                                if j == 2:
                                    last = None
                                continue
                            for c in range(CC):
                                last = pe.transpose(bank[0:rows, (j % 2) * CONV_W + c * P:(j % 2) * CONV_W + (c + 1) * P],
                                                    y[:, c, j * P:j * P + rows], ident[:, :])
                        if last is None:
                            pe.sem_inc(tr.done[(T_YF + q) % tr.n], 1)
                        else:
                            last.then_inc(tr.done[(T_YF + q) % tr.n], 1)
                    G.wait(pe, "yn", 2 * TILES, 2 * nt)
                    for c in range(CC):
                        bank = tr.wait_free(pe, it, T_YB + c)
                        for j in range(nt):
                            last = pe.transpose(bank[:, j * P:j * P + rows], yn[0:rows, j, c * P:(c + 1) * P], ident[0:rows, 0:rows])
                        last.then_inc(tr.done[(T_YB + c) % tr.n], 1)
                    G.wait(pe, "act", CC, CC)
                    for c in range(CC):
                        bank = mm.wait_free(pe, it, CV0 + c)
                        for k in range(CC):
                            last = pe.matmul(bank[:, 0:n], pw[:, k, c * P:(c + 1) * P], y[:, k, 0:n], start=(k == 0), stop=(k == CC - 1))
                        last.then_inc(mm.done[(CV0 + c) % mm.n], 1)

                over_groups(pe, group)


def stage2(nc, a, keep):
    ctx = ExitStack()
    with ctx:
        def sb(name, shape, dt=F32):
            return ctx.enter_context(nc.sbuf_tensor(name, shape, dt))

        def sem(name):
            return ctx.enter_context(nc.semaphore("s2_" + name))

        ident, rden = keep["ident"], keep["rden"]
        NT = SEQ // P
        qraw, kraw, vraw = sb("qraw", [P, SEQ]), sb("kraw", [P, SEQ]), sb("vraw", [P, NT, VDIM])
        q2, k2 = sb("q2", [P, 2, 2, SEQ], F32R), sb("k2", [P, 2, 2, SEQ], F32R)
        v2 = sb("v2", [P, 2, NT, 2 * VDIM], F32R)
        prob = sb("prob", [P, 2, SEQ])
        pT = sb("pT", [P, 2, NT, GROUP], F32R)
        mx, nm = sb("mx", [P, 4, 4]), sb("nm", [P, 4])
        dsum = sb("dsum", [P, 2, NT, 4])
        den = sb("den", [P, 2, NT])
        zero = sb("zero2", [P, 1])
        olo, ost = sb("olo", [VDIM, GROUP]), sb("ost", [VDIM, 2, GROUP])
        ident_b, mask_b, mask_f = sb("ident_b", [P, P], BF16), sb("mask_b", [P, P], BF16), sb("mask_f", [P, P])
        head_jobs = [(t, c, min(GROUP, (t + 1) * P - c * GROUP), c == t // 4) for t in range(NT) for c in range(t // 4 + 1)]
        JH = len(head_jobs)
        jobs = [(hf, *j) for hf in range(2) for j in head_jobs]
        J = len(jobs)
        sc = Banks(sem, "sc", [ctx.enter_context(nc.psum_tensor(f"sc{i}", [P, GROUP], F32)) for i in range(5)], J)
        tr = Banks(sem, "tr", [ctx.enter_context(nc.psum_tensor(f"tp{i}", [P, GROUP], F32)) for i in range(2)], J)
        pv = ctx.enter_context(nc.psum_tensor("pv", [P, GROUP], F32))
        s = {n: sem(n) for n in ("const", "raw", "split", "head_done", "mx", "nm", "pT_hi", "pv_done", "pv_free", "olo", "ost",
                                 "den", "init", "masks", "table", "gather")}
        assert HEADS == DEC_BATCH
        n_phys = a["cache_ckv"].shape[0]
        table = sb("table", [1, DEC_BATCH * N_PAGES], I32)
        o_out = [sem(f"o_out{i}") for i in range(2)]
        SP_N = 6
        ends = {n: (hf, t // 4) for n, (hf, t, c, w, last) in enumerate(jobs) if last and t % 4 == 3}
        tile_no = [hf * NT + t for hf, t, *_ in jobs]
        slice_at = {}
        for n, (_, g) in ends.items():
            for c in range(g + 1):
                slice_at.setdefault(n - g + c + 1, []).append((n, c))
        SLICES = 1 + 2 + 3 + 4

        def slices(i, n, c):
            hf, g = ends[n]
            return (i * 2 + hf) * SLICES + g * (g + 1) // 2 + c + 1

        LEAD = 4

        with nc.Block() as block:
            @block.sync
            def _(sp):
                sp.dma_start(mask_f[:, :], a["causal"]).then_inc(s["const"], 16)
                sp.dma_start(kraw[NOPE:P, :], a["KRT"][:, 0:SEQ]).then_inc(s["const"], 16)

                sp.dma_start(table[:, :], a["page_table"]).then_inc(s["table"], 16)
                sp.wait_ge(s["table"], 16)

                def gather(b, pages):
                    for pg in pages:
                        page = sp.value_load(table[0:1, bass.ds(b * N_PAGES + pg, 1)], min_val=0, max_val=n_phys - 1)
                        sp.dma_start(a["LAT"][bass.ds(b, 1), pg, :, :].rearrange("o p n -> (o p) n"),
                                     a["cache_ckv"][bass.ds(page, 1), :, :].rearrange("o p n -> (o p) n")).then_inc(s["gather"], 16)
                        sp.dma_start(a["KR"][bass.ds(b, 1), pg, :, :].rearrange("o p n -> (o p) n"),
                                     a["cache_krope"][bass.ds(page, 1), :, :].rearrange("o p n -> (o p) n")).then_inc(s["gather"], 16)

                def load(h):
                    sp.dma_start(qraw[:, :], a["QT"][bass.ds(h * P, P), 0:SEQ]).then_inc(s["raw"], 16)
                    sp.dma_start(kraw[0:NOPE, :], a["KT"][bass.ds(h * NOPE, NOPE), 0:SEQ]).then_inc(s["raw"], 16)
                    sp.dma_start(vraw[:, :, :], a["V"][0:SEQ, bass.ds(h * VDIM, VDIM)].rearrange("(k p) d -> p k d", p=P)).then_inc(s["raw"], 16)

                load(0)
                sp.wait_ge(s["split"], SP_N)
                load(1)
                with sp.Fori(0, HEADS // 2) as i:
                    for hf in range(2):
                        sp.wait_ge(s["split"], i * 2 * SP_N + (2 + hf) * SP_N)
                        load((i * 2 + 2 + hf) % HEADS)
                        for g in range(4):
                            gather(i * 2 + hf, range(g * N_PAGES // 4, (g + 1) * N_PAGES // 4))
                            sp.wait_ge(s["ost"], i * 8 + hf * 4 + g + 1)
                            sp.dma_start(a["Y"][bass.ds((i * 2 + hf) * VDIM, VDIM), g * GROUP:(g + 1) * GROUP],
                                         ost[:, g % 2, :]).then_inc(o_out[g % 2], 16)
                sp.wait_ge(s["raw"], 48 * (HEADS + 2))
                sp.wait_ge(s["gather"], 32 * DEC_BATCH * N_PAGES)
                for b in range(2):
                    sp.wait_ge(o_out[b], 16 * (2 * HEADS + 1))

            @block.gpsimd
            def _(pool):
                for b in (*sc.free, *tr.free):
                    pool.sem_inc(b, 1)
                for b in o_out:
                    pool.sem_inc(b, 16)
                pool.sem_inc(s["head_done"], 1)
                pool.sem_inc(s["pv_free"], 1)
                pool.memset(zero[:, :], 0.0).then_inc(s["init"], 1)
                pool.wait_ge(s["init"], 1)
                pool.wait_ge(s["const"], 32)
                pool.tensor_copy(k2[NOPE:P, 0, 0, :], kraw[NOPE:P, :]).then_inc(s["init"], 1)
                pool.tensor_copy(k2[NOPE:P, 1, 0, :], kraw[NOPE:P, :]).then_inc(s["init"], 1)
                pool.wait_ge(s["init"], 3)
                for b in range(2):
                    pool.tensor_tensor(k2[NOPE:P, b, 1, :], kraw[NOPE:P, :], f32(k2[NOPE:P, b, 0, :]), ALU.subtract).then_inc(s["init"], 1)
                pool.wait_ge(s["init"], 5)

                def copy(dst, src):
                    return pool.tensor_tensor(dst, src, spread(zero[0:dst.shape[0], :], dst), ALU.add)

                def split(b, before):
                    for q, (dst, src) in enumerate(((lambda i: q2[:, b, i, :], qraw[:, :]), (lambda i: k2[0:NOPE, b, i, :], kraw[0:NOPE, :]),
                                                    (lambda i: v2[:, b, :, i * VDIM:(i + 1) * VDIM], vraw[:, :, :]))):
                        copy(dst(0), src).then_inc(s["split"], 1)
                        pool.wait_ge(s["split"], before + 2 * q + 1)
                        pool.tensor_tensor(dst(1), src, f32(dst(0)), ALU.subtract).then_inc(s["split"], 1)
                    pool.wait_ge(s["split"], before + SP_N)

                pool.wait_ge(s["raw"], 48)
                split(0, 0)
                with pool.Fori(0, HEADS // 2) as i:
                    for hf in range(2):
                        pool.wait_ge(s["raw"], i * 96 + (2 + hf) * 48)
                        pool.wait_ge(s["head_done"], i * 2 + 1 + hf)
                        split(1 - hf, i * 2 * SP_N + (1 + hf) * SP_N)

            @block.tensor
            def _(pe):
                pe.wait_ge(s["init"], 5)
                pe.wait_ge(s["masks"], 2)

                def scores(i, n):
                    hf, t, c, w, last = jobs[n]
                    if n % JH == 0:
                        pe.wait_ge(s["split"], i * 2 * SP_N + (1 + hf) * SP_N)
                    bank = sc.wait_free(pe, i, n)
                    for q, (pw_, px) in enumerate(PASSES):
                        ins = pe.matmul(bank[:, 0:w], q2[:, hf, pw_, t * P:(t + 1) * P], k2[:, hf, px, c * GROUP:c * GROUP + w],
                                        start=(q == 0), stop=(q == 2 and not last))
                    if last:
                        ins = pe.matmul(bank[:, w - P:w], ident_b[:, :], mask_b[:, :], start=False, stop=True)
                    ins.then_inc(sc.done[n % sc.n], 1)

                def transposes(i, n):
                    hf, t, c, w, last = jobs[n]
                    pe.wait_ge(sc.free[n % sc.n], sc.count(i, n) + 1)
                    bank = tr.wait_free(pe, i, n)
                    for k in range(w // P):
                        ins = pe.transpose(bank[:, k * P:(k + 1) * P], prob[:, t % 2, c * GROUP + k * P:c * GROUP + (k + 1) * P], ident[:, :])
                    ins.then_inc(tr.done[n % tr.n], 1)

                def values(i, n, c):
                    hf, g = ends[n]
                    m = n - g + c
                    pe.wait_ge(tr.free[m % tr.n], tr.count(i, m) + 1)
                    if c == 0:
                        pe.wait_ge(s["pv_free"], i * 8 + hf * 4 + g + 1)
                    for k in range(4 * c, 4 * c + 4):
                        c0 = max(0, k - 4 * g) * P
                        for part in range(2):
                            ins = pe.matmul(pv[:, c0:], v2[:, hf, k, :], pT[:, part, k, c0:], start=(k == 0 and part == 0),
                                            stop=(k == 4 * g + 3 and part == 1))
                    ins.then_inc(s["pv_done"], 1)
                    if g == 3 and c == 3:
                        pe.wait_ge(s["pv_done"], (i * 2 + hf + 1) * SLICES)
                        pe.sem_inc(s["head_done"], 1)

                with pe.Fori(0, HEADS // 2) as i:
                    for n in range(LEAD):
                        scores(i, n)
                    for n in range(J):
                        if n + LEAD < J:
                            scores(i, n + LEAD)
                        transposes(i, n)
                        for e, c in slice_at.get(n, ()):
                            values(i, e, c)
                    for e, c in slice_at[J]:
                        values(i, e, c)

            @block.scalar
            def _(act):
                act.wait_ge(s["const"], 32)
                act.activation(ident_b[:, :], ident[:, :], ACT.Copy).then_inc(s["masks"], 1)
                act.activation(mask_b[:, :], mask_f[:, :], ACT.Copy).then_inc(s["masks"], 1)

                def exps(i, n):
                    hf, t, c, w, last = jobs[n]
                    bank = sc.t[n % sc.n]
                    act.wait_ge(s["nm"], i * 2 * NT + tile_no[n] + 1)
                    act.activation(prob[:, t % 2, c * GROUP:c * GROUP + w], bank[:, 0:w], ACT.Exp, bias=nm[:, t % 4:t % 4 + 1],
                                   accum_out=dsum[:, hf, t, c:c + 1]).then_inc(sc.free[n % sc.n], 1)

                def hi(i, n):
                    hf, t, c, w, last = jobs[n]
                    bank = tr.wait_done(act, i, n)
                    if t % 4 == 0:
                        before = [e for e in ends if e < n]
                        if before and c <= ends[before[-1]][1]:
                            act.wait_ge(s["pv_done"], slices(i, before[-1], c))
                    act.activation(pT[:, 0, 4 * c:4 * c + w // P, (t % 4) * P:(t % 4 + 1) * P],
                                   bank[:, 0:w].rearrange("p (k q) -> p k q", q=P), ACT.Copy).then_inc(s["pT_hi"], 1)

                def values(i, n):
                    hf, g = ends[n]
                    act.wait_ge(s["pv_done"], slices(i, n, g))
                    act.activation(olo[:, :], pv[VDIM:P, :], ACT.Copy).then_inc(s["olo"], 1)

                with act.Fori(0, HEADS // 2) as i:
                    exps(i, 0)
                    for n in range(J):
                        new_tile = n + 1 < J and jobs[n + 1][2] == 0
                        if n + 1 < J and not new_tile:
                            exps(i, n + 1)
                        hi(i, n)
                        if new_tile:
                            exps(i, n + 1)
                        if n - 1 in ends:
                            values(i, n - 1)
                    values(i, J - 1)

            @block.vector
            def _(dve):
                dve.memset(dsum[:, :, :, :], 0.0).then_inc(s["den"], 1)
                dve.memset(rden[:, :, NT:NT + 1], 1.0)
                dve.wait_ge(s["den"], 1)
                DN = 2 * 2

                def maxima(i, n):
                    hf, t, c, w, last = jobs[n]
                    bank = sc.wait_done(dve, i, n)
                    if last and c == 0:
                        dve.reduce_max(nm[:, t % 4:t % 4 + 1], bank[:, 0:w], AXX, negate=True).then_inc(s["nm"], 1)
                        return
                    dve.reduce_max(mx[:, t % 4, c:c + 1], bank[:, 0:w], AXX).then_inc(s["mx"], 1)
                    if last:
                        dve.wait_ge(s["mx"], i * MXN + mxc[n])
                        dve.reduce_max(nm[:, t % 4:t % 4 + 1], mx[:, t % 4, 0:c + 1], AXX, negate=True).then_inc(s["nm"], 1)

                mxc, count = [], 0
                for hf, t, c, w, last in jobs:
                    count += t >= 4
                    mxc.append(count)
                MXN = count

                def lo(i, n):
                    hf, t, c, w, last = jobs[n]
                    bank = tr.t[n % tr.n]
                    dve.wait_ge(s["pT_hi"], i * J + n + 1)
                    cut = lambda part: pT[:, part, 4 * c:4 * c + w // P, (t % 4) * P:(t % 4 + 1) * P]
                    dve.tensor_tensor(cut(1), bank[:, 0:w].rearrange("p (k q) -> p k q", q=P), f32(cut(0)), ALU.subtract)\
                       .then_inc(tr.free[n % tr.n], 1)

                def values(i, n):
                    hf, g = ends[n]
                    dve.wait_ge(s["olo"], i * 8 + hf * 4 + g + 1)
                    dve.wait_ge(o_out[g % 2], i * 64 + hf * 32 + (g // 2) * 16 + 16)
                    dve.tensor_tensor(ost[:, g % 2, :], pv[0:VDIM, :], olo[:, :], ALU.add).then_inc(s["ost"], 1)
                    dve.wait_ge(s["ost"], i * 8 + hf * 4 + g + 1)
                    dve.sem_inc(s["pv_free"], 1)
                    if g == 3:
                        dve.reduce_sum(den[:, hf, :], dsum[:, hf, :, :], AXX).then_inc(s["den"], 1)
                        dve.wait_ge(s["den"], i * DN + 2 + 2 * hf)
                        dve.reciprocal(rden[:, bass.ds(i * 2 + hf, 1), 0:NT].rearrange("p o t -> p (o t)"), den[:, hf, :]).then_inc(s["den"], 1)

                with dve.Fori(0, HEADS // 2) as i:
                    for n in range(LEAD):
                        maxima(i, n)
                    for n in range(J):
                        if n + LEAD < J:
                            maxima(i, n + LEAD)
                        lo(i, n)
                        if n - 1 in ends:
                            values(i, n - 1)
                    values(i, J - 1)


def stage3(nc, a, keep):
    ctx = ExitStack()
    with ctx:
        def sb(name, shape, dt=F32):
            return ctx.enter_context(nc.sbuf_tensor(name, shape, dt))

        def ps(name):
            return ctx.enter_context(nc.psum_tensor(name, [P, GROUP], F32))

        def sem(name):
            return ctx.enter_context(nc.semaphore("s3_" + name))

        ident = keep["ident"]
        B4 = 4
        PAST = N_PAGES * PAGE
        CH = PAST // GROUP
        PC = GROUP // PAGE
        w_gate = keep["w_gate"]
        stage, g_pre, zero = sb("stage3", [P, 2, D_MIX]), sb("g_pre3", [P, KC]), sb("zero3", [P, 1])
        qs = sb("qs", [NOPE, HEADS, SAMPLES])
        qra, qrb = sb("qra", [P, HEADS, SAMPLES]), sb("qrb", [P, HEADS, SAMPLES])
        q_abs = sb("q_abs", [P, HEADS, SAMPLES])
        q_rope = sb("q_rope", [P, PC, HEADS, SAMPLES])
        w_ukT = sb("w_ukT", [NOPE, HEADS, KV_RANK])
        w_uv = sb("w_uv3", [P, ATT_W])
        mask4 = sb("mask4", [P, DEC_SEQ])
        new_lat = sb("new_lat", [DEC_SEQ, DEC_BATCH, KV_RANK])
        new_tok = sb("new_tok", [SAMPLES, KV_RANK])
        new_latT = sb("new_latT", [P, SAMPLES])
        new_krT = sb("new_krT", [P, SAMPLES])
        lat = sb("lat", [P, B4, N_PAGES, KV_RANK])
        kr = sb("kr", [P, B4, N_PAGES, ROPE])
        qb = sb("qb", [P, B4, 1 + PC, HEADS * DEC_SEQ])
        now_latT, now_krT = sb("now_latT", [P, B4 * DEC_SEQ]), sb("now_krT", [P, B4 * DEC_SEQ])
        now_lat = sb("now_lat", [DEC_SEQ, B4, KV_RANK])
        latT = sb("latT", [P, 2, PAST])
        krT = sb("krT", [P, 2, CH, PAGE])
        prob = sb("prob3", [P, PAST + P])
        probT = sb("probT", [P, N_PAGES + 1, P])
        snew = sb("snew", [P, DEC_SEQ])
        mx, nm, dsum, den = sb("mx3", [P, CH + 1]), sb("nm3", [P, 2]), sb("dsum3", [P, CH + 1]), sb("den3", [P, 2])
        o_lat, o_latT = sb("o_lat", [P, KV_RANK]), sb("o_latT", [P, P])
        o_att = sb("o_att", [VDIM, HEADS, B4 * DEC_SEQ])
        sc = [ps(f"s3sc{i}") for i in range(CH)]
        sn = ps("s3new")
        tp = [ps(f"s3tp{i}") for i in range(2)]
        acc = ps("s3acc")
        s = {n: sem(n) for n in ("const", "lat_free", "prep", "prepd", "qabs", "latT", "tdone", "t_free", "krT", "sdone", "snew", "mx", "nm",
                                 "exp", "den", "pT", "pTd", "pv", "olat", "olT", "olTd", "att", "oatt", "out", "zero", "sfree", "w", "g_pre")}
        w_ld = [sem(f"w_ld{i}") for i in range(2)]
        NQ = B4 * (1 + PC) + 3
        NC_ = 15 * 16
        ld = [sem(f"ld{i}") for i in range(B4)]
        NTR = B4 * (CH + 1)
        NPT = (N_PAGES + 1 + 3) // 4
        TB = NTR + NPT + 1
        assert TB % 2 == 0
        kdims = (HEADS, SAMPLES)

        with nc.Block() as block:
            @block.sync
            def _(sp):
                def pages(i, b):
                    sample = bass.ds(i * B4 + b, 1)
                    for g in range(2):
                        k = slice(g * N_PAGES // 2, (g + 1) * N_PAGES // 2)
                        sp.dma_start(lat[:, b, k, :], a["LAT"][sample, k, :, :].rearrange("o k p n -> p (o k) n")).then_inc(ld[b], 16)
                    sp.dma_start(kr[:, b, :, :], a["KR"][sample, :, :, :].rearrange("o k p n -> p (o k) n")).then_inc(ld[b], 16)

                q_s = a["QT"][0:HEADS * P, SEQ:SEQ + SAMPLES].rearrange("(h p) n -> p h n", p=P)
                sp.dma_start(qs[:, :, :], q_s[0:NOPE, :, :]).then_inc(s["const"], 16)
                for j in range(PC):
                    sp.dma_start(qra[j * ROPE:(j + 1) * ROPE, :, :], q_s[NOPE:NOPE + ROPE, :, :]).then_inc(s["const"], 16)
                    sp.dma_start(qrb[j * ROPE:(j + 1) * ROPE, :, :], q_s[NOPE + ROPE:, :, :]).then_inc(s["const"], 16)
                sp.dma_start(w_ukT[:, :, :], a["w_ukT"]).then_inc(s["const"], 16)
                sp.dma_start(w_uv[:, :], a["w_uv"]).then_inc(s["const"], 16)
                sp.dma_start(mask4[:, :], a["causal4"]).then_inc(s["const"], 16)
                sp.dma_start(new_tok[:, :], a["ckv_s"]).then_inc(s["const"], 16)
                sp.dma_start(new_lat[:, :, :], a["ckv_s"].rearrange("(b l) n -> l b n", l=DEC_SEQ)).then_inc(s["const"], 16)
                sp.wait_ge(s["zero"], 2)
                sp.dma_start(new_krT[0:ROPE, :], a["KRT"][0:ROPE, SEQ:SEQ + SAMPLES]).then_inc(s["const"], 16)
                with sp.Fori(0, 2) as i:
                    for b in range(B4):
                        sp.wait_ge(s["lat_free"], i * B4 + b + 1)
                        pages(i, b)
                    sp.wait_ge(s["oatt"], i + 1)
                    sp.dma_start(a["Y"][0:ATT_W, bass.ds(i * (B4 * DEC_SEQ) + SEQ, B4 * DEC_SEQ)].rearrange("(h d) n -> d h n", d=VDIM),
                                 o_att[:, :, :]).then_inc(s["out"], 16)
                sp.wait_ge(s["out"], 48)

            @block.gpsimd
            def _(pool):
                pool.memset(q_rope[:, :, :, :], 0.0).then_inc(s["zero"], 1)
                pool.memset(new_krT[:, :], 0.0).then_inc(s["zero"], 1)
                pool.memset(prob[:, PAST:], 0.0).then_inc(s["zero"], 1)
                pool.sem_inc(s["lat_free"], B4)
                pool.sem_inc(s["t_free"], 2)
                pool.sem_inc(s["sfree"], 1)
                pool.sem_inc(s["out"], 16)
                pool.memset(zero[:, :], 0.0).then_inc(s["w"], 1)
                pool.dma_start(g_pre[:, :], a["norm_pre_c"]).then_inc(s["g_pre"], 16)

                def load_w(k):
                    pool.dma_start(stage[:, k % 2, :], a["w_gate"][k * P:(k + 1) * P, :]).then_inc(w_ld[k % 2], 16)

                load_w(0)
                load_w(1)
                pool.wait_ge(s["g_pre"], 16)
                pool.wait_ge(s["w"], 1)
                for k in range(KC):
                    raw = stage[:, k % 2, :]
                    pool.wait_ge(w_ld[k % 2], 16 * (k // 2) + 16)
                    pool.tensor_tensor(raw, raw, spread(g_pre[:, k:k + 1], raw), ALU.mult).then_inc(s["w"], 1)
                    pool.wait_ge(s["w"], 3 * k + 2)
                    pool.tensor_tensor(w_gate[:, 0, k, :], raw, spread(zero[:, :], raw), ALU.add).then_inc(s["w"], 1)
                    pool.wait_ge(s["w"], 3 * k + 3)
                    pool.tensor_tensor(w_gate[:, 1, k, :], raw, f32(w_gate[:, 0, k, :]), ALU.subtract).then_inc(s["w"], 1)
                    if k + 2 < KC:
                        pool.wait_ge(s["w"], 3 * k + 4)
                        load_w(k + 2)
                pool.wait_ge(s["w"], 3 * KC + 1)

            @block.tensor
            def _(pe):
                pe.wait_ge(s["const"], NC_)
                for h in range(HEADS):
                    last = pe.matmul(acc[:, h * SAMPLES:(h + 1) * SAMPLES], w_ukT[:, h, :], qs[:, h, :], start=True, stop=True)
                last.then_inc(s["prep"], 1)
                pe.transpose(sn[:, 0:SAMPLES], new_tok[:, :], ident[0:SAMPLES, 0:SAMPLES]).then_inc(s["prep"], 1)
                pe.wait_ge(s["prepd"], PC + 2)

                with pe.Fori(0, 2) as i:
                    use = [0]

                    def t_bank():
                        u = use[0]
                        use[0] += 1
                        pe.wait_ge(s["t_free"], i * TB + u + 1)
                        return tp[u % 2]

                    pe.wait_ge(s["qabs"], i * NQ + NQ)
                    for b in range(B4):
                        pe.wait_ge(ld[b], i * 48 + 48)
                        for c in range(CH):
                            bank = t_bank()
                            for k in range(PC):
                                last = pe.transpose(bank[:, k * P:(k + 1) * P], lat[:, b, c * PC + k, :], ident[:, :])
                            last.then_inc(s["tdone"], 1)
                        bank = t_bank()
                        for c in range(CH):
                            last = pe.transpose(bank[:, c * P:(c + 1) * P], kr[:, b, c * PC:(c + 1) * PC, :].rearrange("p k r -> p (k r)"), ident[:, :])
                        last.then_inc(s["tdone"], 1)
                        if b == 0:
                            pe.wait_ge(s["sfree"], i + 1)
                        row = slice(b * SAMPLES, (b + 1) * SAMPLES)
                        pe.wait_ge(s["latT"], i * NTR + (b + 1) * (CH + 1))
                        tok = slice(b * DEC_SEQ, (b + 1) * DEC_SEQ)
                        for c in range(CH):
                            pe.matmul(sc[c][row, :], qb[:, b, 0, :], latT[:, b % 2, c * GROUP:(c + 1) * GROUP], start=True, stop=False)
                            for j in range(PC):
                                last = pe.matmul(sc[c][row, j * P:(j + 1) * P], qb[:, b, 1 + j, :], krT[:, b % 2, c, :], start=False, stop=(j == PC - 1))
                            last.then_inc(s["sdone"], 1)
                        pe.matmul(sn[row, 0:DEC_SEQ], qb[:, b, 0, :], now_latT[:, tok], start=True, stop=False)
                        pe.matmul(sn[row, 0:DEC_SEQ], qb[:, b, 1, :], now_krT[:, tok], start=False, stop=True).then_inc(s["sdone"], 1)
                    pe.wait_ge(s["exp"], i * (CH + 1) + CH + 1)
                    for g in range(NPT):
                        bank = t_bank()
                        for k in range(4 * g, min(4 * g + 4, N_PAGES + 1)):
                            last = pe.transpose(bank[:, (k % 4) * P:(k % 4 + 1) * P], prob[:, k * P:(k + 1) * P], ident[:, :])
                        last.then_inc(s["tdone"], 1)
                    pe.wait_ge(s["pT"], i * NPT + NPT)
                    for b in range(B4):
                        row = slice(b * SAMPLES, (b + 1) * SAMPLES)
                        for pg in range(N_PAGES):
                            pe.matmul(acc[row, 0:KV_RANK], probT[:, pg, row], lat[:, b, pg, :], start=(pg == 0), stop=False)
                        pe.matmul(acc[row, 0:KV_RANK], probT[0:DEC_SEQ, N_PAGES, row],
                                  now_lat[:, b, :], start=False, stop=True).then_inc(s["lat_free"], 1)
                    pe.wait_ge(s["olat"], i + 1)
                    bank = t_bank()
                    pe.transpose(bank[:, 0:P], o_lat[:, :], ident[:, :]).then_inc(s["tdone"], 1)
                    pe.wait_ge(s["olT"], i + 1)
                    oT = o_latT[:, :].rearrange("p (b h l) -> p b h l", b=B4, h=HEADS)
                    for h in range(HEADS):
                        last = pe.matmul(acc[0:VDIM, GROUP // 2 + h * 16:GROUP // 2 + (h + 1) * 16].rearrange("p (b l) -> p b l", l=DEC_SEQ), w_uv[:, h * VDIM:(h + 1) * VDIM],
                                         oT[:, :, h, :], start=True, stop=True)
                    last.then_inc(s["att"], 1)
                    assert use[0] == TB, (use, TB)

            @block.scalar
            def _(act):
                act.wait_ge(s["zero"], 3)
                with act.Fori(0, 2) as i:
                    for c in range(CH + 1):
                        if c == 0:
                            act.wait_ge(s["nm"], i + 1)
                        src = sc[c][:, :] if c < CH else snew[:, :]
                        dst = prob[:, c * GROUP:(c + 1) * GROUP] if c < CH else prob[:, PAST:PAST + DEC_SEQ]
                        act.activation(dst, src, ACT.Exp, bias=nm[:, 1:2], accum_out=dsum[:, c:c + 1]).then_inc(s["exp"], 1)

            @block.vector
            def _(dve):
                dve.wait_ge(s["prep"], 2)
                dve.wait_ge(s["zero"], 3)
                dve.tensor_copy(q_abs[:, :, :], acc[:, 0:HEADS * SAMPLES].rearrange("p (h n) -> p h n", h=HEADS)).then_inc(s["prepd"], 1)
                dve.tensor_copy(new_latT[:, :], sn[:, 0:SAMPLES]).then_inc(s["prepd"], 1)
                dve.wait_ge(s["const"], NC_)
                for j in range(PC):
                    r = slice(j * ROPE, (j + 1) * ROPE)
                    dve.tensor_tensor(q_rope[r, j, :, :], qra[r, :, :], qrb[r, :, :], ALU.add).then_inc(s["prepd"], 1)
                dve.wait_ge(s["prepd"], PC + 2)
                with dve.Fori(0, 2) as i:
                    for b in range(B4):
                        tok = bass.ds(i * (B4 * DEC_SEQ) + b * DEC_SEQ, DEC_SEQ)
                        dve.tensor_copy(qb[:, b, 0, :].rearrange("p (h l) -> p h l", l=DEC_SEQ), q_abs[:, :, tok]).then_inc(s["qabs"], 1)
                        for j in range(PC):
                            dve.tensor_copy(qb[:, b, 1 + j, :].rearrange("p (h l) -> p h l", l=DEC_SEQ), q_rope[:, j, :, tok]).then_inc(s["qabs"], 1)
                    now = bass.ds(i * (B4 * DEC_SEQ), B4 * DEC_SEQ)
                    dve.tensor_copy(now_latT[:, :], new_latT[:, now]).then_inc(s["qabs"], 1)
                    dve.tensor_copy(now_krT[:, :], new_krT[:, now]).then_inc(s["qabs"], 1)
                    dve.tensor_copy(now_lat[:, :, :], new_lat[:, bass.ds(i * B4, B4), :]).then_inc(s["qabs"], 1)
                    use = [0]

                    def from_bank(out, cols_, done):
                        u = use[0]
                        use[0] += 1
                        dve.wait_ge(s["tdone"], i * TB + u + 1)
                        dve.tensor_copy(out, tp[u % 2][:, 0:cols_]).then_inc(s[done], 1)
                        return u

                    def release(name, value):
                        dve.wait_ge(s[name], value)
                        dve.sem_inc(s["t_free"], 1)

                    for b in range(B4):
                        if b >= 2:
                            dve.wait_ge(s["sdone"], i * (B4 * (CH + 1)) + (b - 1) * (CH + 1))
                        for c in range(CH):
                            from_bank(latT[:, b % 2, c * GROUP:(c + 1) * GROUP], GROUP, "latT")
                            release("latT", i * NTR + b * (CH + 1) + c + 1)
                        from_bank(krT[:, b % 2, :, :].rearrange("p c n -> p (c n)"), GROUP, "latT")
                        release("latT", i * NTR + (b + 1) * (CH + 1))
                    dve.wait_ge(s["sdone"], (i + 1) * (B4 * (CH + 1)))
                    dve.tensor_tensor(snew[:, :], sn[:, 0:DEC_SEQ], mask4[:, :], ALU.add).then_inc(s["snew"], 1)
                    for c in range(CH):
                        dve.reduce_max(mx[:, c:c + 1], sc[c][:, :], AXX).then_inc(s["mx"], 1)
                    dve.wait_ge(s["snew"], i + 1)
                    dve.reduce_max(mx[:, CH:CH + 1], snew[:, :], AXX).then_inc(s["mx"], 1)
                    dve.wait_ge(s["mx"], i * (CH + 2) + CH + 1)
                    dve.reduce_max(nm[:, 0:1], mx[:, :], AXX).then_inc(s["mx"], 1)
                    dve.wait_ge(s["mx"], (i + 1) * (CH + 2))
                    dve.tensor_scalar(nm[:, 1:2], nm[:, 0:1], -1.0, None, ALU.mult).then_inc(s["nm"], 1)
                    dve.wait_ge(s["exp"], (i + 1) * (CH + 1))
                    dve.sem_inc(s["sfree"], 1)
                    dve.reduce_sum(den[:, 0:1], dsum[:, :], AXX).then_inc(s["den"], 1)
                    dve.wait_ge(s["den"], i * 2 + 1)
                    dve.reciprocal(den[:, 1:2], den[:, 0:1]).then_inc(s["den"], 1)
                    for g in range(NPT):
                        k0, k1 = 4 * g, min(4 * g + 4, N_PAGES + 1)
                        from_bank(probT[:, k0:k1, :].rearrange("p k n -> p (k n)"), (k1 - k0) * P, "pT")
                        release("pT", i * NPT + g + 1)
                    dve.wait_ge(s["lat_free"], (i + 2) * B4)
                    dve.wait_ge(s["den"], i * 2 + 2)
                    dve.tensor_scalar(o_lat[:, :], acc[:, 0:KV_RANK], den[:, 1:2], None, ALU.mult).then_inc(s["olat"], 1)
                    from_bank(o_latT[:, :], P, "olT")
                    release("olT", i + 1)
                    dve.wait_ge(s["att"], i + 1)
                    dve.wait_ge(s["out"], i * 16 + 16)
                    dve.tensor_copy(o_att[:, :, :], acc[0:VDIM, GROUP // 2:GROUP // 2 + HEADS * 16].rearrange("p (h n) -> p h n", h=HEADS)).then_inc(s["oatt"], 1)


def stage4(nc, a, keep):
    ctx = ExitStack()
    with ctx:
        def sb(name, shape, dt=F32):
            return ctx.enter_context(nc.sbuf_tensor(name, shape, dt))

        def sem(name):
            return ctx.enter_context(nc.semaphore("s4_" + name))

        ident, rstd_all, rden = keep["ident"], keep["rstd_all"], keep["rden"]
        NT = SEQ // P
        MC = D_MIX // P
        WB = 2
        w_gate = keep["w_gate"]
        w_out = sb("w_out", [P, 2, MC, D_MODEL], F32R)
        g_post = sb("g_post", [P, D_MODEL])
        half, eps = sb("half4", [P, 1]), sb("eps4", [P, 1])
        stage = sb("stage4", [P, WB, D_MODEL])
        xraw = sb("xraw", [P, 2, KC, P])
        hT = sb("hT4", [P, 2, 2, KC, P], F32R)
        gate = sb("gate", [P, D_MIX])
        yt = sb("yt", [P, 2, MC, P])
        mf = sb("mf", [P, MC, P])
        m2 = sb("m2", [P, 2, MC, P], F32R)
        xt = sb("xt", [P, 2, D_MODEL])
        ot = sb("ot", [P, 2, D_MODEL])
        junk = sb("junk4", [P, GROUP], BF16)
        rs = sb("rs", [P, 2])
        sq, rq = sb("sq4", [P, 2, 2]), sb("rq4", [P, 2, 2])
        mm = [ctx.enter_context(nc.psum_tensor(f"m4_{i}", [P, GROUP], F32)) for i in range(4)]
        tp = [ctx.enter_context(nc.psum_tensor(f"t4_{i}", [P, GROUP], F32)) for i in range(2)]
        s = {n: sem(n) for n in ("xT_free", "split", "cols", "gates", "silu", "tr", "yr", "mix", "hi", "pair", "outs",
                                 "square", "rms", "mid", "final", "o_done", "gate_free", "out_free", "mixed", "g_post", "init", "x_hi", "w_hi", "w_lo")}
        staged = [sem(f"staged{i}") for i in range(WB)]
        x_ld, xt_ld, y_ld, stored = ([sem(f"{n}{i}") for i in range(2)] for n in ("x_ld", "xt_ld", "y_ld", "stored"))

        class Tile:

            def __init__(self, i, hf, smp=False):
                self.t, self.b, self.smp = i * 2 + hf, hf, smp
                self.i = i
                self.rows = SAMPLES if smp else P

        def over_tiles(eng, f):
            with eng.Fori(0, NT // 2) as i:
                for hf in range(2):
                    f(Tile(i, hf))
            f(Tile(NT // 2, 0, True))

        with nc.Block() as block:
            @block.sync
            def _(sp):
                def load_x(t, b, wait=True):
                    if wait:
                        sp.wait_ge(s["xT_free"], t - 1)
                    sp.dma_start(xraw[:, b, :, :], a["xT"][:, bass.ds(t * P, P)].rearrange("(k p) n -> p k n", p=P)).then_inc(x_ld[b], 16)

                def store(t, n, b):
                    sp.wait_ge(s["o_done"], t + 1)
                    sp.dma_start(a["y"][bass.ds(t * P, n), :], ot[0:n, b, :]).then_inc(stored[b], 16)

                def tile(T, ahead=True, back=True):
                    n = T.rows
                    if ahead:
                        load_x(T.t + 2, T.b)
                    if back:
                        sp.wait_ge(s["mixed"], T.t - 1)
                    sp.dma_start(yt[:, T.b, :, 0:n], a["Y"][:, bass.ds(T.t * P, n)].rearrange("(k p) n -> p k n", p=P)).then_inc(y_ld[T.b], 16)
                    if back:
                        store(T.t - 2, P, T.b)
                    sp.dma_start(xt[0:n, T.b, :], a["x"][bass.ds(T.t * P, n), :]).then_inc(xt_ld[T.b], 16)

                load_x(0, 0, False)
                load_x(1, 1, False)
                sp.dma_start(g_post[:, :], a["norm_post"].broadcast_to([P, D_MODEL])).then_inc(s["g_post"], 16)
                for k in range(MC):
                    if k >= WB:
                        sp.wait_ge(s["w_lo"], k - WB + 1)
                    sp.dma_start(stage[:, k % WB, :], a["w_out"][k * P:(k + 1) * P, :]).then_inc(staged[k % WB], 16)
                    if k == WB - 1:
                        tile(Tile(0, 0), back=False)
                        tile(Tile(0, 1), back=False)
                with sp.Fori(1, NT // 2 - 1) as i:
                    for hf in range(2):
                        tile(Tile(i, hf))
                tile(Tile(NT // 2 - 1, 0))
                tile(Tile(NT // 2 - 1, 1), ahead=False)
                tile(Tile(NT // 2, 0, True), ahead=False)
                store(NT - 1, P, 1)
                store(NT, SAMPLES, 0)
                sp.wait_ge(stored[0], 16 * (NT // 2 + 2))
                sp.wait_ge(stored[1], 16 * (NT // 2 + 1))

            @block.gpsimd
            def _(pool):
                pool.memset(half[:, :], -0.5).then_inc(s["init"], 1)
                pool.wait_ge(s["init"], 1)
                pool.memset(eps[:, :], EPS).then_inc(s["init"], 1)
                pool.wait_ge(s["init"], 2)
                pool.sem_inc(s["gate_free"], 2)
                pool.sem_inc(s["out_free"], 2)
                for b in stored:
                    pool.sem_inc(b, 16)

                def split(t, b):
                    pool.wait_ge(s["x_hi"], t + 1)
                    pool.tensor_tensor(hT[:, b, 1, :, :], xraw[:, b, :, :], f32(hT[:, b, 0, :, :]), ALU.subtract).then_inc(s["split"], 1)
                    pool.wait_ge(s["split"], t + 1)
                    pool.sem_inc(s["xT_free"], 1)

                def post(T):
                    n, b = T.rows, T.b
                    pool.wait_ge(s["square"], T.t * 2 + 2)
                    pool.tensor_tensor(rq[0:n, b, 0:1], sq[0:n, b, 0:1], sq[0:n, b, 1:2], ALU.add).then_inc(s["mid"], 1)
                    pool.wait_ge(s["mid"], T.t * 2 + 1)
                    pool.tensor_tensor(rq[0:n, b, 0:1], rq[0:n, b, 0:1], eps[0:n, :], ALU.add).then_inc(s["mid"], 1)
                    pool.wait_ge(s["mid"], T.t * 2 + 2)
                    pool.tensor_tensor(rq[0:n, b, 1:2], rq[0:n, b, 0:1], half[0:n, :], ALU.pow).then_inc(s["rms"], 1)
                    pool.wait_ge(s["final"], T.t * 2 + 2)
                    pool.wait_ge(xt_ld[b], T.i * 16 + 16)
                    pool.tensor_tensor(ot[0:n, b, :], ot[0:n, b, :], xt[0:n, b, :], ALU.add).then_inc(s["o_done"], 1)

                split(0, 0)
                split(1, 1)
                with pool.Fori(0, NT // 2 - 1) as i:
                    for hf in range(2):
                        T = Tile(i, hf)
                        split(T.t + 2, hf)
                        post(T)
                split(NT, 0)
                post(Tile(NT // 2 - 1, 0))
                post(Tile(NT // 2 - 1, 1))
                post(Tile(NT // 2, 0, True))

            @block.tensor
            def _(pe):
                def passes(out, w, x, n):
                    for k in range(n):
                        for q, (pw_, px) in enumerate(PASSES):
                            last = pe.matmul(out, w(pw_, k), x(px, k), start=(k == 0 and q == 0), stop=(k == n - 1 and q == 2))
                    return last

                def gates(t, b):
                    pe.wait_ge(s["split"], t + 1)
                    pe.wait_ge(s["gate_free"], t * 2 + 2)
                    for c in range(2):
                        ins = passes(mm[c][:, :], lambda i, k: hT[:, b, i, k, :], lambda i, k: w_gate[:, i, k, c * GROUP:(c + 1) * GROUP], KC)
                        ins.then_inc(s["gates"], 1)

                def transposes(T):
                    n, b = T.rows, T.b
                    for c in (1, 0):
                        if c:
                            pe.wait_ge(s["silu"], T.t * 2 + 2)
                        else:
                            pe.wait_ge(s["yr"], T.t + 1)
                        for k in range(4):
                            ins = pe.transpose(tp[c][:, k * P:k * P + n], gate[0:n, (4 * c + k) * P:(4 * c + k + 1) * P], ident[0:n, 0:n])
                        ins.then_inc(s["tr"], 1)

                def outs(T):
                    n = T.rows
                    pe.wait_ge(s["pair"], T.t * 2 + 2)
                    pe.wait_ge(s["out_free"], T.t * 2 + 2)
                    for c in range(2):
                        ins = passes(mm[2 + c][0:n, :], lambda i, k: m2[:, i, k, 0:n], lambda i, k: w_out[:, i, k, c * GROUP:(c + 1) * GROUP], MC)
                        ins.then_inc(s["outs"], 1)

                gates(0, 0)
                pe.wait_ge(s["w_lo"], MC)
                with pe.Fori(0, NT // 2) as i:
                    for hf in range(2):
                        T = Tile(i, hf)
                        transposes(T)
                        gates(T.t + 1, 1 - hf)
                        outs(T)
                T = Tile(NT // 2, 0, True)
                transposes(T)
                outs(T)

            @block.scalar
            def _(act):
                def silu(t, b):
                    for c in range(2):
                        act.wait_ge(s["gates"], t * 2 + c + 1)
                        act.activation(gate[:, c * GROUP:(c + 1) * GROUP], mm[c][:, :], ACT.Silu, scale=rs[:, b:b + 1]).then_inc(s["silu"], 1)
                    act.wait_ge(s["silu"], t * 2 + 2)
                    act.sem_inc(s["gate_free"], 2)

                def x_hi(T2, i, b):
                    act.activation(rs[:, b:b + 1], rstd_all[:, bass.ds(T2, 1)], ACT.Copy).then_inc(s["cols"], 1)
                    act.wait_ge(x_ld[b], i * 16 + 16)
                    act.activation(hT[:, b, 0, :, :], xraw[:, b, :, :], ACT.Copy).then_inc(s["x_hi"], 1)
                    act.wait_ge(s["x_hi"], T2 + 1)

                def hi(T):
                    for q, c in enumerate((1, 0)):
                        act.wait_ge(s["mix"], T.t * 2 + q + 1)
                        act.activation(m2[:, 0, 4 * c:4 * c + 4, 0:T.rows], mf[:, 4 * c:4 * c + 4, 0:T.rows], ACT.Copy).then_inc(s["hi"], 1)

                def squares(T):
                    n = T.rows
                    for c in range(2):
                        act.wait_ge(s["outs"], T.t * 2 + c + 1)
                        act.activation(junk[0:n, :], mm[2 + c][0:n, :], ACT.Square, scale=D_MODEL ** -0.5, accum_out=sq[0:n, T.b, c:c + 1]).then_inc(s["square"], 1)
                        act.wait_ge(s["square"], T.t * 2 + c + 1)

                x_hi(0, 0, 0)
                x_hi(1, 0, 1)
                for k in range(MC):
                    act.wait_ge(staged[k % WB], 16 * (k // WB) + 16)
                    act.activation(w_out[:, 0, k, :], stage[:, k % WB, :], ACT.Copy).then_inc(s["w_hi"], 1)
                silu(0, 0)

                def tile(T, ahead=True):
                    if ahead:
                        x_hi(T.t + 2, T.i + 1, T.b)
                    hi(T)
                    silu(T.t + 1, 1 - T.b)
                    squares(T)

                with act.Fori(0, NT // 2 - 1) as i:
                    for hf in range(2):
                        tile(Tile(i, hf))
                tile(Tile(NT // 2 - 1, 0))
                tile(Tile(NT // 2 - 1, 1), ahead=False)
                T = Tile(NT // 2, 0, True)
                hi(T)
                squares(T)

            @block.vector
            def _(dve):
                def divide(t):
                    dve.wait_ge(s["silu"], t * 2 + 1)
                    g4 = gate[:, 0:ATT_W].rearrange("p (h d) -> p h d", d=VDIM)
                    dve.tensor_tensor(g4, g4, rden[:, :, bass.ds(t, 1)].broadcast_to([P, HEADS, VDIM]), ALU.mult).then_inc(s["yr"], 1)

                def tile(T):
                    n, b = T.rows, T.b
                    dve.wait_ge(y_ld[b], T.i * 16 + 16)
                    for q, c in enumerate((1, 0)):
                        dve.wait_ge(s["tr"], T.t * 2 + 1 + q)
                        dve.tensor_tensor(mf[:, 4 * c:4 * c + 4, 0:n], tp[c][:, :].rearrange("p (k n) -> p k n", k=4)[:, :, 0:n],
                                          yt[:, b, 4 * c:4 * c + 4, 0:n], ALU.mult).then_inc(s["mix"], 1)
                    for q, c in enumerate((1, 0)):
                        dve.wait_ge(s["hi"], T.t * 2 + q + 1)
                        dve.tensor_tensor(m2[:, 1, 4 * c:4 * c + 4, 0:n], mf[:, 4 * c:4 * c + 4, 0:n], f32(m2[:, 0, 4 * c:4 * c + 4, 0:n]),
                                          ALU.subtract).then_inc(s["pair"], 1)
                    dve.wait_ge(s["mix"], T.t * 2 + 2)
                    dve.sem_inc(s["mixed"], 1)
                    if not T.smp:
                        divide(T.t + 1)
                    dve.wait_ge(s["rms"], T.t + 1)
                    dve.wait_ge(stored[b], T.i * 16 + 16)
                    for c in range(2):
                        dve.scalar_tensor_tensor(ot[0:n, b, c * GROUP:(c + 1) * GROUP], mm[2 + c][0:n, :], rq[0:n, b, 1:2],
                                                 g_post[0:n, c * GROUP:(c + 1) * GROUP], ALU.mult, ALU.mult).then_inc(s["final"], 1)
                    dve.wait_ge(s["final"], T.t * 2 + 2)
                    dve.sem_inc(s["out_free"], 2)

                for k in range(MC):
                    dve.wait_ge(s["w_hi"], k + 1)
                    dve.tensor_tensor(w_out[:, 1, k, :], stage[:, k % WB, :], f32(w_out[:, 0, k, :]), ALU.subtract).then_inc(s["w_lo"], 1)
                dve.wait_ge(s["g_post"], 16)
                divide(0)
                over_tiles(dve, tile)


def build(nc, a):
    with nc.sbuf_tensor("ident", [P, P], F32) as ident, nc.sbuf_tensor("rstd_all", [P, GROUPS * TILES + 1], F32) as rstd_all:
        keep = {"ident": ident, "rstd_all": rstd_all}
        stage1(nc, a, keep)
        nc.clear_and_free_semaphores(keep["stage1_sems"])
        nc.all_engine_barrier()
        with nc.sbuf_tensor("rden", [P, HEADS, GROUPS * TILES + 1], F32) as rden:
            keep["rden"] = rden
            stage2(nc, a, keep)
            with nc.sbuf_tensor("w_gate", [P, 2, KC, D_MIX], F32R) as w_gate:
                keep["w_gate"] = w_gate
                stage3(nc, a, keep)
                stage4(nc, a, keep)


def _columns(np, v, n):
    return np.ascontiguousarray(np.asarray(v).reshape(n, 128).T)


def _arrange(np, i):
    f = np.float32
    x = np.zeros((SEQ + GROUP, D_MODEL), f)
    x[:SEQ] = i["x_prompt"][0]
    x[SEQ:SEQ + SAMPLES] = i["x_sample"].reshape(SAMPLES, D_MODEL)
    w = i["w_in"][0]
    o_pool = TOK_COLS
    o_conv = o_pool + POOL_W
    o_gate = o_conv + 2 * CONV_W
    order = [w[:, :TOK_COLS]]
    for c in range(CC):
        order += [w[:, o_conv + CONV_W + c * P:o_conv + CONV_W + (c + 1) * P], w[:, o_conv + c * P:o_conv + (c + 1) * P]]
    order.append(w[:, o_pool:o_pool + POOL_W])
    uq = i["w_uq"][0].reshape(Q_RANK, HEADS, NOPE + ROPE)
    uq = np.concatenate([uq, uq[:, :, NOPE + HALF:], uq[:, :, NOPE:NOPE + HALF]], axis=2)
    gate_order = w[:, o_gate:]
    blocks = np.zeros((P, CC, P), f)
    for g in range(4):
        r = (g % 2) * 64
        blocks[r:r + 64, g // 2, r:r + 64] = i["pool_w"][0, g]
    dw = i["conv_dw"][0]
    windows = np.array([2, 4, 8, 16])
    win = np.repeat(windows, 64).reshape(CC, P).T
    cols = np.concatenate([
        _columns(np, i["norm_pre"][0], 8), _columns(np, i["q_norm"][0], 2), _columns(np, i["pool_scale"][0], 2),
        _columns(np, i["conv_ln_g"][0], 2), _columns(np, i["conv_ln_b"][0], 2), _columns(np, i["conv_b"][0], 2),
        (f(1) / win.astype(f)), dw.reshape(CONV_K, CC, P).transpose(2, 1, 0).reshape(P, CC * CONV_K)], axis=1)
    inv = (f(10000.0) ** (-np.arange(0, ROPE, 2, dtype=f) / f(ROPE))).astype(f)
    pos = np.arange(SEQ + SAMPLES)
    pos[SEQ:] = N_PAGES * PAGE + np.arange(SAMPLES) % DEC_SEQ
    ang = pos.astype(f)[:, None] * inv[None, :]
    cos, sin = np.cos(ang).astype(f), np.sin(ang).astype(f)
    scale = f((NOPE + ROPE) ** -0.5)
    cs_T = np.concatenate([np.full((SEQ + SAMPLES, NOPE), scale), cos * scale, cos * scale, -sin * scale, sin * scale], axis=1).T
    cs_tok = np.zeros(((GROUPS + 1) * GROUP, ROPE), f)
    cs_tok[:SEQ + SAMPLES] = np.concatenate([cos, sin], axis=1)
    cs_tok = cs_tok.reshape(GROUPS + 1, TILES, P, ROPE).transpose(0, 2, 1, 3)
    icnt = np.ones((GROUPS, UH)) * 1.0
    t = np.arange(GROUPS)[:, None] * GROUP + np.arange(UH)[None, :]
    icnt = 1.0 / np.minimum(t[None, :, None, :] + 1, win[:, None, :, None])
    return {
        "x": x, "xT": x.T, "w_in": np.concatenate(order, axis=1), "w_uq": uq.reshape(Q_RANK, HEADS * P),
        "w_uk": i["w_uk"][0].reshape(KV_RANK, HEADS * NOPE), "w_uv": i["w_uv"][0].reshape(KV_RANK, HEADS * VDIM),
        "cols": cols.astype(f), "kv_norm": i["kv_norm"][0].reshape(1, KV_RANK), "ident": np.eye(P, dtype=f),
        "cs_T": cs_T.astype(f), "cs_tok": cs_tok, "icnt": icnt.astype(f), "conv_pw": i["conv_pw"][0], "pool_w": blocks,
        "state_conv": i["state_conv"][0].reshape(DEC_BATCH, CONV_HIST, CC, P).transpose(3, 2, 0, 1),
        "state_pool": i["state_pool"][0].reshape(DEC_BATCH, POOL_HIST, CC, P).transpose(3, 2, 0, 1),
        "w_gate": gate_order, "w_out": i["w_out"][0], "norm_post": i["norm_post"][0].reshape(1, D_MODEL),
        "cache_ckv": i["cache_ckv"][0], "cache_krope": i["cache_krope"][0],
        "page_table": np.asarray(i["page_table"]).astype(np.int32).reshape(1, DEC_BATCH * N_PAGES),
        "w_ukT": i["w_uk"][0].transpose(2, 1, 0),
        "norm_pre_c": _columns(np, i["norm_pre"][0], 8),
        "causal": np.where(np.arange(P)[None, :] <= np.arange(P)[:, None], 0.0, -1e30).astype(f),
        "causal4": np.where(np.arange(DEC_SEQ)[None, :] <= (np.arange(P) % DEC_SEQ)[:, None], 0.0, -1e30).astype(f),
    }


_OUT = {"y": (SEQ + SAMPLES, D_MODEL), "ckv_p": (SEQ, KV_RANK), "krope_p": (SEQ, ROPE), "pool_p": (POOL_W, POOL_HIST),
        "conv_p": (CONV_W, CONV_HIST), "ckv_s": (SAMPLES, KV_RANK), "krope_s": (SAMPLES, ROPE),
        "pool_s": (P, CC, DEC_BATCH, POOL_HIST), "conv_s": (P, CC, DEC_BATCH, CONV_HIST)}
_SCRATCH = {"QT": (HEADS * P, SEQ + SAMPLES), "KT": (HEADS * NOPE, SEQ + SAMPLES), "KRT": (P - NOPE, SEQ + SAMPLES),
            "V": (SEQ + 4 * SAMPLES, ATT_W), "Y": (D_MIX, SEQ + SAMPLES), 
            "LAT": (DEC_BATCH, N_PAGES, PAGE, KV_RANK), "KR": (DEC_BATCH, N_PAGES, PAGE, ROPE)}


def program(nc, arrays, scratch_kind="Internal"):
    a = {n: nc.dram_tensor("in_" + n, v.shape, mybir.dt.from_np(v.dtype), kind="ExternalInput").ap() for n, v in arrays.items()}
    a |= {n: nc.dram_tensor("out_" + n, shape, F32, kind="ExternalOutput").ap() for n, shape in _OUT.items()}
    a |= {n: nc.dram_tensor(n, shape, F32, kind=scratch_kind).ap() for n, shape in _SCRATCH.items()}
    build(nc, a)


def kernel(**inputs):
    import concourse.bacc as bacc
    import numpy as np
    from concourse.bass_utils import run_bass_kernel_spmd

    inputs = {n: np.asarray(v) for n, v in inputs.items()}
    arrays = {n: np.ascontiguousarray(v) for n, v in _arrange(np, inputs).items()}
    nc = bacc.Bacc("TRN2", target_bir_lowering=False, num_devices=1)
    program(nc, arrays)
    r = run_bass_kernel_spmd(nc, [{"in_" + n: v for n, v in arrays.items()}], core_ids=[0]).results[0]
    o = {n: np.asarray(r["out_" + n]) for n in _OUT}

    def state(v):
        return np.ascontiguousarray(v.transpose(2, 3, 1, 0)).reshape(1, DEC_BATCH, v.shape[3], CC * P)

    return (o["y"][:SEQ].reshape(1, SEQ, D_MODEL), o["y"][SEQ:].reshape(DEC_BATCH, DEC_SEQ, D_MODEL),
            o["ckv_p"].reshape(1, 1, SEQ, KV_RANK), o["krope_p"].reshape(1, 1, SEQ, ROPE),
            np.ascontiguousarray(o["pool_p"].T)[None, None], np.ascontiguousarray(o["conv_p"].T)[None, None],
            o["ckv_s"].reshape(1, DEC_BATCH, DEC_SEQ, KV_RANK), o["krope_s"].reshape(1, DEC_BATCH, DEC_SEQ, ROPE),
            state(o["pool_s"]), state(o["conv_s"]))
```

```python
from contextlib import ExitStack

import concourse.bass as bass
from concourse import mybir
from concourse.alu_op_type import AluOpType as ALU

F32 = mybir.dt.float32
F32R = mybir.dt.float32r
BF16 = mybir.dt.bfloat16
I32 = mybir.dt.int32
ACT = mybir.ActivationFunctionType
AXX = mybir.AxisListType.X

P = 128
D_MODEL, D_MIX = 1024, 1024
SEQ, DEC_BATCH, DEC_SEQ = 2048, 8, 4
SAMPLES = DEC_BATCH * DEC_SEQ
HEADS, NOPE, ROPE, VDIM = 8, 64, 32, 64
HALF = ROPE // 2
Q_RANK, KV_RANK = 256, 128
POOL_W, CONV_W = 256, 256
POOL_HIST, CONV_K = 15, 31
CONV_HIST = CONV_K - 1
ATT_W = HEADS * VDIM
PAGE, N_PAGES = 128, 16
EPS = 1e-6

GROUP = 512
TILES = GROUP // P
GROUPS = SEQ // GROUP
KC = D_MODEL // P
TOK_COLS = Q_RANK + KV_RANK + ROPE
IN1 = TOK_COLS + 2 * CONV_W + POOL_W
QC, CC = Q_RANK // P, CONV_W // P
UH = POOL_HIST + 1
PASSES = ((0, 0), (1, 0), (0, 1))
N_COLS = 10 + 10 + CC * CONV_K


def f32(ap):
    return ap.bitcast(F32)


def spread(col, ap):
    if len(ap.shape) == 3:
        col = col.rearrange("p (a b) -> p a b", a=1)
    if len(ap.shape) == 4:
        col = col.rearrange("p (a b c) -> p a b c", a=1, b=1)
    return col.broadcast_to(list(ap.shape))


class Banks:

    def __init__(self, sem, name, tensors, per_group):
        self.t, self.n = tensors, len(tensors)
        self.per = per_group // self.n
        self.done = [sem(f"{name}_done{b}") for b in range(self.n)]
        self.free = [sem(f"{name}_free{b}") for b in range(self.n)]

    def count(self, it, job):
        return it * self.per + job // self.n + 1

    def wait_free(self, eng, it, job):
        eng.wait_ge(self.free[job % self.n], self.count(it, job))
        return self.t[job % self.n]

    def wait_done(self, eng, it, job):
        eng.wait_ge(self.done[job % self.n], self.count(it, job))
        return self.t[job % self.n]


def stage1(nc, a, keep):
    ctx = ExitStack()
    with ctx:
        def sb(name, shape, dt=F32):
            return ctx.enter_context(nc.sbuf_tensor(name, shape, dt))

        def sem(name):
            sems.append(nc.alloc_semaphore("s1_" + name))
            return sems[-1]

        sems = keep["stage1_sems"] = []
        ident, rstd_all = keep["ident"], keep["rstd_all"]
        w_in = sb("w_in", [P, 2, KC, IN1], F32R)
        w_uq = sb("w_uq", [P, 2, QC, HEADS * P], F32R)
        w_uk = sb("w_uk", [P, 2, HEADS * NOPE], F32R)
        w_uv = sb("w_uv", [P, 2, HEADS * VDIM], F32R)
        cols = sb("cols", [P, N_COLS])
        g_pre, g_q = cols[:, 0:8], cols[:, 8:10]
        pool_s, ln_g, ln_b = cols[:, 10:12], cols[:, 12:14], cols[:, 14:16]
        conv_b, inv_w = cols[:, 16:18], cols[:, 18:20]
        dw = cols[:, 20:].rearrange("p (c k) -> p c k", c=CC)
        g_kv = sb("g_kv", [P, KV_RANK])
        half, eps = sb("half", [P, 2 * TILES]), sb("eps", [P, 2 * TILES])
        zero, inv_rank = sb("zero", [P, 1]), sb("inv_rank", [P, 2 * TILES])

        xT = sb("xT", [P, 2, GROUP])
        hT = sb("hT", [P, 2, KC, GROUP], F32R)
        xtok = sb("xtok", [P, D_MODEL])
        junk = sb("junk", [P, Q_RANK], BF16)
        ssx, rx = sb("ssx", [P, TILES]), sb("rx", [P, TILES])
        ssq, rq = sb("ssq", [P, 2 * TILES]), sb("rq", [P, 2 * TILES])
        rb = sb("rb", [P, GROUP])
        zt = sb("zt", [P, TILES, TOK_COLS])
        krd = sb("krd", [P, TILES, P])
        rope4 = sb("rope4", [P, 4, TILES, HALF])
        cq = sb("cq", [P, 2, QC, GROUP], F32R)
        ckv = sb("ckv", [P, 2, GROUP], F32R)
        cs = sb("cs", [P, GROUP])
        cst = sb("cst", [P, TILES, ROPE])
        sg = sb("sg", [P, GROUP])
        krt = sg
        aT = sb("aT", [P, CC, CONV_HIST + GROUP])
        uT = sb("uT", [P, CC, UH + GROUP])
        icnt = sb("icnt", [P, GROUPS, CC, UH])
        sA, sB = sb("sA", [P, CC, UH + GROUP]), sb("sB", [P, CC, UH + GROUP])
        y = sb("y", [P, CC, GROUP])
        yn = sb("yn", [P, TILES, CONV_W])
        ya = yn[:, :, :].rearrange("p j n -> p (j n)").rearrange("p (c n) -> p c n", c=CC)
        st6, mv, ry = sb("st6", [P, TILES, 6]), sb("mv", [P, TILES, 2]), sb("ry", [P, TILES])
        qst, kst = sb("qst", [P, 2, GROUP]), sb("kst", [P, 2, GROUP])
        aS = sb("aS", [P, CC, DEC_BATCH, CONV_HIST + DEC_SEQ])
        uS = sb("uS", [P, CC, DEC_BATCH, UH + DEC_SEQ])
        pw, plw = sb("pw", [P, CC, CONV_W]), sb("plw", [P, CC, P])
        mm = Banks(sem, "mm", [ctx.enter_context(nc.psum_tensor(f"mm{i}", [P, GROUP], F32)) for i in range(4)], 28)
        tr = Banks(sem, "tr", [ctx.enter_context(nc.psum_tensor(f"tr{i}", [P, GROUP], F32)) for i in range(2)], 6)
        cv = Banks(sem, "cv", [ctx.enter_context(nc.psum_tensor(f"cv{i}", [P, GROUP], F32)) for i in range(2)], 8)

        s = {n: sem(n) for n in (
            "const", "split", "hT_free", "xtok_ld", "xtok_free", "rx", "rx_free", "rb", "u_ld",
            "sgate", "sig", "aval", "glu", "a_free", "upool", "u_free", "conv", "z", "zt_free", "ckv_out",
            "ssq", "rq", "nrm", "kr", "krd_free", "kr_out", "hi", "pair", "krt", "krt_out", "cs_ld", "cst_ld", "cs_free",
            "qst", "kst", "d", "pool", "mv", "ry", "yn", "act", "prep", "tail_out", "rmid", "stats", "x_hi", "rstd", "vmid", "small", "vst")}
        xt_ld = [sem(f"xt_ld{i}") for i in range(4)]
        q_out, k_out = ([sem(f"{n}{i}") for i in range(2)] for n in ("q_out", "k_out"))

        load, w_hi, w_lo = sem("load"), sem("w_hi"), sem("w_lo")
        WS = [t[:, :, :].rearrange("p c n -> p (c n)") for t in (y, yn, qst, kst)]
        staged = [sem(f"staged{i}") for i in range(len(WS))]
        parts = [(a["w_in"][k * P:(k + 1) * P, c0:c1], w_in[:, 0, k, c0:c1], w_in[:, 1, k, c0:c1], g_pre[:, k:k + 1])
                 for c0, c1 in ((0, TOK_COLS), (TOK_COLS, IN1)) for k in range(KC)]
        parts += [(a["w_uq"][k * P:(k + 1) * P, :], w_uq[:, 0, k, :], w_uq[:, 1, k, :], g_q[:, k:k + 1])
                  for k in range(QC)]
        parts += [(a["w_uk"], w_uk[:, 0, :], w_uk[:, 1, :], 1.0), (a["w_uv"], w_uv[:, 0, :], w_uv[:, 1, :], 1.0)]
        W_TOK, W_T, W_Q, W_ALL = 0, KC, 2 * KC + QC, 2 * KC + QC + 2

        def staging(n):
            return WS[n % len(WS)][:, 0:parts[n][0].shape[1]], staged[n % len(WS)], 16 * (n // len(WS)) + 16

        def xbuf(k):
            return xT[:, k % 2, :] if k % 4 < 2 else sB[:, k % 2, 0:GROUP]

        TOK0, T0, Q0, SPARE0 = 0, 4, 10, 26
        KV = (("k", 0), ("k", 1), ("v", 0), ("v", 1), ("k", 2), ("k", 3), ("v", 2), ("v", 3))
        KV0 = 18
        T_R, T_CQ, T_CKV, T_KR, T_SPARE = 0, 1, 3, 4, 5
        PL, YF, YB, CV = 0, 2, 4, 6
        KST, QST = 8, HEADS + TILES
        POOL_OPS, CONV_OPS = 10, CC * CONV_K
        TAPS_OWN = 40

        class Group:

            def __init__(self, it, smp):
                self.it, self.smp = it, smp
                self.n, self.tiles, self.rows = (SAMPLES, 1, SAMPLES) if smp else (GROUP, TILES, P)

            def wait(self, eng, name, per, n):
                eng.wait_ge(s[name] if isinstance(name, str) else name, self.it * per + n)

            def bl(self, ap):
                return ap.rearrange("p (b l) -> p b l", l=DEC_SEQ) if self.smp else ap

        def over_groups(eng, group, tail, between=None):
            group(Group(0, False), None)
            with eng.Fori(1, GROUPS) as it:
                group(Group(it, False), Group(it - 1, False))
            if between:
                between()
            group(Group(GROUPS, True), Group(GROUPS - 1, False))
            tail(Group(GROUPS, True))

        with nc.Block() as block:
            @block.sync
            def _(sp):
                sp.dma_start(cols[:, :], a["cols"]).then_inc(load, 16)
                sp.dma_start(ident[:, :], a["ident"]).then_inc(load, 16)
                for n, (src, _, _, _) in enumerate(parts):
                    if n >= len(WS):
                        sp.wait_ge(w_lo, n - len(WS) + 1)
                    raw, landed, _ = staging(n)
                    sp.dma_start(raw, src).then_inc(landed, 16)
                sp.dma_start(g_kv[:, :], a["kv_norm"].broadcast_to([P, KV_RANK])).then_inc(s["const"], 16)
                sp.dma_start(icnt[:, :, :, :], a["icnt"]).then_inc(s["const"], 16)
                sp.dma_start(pw[:, :, :], a["conv_pw"].rearrange("(c p) n -> p c n", p=P)).then_inc(s["const"], 16)
                sp.dma_start(plw[:, :, :], a["pool_w"]).then_inc(s["const"], 16)
                sp.dma_start(aS[:, :, :, 0:CONV_HIST], a["state_conv"]).then_inc(s["const"], 16)
                sp.dma_start(uS[:, :, :, 1:UH], a["state_pool"]).then_inc(s["const"], 16)

                def store_k(G, n):
                    G.wait(sp, "kst", KST, n + 1)
                    dst = a["KT"][n * P:(n + 1) * P, :] if n < 4 else a["Y"][ATT_W + (n - 4) * P:ATT_W + (n - 3) * P, :]
                    sp.dma_start(dst[:, bass.ds(SEQ if G.smp else G.it * GROUP, G.n)], kst[:, n % 2, 0:G.n]).then_inc(k_out[n % 2], 16)

                def store_v(G, j):
                    G.wait(sp, "vst", TILES, j + 1)
                    first = SEQ + j * SAMPLES if G.smp else G.it * GROUP + j * P
                    sp.dma_start(a["V"][bass.ds(first, G.rows), :], qst[0:G.rows, j % 2, :]).then_inc(q_out[j % 2], 16)

                def tail(G):
                    for n in range(4, KST):
                        store_k(G, n)

                def group(G, before):
                    it = G.it
                    first = SEQ if G.smp else it * GROUP
                    rows = bass.ds(first, G.n)
                    G.wait(sp, "cs_free", 1, 1)
                    sp.dma_start(cs[:, 0:G.n], a["cs_T"][:, rows]).then_inc(s["cs_ld"], 16)
                    G.wait(sp, "kr", 1, 1)
                    sp.dma_start(cst[:, :, :], a["cs_tok"][bass.ds(GROUPS if G.smp else it, 1), :, :, :].rearrange("o p j n -> (o p) j n")).then_inc(s["cst_ld"], 16)
                    G.wait(sp, "nrm", 2 * TILES, 2 * G.tiles)
                    lat = zt[0:G.rows, 0:G.tiles, Q_RANK:Q_RANK + KV_RANK]
                    rot = krd[0:G.rows, 0:G.tiles, NOPE:NOPE + ROPE]
                    if G.smp:
                        sp.dma_start(a["ckv_s"], lat[:, 0, :]).then_inc(s["ckv_out"], 16)
                        G.wait(sp, "kr", 1, 2)
                        sp.dma_start(a["krope_s"], rot[:, 0, :]).then_inc(s["kr_out"], 16)
                    else:
                        sp.dma_start(a["ckv_p"][rows, :].rearrange("(j p) n -> p j n", p=P), lat).then_inc(s["ckv_out"], 16)
                        G.wait(sp, "kr", 1, 2)
                        sp.dma_start(a["krope_p"][rows, :].rearrange("(j p) n -> p j n", p=P), rot).then_inc(s["kr_out"], 16)
                    if before:
                        tail(before)
                    G.wait(sp, "krt", 1, 1)
                    sp.dma_start(a["KRT"][:, rows], krt[NOPE:P, 0:G.n]).then_inc(s["krt_out"], 16)
                    for h in range(HEADS):
                        G.wait(sp, "qst", HEADS, h + 1)
                        sp.dma_start(a["QT"][h * P:(h + 1) * P, rows], qst[:, h % 2, 0:G.n]).then_inc(q_out[h % 2], 16)
                    for kind, n in KV:
                        (store_k if kind == "k" else store_v)(G, n)

                def histories():
                    sp.wait_ge(s["u_free"], GROUPS + 1)
                    sp.dma_start(a["pool_p"].rearrange("(c p) n -> p c n", p=P), uT[:, :, 1:UH]).then_inc(s["tail_out"], 16)
                    sp.wait_ge(s["a_free"], GROUPS + 1)
                    sp.dma_start(a["conv_p"].rearrange("(c p) n -> p c n", p=P), aT[:, :, 0:CONV_HIST]).then_inc(s["tail_out"], 16)

                over_groups(sp, group, tail, histories)
                sp.dma_start(a["pool_s"], uS[:, :, :, DEC_SEQ + 1:]).then_inc(s["tail_out"], 16)
                sp.dma_start(a["conv_s"], aS[:, :, :, DEC_SEQ:]).then_inc(s["tail_out"], 16)
                sp.wait_ge(s["tail_out"], 64)
                for name in ("ckv_out", "kr_out", "krt_out"):
                    sp.wait_ge(s[name], 16 * (GROUPS + 2))
                for i in range(2):
                    sp.wait_ge(q_out[i], 16 * (QST // 2 * (GROUPS + 1) + 1))
                    sp.wait_ge(k_out[i], 16 * (KST // 2 * (GROUPS + 1) + 1))

            @block.gpsimd
            def _(pool):
                for name in ("rx_free", "a_free", "u_free", "krd_free", "zt_free", "cs_free", "kr"):
                    pool.sem_inc(s[name], 1)
                for sm in (s["ckv_out"], s["kr_out"], s["krt_out"], *q_out, *k_out):
                    pool.sem_inc(sm, 16)
                for b in (*mm.free, *tr.free, *cv.free):
                    pool.sem_inc(b, 1)

                def load_chunk(first, k):
                    pool.dma_start(xbuf(k), a["xT"][k * P:(k + 1) * P, bass.ds(first, GROUP)]).then_inc(xt_ld[k % 4], 16)

                for k in range(4):
                    load_chunk(0, k)
                for t, v in ((half[:, :], -0.5), (eps[:, :], EPS), (zero[:, :], 0.0), (inv_rank[:, 0:TILES], 1.0 / Q_RANK),
                             (inv_rank[:, TILES:], 1.0 / KV_RANK)):
                    pool.memset(t, v).then_inc(s["prep"], 1)
                pool.memset(krd[:, :, :], 0.0).then_inc(s["prep"], 1)
                pool.memset(aT[:, :, 0:CONV_HIST], 0.0).then_inc(s["prep"], 1)
                pool.memset(uT[:, :, 0:UH], 0.0).then_inc(s["prep"], 1)
                pool.memset(uS[:, :, :, 0:1], 0.0).then_inc(s["prep"], 1)
                pool.memset(rstd_all[:, :], 0.0).then_inc(s["prep"], 1)
                pool.wait_ge(s["prep"], 10)

                def rms_x(value):
                    pool.tensor_tensor(ssx[:, :], ssx[:, :], eps[:, 0:TILES], ALU.add).then_inc(s["rmid"], 1)
                    pool.wait_ge(s["rmid"], value)
                    pool.tensor_tensor(rx[:, :], ssx[:, :], half[:, 0:TILES], ALU.pow).then_inc(s["rx"], 1)

                def copy(dst, src):
                    p0 = P - dst.shape[0]
                    return pool.tensor_tensor(dst, src, spread(zero[p0:P, :], dst), ALU.add)

                def second_parts(g):
                    for k in range(KC):
                        pool.wait_ge(s["x_hi"], g * KC + k + 1)
                        pool.tensor_tensor(hT[:, 1, k, :], xbuf(k), f32(hT[:, 0, k, :]), ALU.subtract).then_inc(s["split"], 1)
                        if k + 4 < KC:
                            pool.wait_ge(s["split"], g * KC + k + 1)
                            load_chunk(g * GROUP, k + 4)

                def inv_std(G):
                    nt, rows = G.tiles, G.rows
                    G.wait(pool, "mv", TILES, nt)
                    pool.tensor_tensor(mv[0:rows, 0:nt, 1], mv[0:rows, 0:nt, 1], eps[0:rows, 0:nt], ALU.add).then_inc(s["vmid"], 1)
                    G.wait(pool, "vmid", 1, 1)
                    pool.tensor_tensor(ry[0:rows, 0:nt], mv[0:rows, 0:nt, 1], half[0:rows, 0:nt], ALU.pow).then_inc(s["ry"], 1)

                second_parts(0)
                pool.wait_ge(s["xtok_free"], TILES)
                rms_x(1)
                pool.wait_ge(s["const"], 96)

                def pooling(G):
                    it = G.it
                    done = [0]

                    def step(ins):
                        ins.then_inc(s["pool"], 1)
                        done[0] += 1
                        G.wait(pool, "pool", POOL_OPS, done[0])

                    G.wait(pool, "upool", CC, CC)
                    L = UH + (DEC_SEQ if G.smp else GROUP)

                    def cut(t, c0, c1, p0, lo, hi):
                        if not G.smp:
                            return t[p0:P, c0:c1, lo:hi]
                        if t is uS:
                            return t[p0:P, c0:c1, :, lo:hi]
                        v = t[p0:P, :, :].rearrange("p c n -> p (c n)")[:, 0:CC * DEC_BATCH * L]
                        return v.rearrange("p (c b n) -> p c b n", c=CC, b=DEC_BATCH)[:, c0:c1, :, lo:hi]

                    def both(c0, c1, f):
                        if not G.smp:
                            return [f(c0, c1)]
                        return [f(c, c + 1) for c in range(c0, c1)]

                    def add(dst, src, c0, c1, p0, lo, w):
                        if G.smp:
                            for c in range(c0, c1):
                                last = pool.tensor_tensor(cut(dst, c, c + 1, p0, lo, L), cut(src, c, c + 1, p0, lo, L),
                                                          cut(src, c, c + 1, p0, lo - w, L - w), ALU.add)
                                step(last)
                        else:
                            step(pool.tensor_tensor(cut(dst, c0, c1, p0, lo, L), cut(src, c0, c1, p0, lo, L),
                                                    cut(src, c0, c1, p0, lo - w, L - w), ALU.add))

                    u = uS if G.smp else uT
                    add(sA, u, 0, 2, 0, 1, 1)
                    add(sB, sA, 0, 2, 0, 3, 2)
                    step(copy(cut(sA, 0, 1, 64, UH, L), cut(sB, 0, 1, 64, UH, L)))
                    add(sA, sB, 1, 2, 0, 7, 4)
                    add(sB, sA, 1, 2, 64, 15, 8)
                    step(copy(cut(sA, 1, 2, 64, UH, L), cut(sB, 1, 2, 64, UH, L)))
                    for c in range(CC):
                        if G.smp:
                            part = sA[:, :, :].rearrange("p c n -> p (c n)")[:, c * DEC_BATCH * L:(c + 1) * DEC_BATCH * L].rearrange("p (b n) -> p b n", b=DEC_BATCH)[:, :, UH:]
                            last = pool.tensor_tensor(part, part, spread(inv_w[:, c:c + 1], part), ALU.mult)
                        else:
                            step(pool.tensor_tensor(sA[:, c, UH:2 * UH], sA[:, c, UH:2 * UH],
                                                    icnt[:, bass.ds(it, 1), c, :].rearrange("p o n -> p (o n)"), ALU.mult))
                            last = pool.tensor_tensor(sA[:, c, 2 * UH:L], sA[:, c, 2 * UH:L], spread(inv_w[:, c:c + 1], sA[:, c, 2 * UH:L]), ALU.mult)
                        step(last)
                    for c in range(CC):
                        pool.tensor_tensor(cut(sA, c, c + 1, 0, UH, L), cut(sA, c, c + 1, 0, UH, L), cut(u, c, c + 1, 0, UH, L),
                                           ALU.subtract).then_inc(s["d"], 1)
                    G.wait(pool, "d", CC, CC)
                    if not G.smp:
                        copy(uT[:, :, 1:UH], uT[:, :, GROUP + 1:]).then_inc(s["u_free"], 1)
                    assert G.smp or done[0] == POOL_OPS, done

                def tail(G):
                    pooling(G)
                    inv_std(G)

                def group(G, before):
                    it, n, nt, rows = G.it, G.n, G.tiles, G.rows
                    done = [0]

                    def step(ins):
                        ins.then_inc(s["small"], 1)
                        done[0] += 1
                        G.wait(pool, "small", 6, done[0])

                    if not G.smp:
                        G.wait(pool, "split", KC, KC)
                        for k in range(2):
                            load_chunk(it * GROUP + GROUP, k)
                    if before:
                        pooling(before)
                    if not G.smp:
                        for k in (2, 3):
                            load_chunk(it * GROUP + GROUP, k)
                    G.wait(pool, "ssq", 2 * TILES, 2 * nt)
                    step(pool.tensor_tensor(ssq[0:rows, :], ssq[0:rows, :], inv_rank[0:rows, :], ALU.mult))
                    step(pool.tensor_tensor(ssq[0:rows, :], ssq[0:rows, :], eps[0:rows, :], ALU.add))
                    pool.tensor_tensor(rq[0:rows, :], ssq[0:rows, :], half[0:rows, :], ALU.pow).then_inc(s["rq"], 1)
                    G.wait(pool, "krd_free", 1, 1)
                    G.wait(pool, "kr_out", 16, 16)
                    x1, x2 = (zt[0:rows, 0:nt, TOK_COLS - ROPE + o:TOK_COLS - ROPE + o + HALF] for o in (0, HALF))
                    G.wait(pool, "cst_ld", 16, 16)
                    tab = cst[0:rows, 0:nt, :]
                    cos, sin = tab[:, :, 0:HALF], tab[:, :, HALF:]
                    for q, (xx, t) in enumerate(((x1, cos), (x2, sin), (x1, sin), (x2, cos))):
                        step(pool.tensor_tensor(rope4[0:rows, q, 0:nt, :], xx, t, ALU.mult))
                    for o in (NOPE, NOPE + ROPE):
                        pool.tensor_tensor(krd[0:rows, 0:nt, o:o + HALF], rope4[0:rows, 0, 0:nt, :], rope4[0:rows, 1, 0:nt, :], ALU.subtract)
                        last = pool.tensor_tensor(krd[0:rows, 0:nt, o + HALF:o + ROPE], rope4[0:rows, 2, 0:nt, :], rope4[0:rows, 3, 0:nt, :], ALU.add)
                    last.then_inc(s["kr"], 1)
                    for c in range(CC):
                        G.wait(pool, "sig", CC, c + 1)
                        G.wait(pool, "aval", CC, c + 1)
                        v = aS[:, c, :, CONV_HIST:] if G.smp else aT[:, c, CONV_HIST:]
                        pool.tensor_tensor(v, v, G.bl(sg[:, 0:n]), ALU.mult).then_inc(s["glu"], 1)
                        if before and c == 0:
                            inv_std(before)
                    if not G.smp:
                        second_parts(it + 1)
                        G.wait(pool, "xtok_free", TILES, 2 * TILES)
                        G.wait(pool, "rx_free", 1, 1)
                        rms_x(it + 2)
                    assert done[0] == 6

                over_groups(pool, group, tail)

            @block.scalar
            def _(act):
                def load_xtok(row):
                    act.dma_start(xtok[:, :], a["x"][bass.ds(row, P), :]).then_inc(s["xtok_ld"], 16)

                def square_x(g, j):
                    act.wait_ge(s["xtok_ld"], g * (16 * TILES) + 16 * (j + 1))
                    act.activation(xtok[:, :], xtok[:, :], ACT.Square, scale=D_MODEL ** -0.5, accum_out=ssx[:, j:j + 1]).then_inc(s["xtok_free"], 1)
                    act.wait_ge(s["xtok_free"], g * TILES + j + 1)
                    if j + 1 < TILES:
                        load_xtok(g * GROUP + (j + 1) * P)

                def first_part(g, k):
                    act.wait_ge(xt_ld[k % 4], g * (4 * KC) + 16 * (k // 4 + 1))
                    act.activation(hT[:, 0, k, :], xbuf(k), ACT.Copy).then_inc(s["x_hi"], 1)

                def weight(n):
                    raw, landed, count = staging(n)
                    act.wait_ge(landed, count)
                    act.activation(parts[n][1], raw, ACT.Copy, scale=parts[n][3]).then_inc(w_hi, 1)

                load_xtok(0)
                act.wait_ge(load, 32)
                for k in range(KC):
                    weight(k)
                    first_part(0, k)
                    if k % 2:
                        square_x(0, k // 2)
                for n in range(KC, W_ALL):
                    weight(n)
                act.wait_ge(w_lo, W_ALL)
                act.wait_ge(s["const"], 96)

                def stage_out(G, u, banks, job, rows_=P, cols_=None, **scale):
                    bank = banks.wait_done(act, G.it, job)
                    G.wait(act, k_out[u % 2], 16 * KST // 2, 16 * (u // 2 + 1))
                    w = cols_ or G.n
                    act.activation(kst[0:rows_, u % 2, 0:w], bank[0:rows_, 0:w], ACT.Copy, **scale).then_inc(s["kst"], 1)
                    G.wait(act, "kst", KST, u + 1)
                    act.sem_inc(banks.free[job % banks.n], 1)

                def value_out(G, job, j):
                    bank = mm.wait_done(act, G.it, job)
                    G.wait(act, q_out[j % 2], 16 * QST // 2, 16 * ((HEADS + j) // 2 + 1))
                    act.activation(qst[0:G.rows, j % 2, :], bank[0:G.rows, :], ACT.Copy).then_inc(s["vst"], 1)
                    G.wait(act, "vst", TILES, j + 1)
                    act.sem_inc(mm.free[job % mm.n], 1)

                def pooled(G):
                    for c in range(CC):
                        stage_out(G, 4 + c, cv, PL + c, scale=pool_s[:, c:c + 1])

                def conv_end(G):
                    n = G.n
                    cv.wait_done(act, G.it, YB + 1)
                    for c in range(CC):
                        bank = cv.wait_done(act, G.it, YB + c)
                        act.activation(ya[:, c, 0:n], bank[:, 0:n], ACT.Silu, scale=ln_g[:, c:c + 1], bias=ln_b[:, c:c + 1]).then_inc(s["act"], 1)
                        G.wait(act, "act", CC, c + 1)
                        act.sem_inc(cv.free[(YB + c) % cv.n], 1)
                    for c in range(CC):
                        stage_out(G, 6 + c, cv, CV + c)

                def group(G, before):
                    it, n, nt, rows = G.it, G.n, G.tiles, G.rows
                    if not G.smp:
                        load_xtok(it * GROUP + GROUP)
                    G.wait(act, "zt_free", 1, 1)
                    G.wait(act, "ckv_out", 16, 16)
                    G.wait(act, "rx", 1, 1)
                    for j in range(nt):
                        bank = mm.wait_done(act, it, TOK0 + j)
                        act.activation(zt[0:rows, j, :], bank[0:rows, 0:TOK_COLS], ACT.Copy, scale=rx[0:rows, j:j + 1]).then_inc(s["z"], 1)
                        G.wait(act, "z", TILES, j + 1)
                        act.sem_inc(mm.free[(TOK0 + j) % mm.n], 1)
                        act.activation(junk[0:rows, 0:Q_RANK], zt[0:rows, j, 0:Q_RANK], ACT.Square,
                                       accum_out=ssq[0:rows, j:j + 1]).then_inc(s["ssq"], 1)
                        G.wait(act, "ssq", 2 * TILES, 2 * j + 1)
                        act.activation(junk[0:rows, 0:KV_RANK], zt[0:rows, j, Q_RANK:Q_RANK + KV_RANK], ACT.Square,
                                       accum_out=ssq[0:rows, TILES + j:TILES + j + 1]).then_inc(s["ssq"], 1)
                        G.wait(act, "ssq", 2 * TILES, 2 * j + 2)
                    bank = tr.wait_done(act, it, T_R)
                    act.activation(rb[:, 0:n], bank[:, 0:n], ACT.Copy).then_inc(s["rb"], 1)
                    G.wait(act, "rb", 1, 1)
                    act.sem_inc(tr.free[T_R], 1)
                    act.activation(rstd_all[0:rows, bass.ds(GROUPS * TILES if G.smp else it * TILES, nt)], rx[0:rows, 0:nt], ACT.Copy)
                    act.sem_inc(s["rx_free"], 1)
                    for c in range(CC):
                        G.wait(act, "sgate", CC, c + 1)
                        act.activation(sg[:, 0:n], sg[:, 0:n], ACT.Sigmoid).then_inc(s["sig"], 1)
                        if before and c == 0:
                            pooled(before)
                    if before:
                        conv_end(before)
                    for q in range(3):
                        bank = tr.wait_done(act, it, T_CQ + q)
                        dst = cq[:, 0, q, 0:n] if q < QC else ckv[:, 0, 0:n]
                        act.activation(dst, bank[:, 0:n], ACT.Copy).then_inc(s["hi"], 1)
                    bank = tr.wait_done(act, it, T_KR)
                    G.wait(act, "krt_out", 16, 16)
                    G.wait(act, "glu", CC, CC)
                    act.activation(krt[NOPE:P, 0:n], bank[NOPE:P, 0:n], ACT.Copy).then_inc(s["krt"], 1)
                    G.wait(act, "krt", 1, 1)
                    act.sem_inc(tr.free[T_KR % tr.n], 1)
                    if not G.smp:
                        G.wait(act, "hT_free", 1, 1)
                        G.wait(act, "rx", 1, 1)
                        for k in range(6):
                            first_part(it + 1, k)
                            if k in (3, 5):
                                square_x(it + 1, k // 4)
                    for u in range(8):
                        kind, m = KV[u]
                        if kind == "k":
                            stage_out(G, m, mm, KV0 + u)
                        else:
                            value_out(G, KV0 + u, m)
                        if not G.smp and u < 2:
                            first_part(it + 1, 6 + u)
                        if not G.smp and u in (4, 7):
                            square_x(it + 1, 1 + u // 4 + u // 7)

                def tail(G):
                    pooled(G)
                    conv_end(G)

                over_groups(act, group, tail)

            @block.vector
            def _(dve):
                dve.wait_ge(load, 32)
                for n, (_, hi, lo, g) in enumerate(parts):
                    dve.wait_ge(w_hi, n + 1)
                    dve.scalar_tensor_tensor(lo, staging(n)[0], g, f32(hi), ALU.mult, ALU.subtract).then_inc(w_lo, 1)
                dve.wait_ge(w_lo, W_ALL)
                dve.wait_ge(s["prep"], 10)
                dve.wait_ge(s["const"], 96)

                def stats(G):
                    rows = G.rows
                    for q in range(2):
                        cv.wait_done(dve, G.it, YF + q)
                    for j in range(G.tiles):
                        v = cv.t[(YF + j // 2) % cv.n][0:rows, (j % 2) * CONV_W:(j % 2 + 1) * CONV_W]
                        dve.bn_stats(st6[0:rows, j, :], v).then_inc(s["yn"], 1)
                    for j in range(G.tiles):
                        G.wait(dve, "yn", 2 * TILES, j + 1)
                        dve.sem_inc(s["stats"], 1)
                        dve.bn_aggr(mv[0:rows, j, :], st6[0:rows, j, :]).then_inc(s["mv"], 1)

                def normalise(G):
                    rows = G.rows
                    G.wait(dve, "ry", 1, 1)
                    for j in range(G.tiles):
                        v = cv.t[(YF + j // 2) % cv.n][0:rows, (j % 2) * CONV_W:(j % 2 + 1) * CONV_W]
                        dve.tensor_scalar(yn[0:rows, j, :], v, mv[0:rows, j, 0:1], ry[0:rows, j:j + 1], ALU.subtract, ALU.mult).then_inc(s["yn"], 1)
                    G.wait(dve, "yn", 2 * TILES, 2 * G.tiles)
                    for q in range(2):
                        dve.sem_inc(cv.free[(YF + q) % cv.n], 1)

                def taps(G, first, stop):
                    for m in range(first, stop):
                        c, k = divmod(m, CONV_K)
                        if k == 0:
                            G.wait(dve, "glu", CC, c + 1)
                        src = aS[:, c, :, k:k + DEC_SEQ] if G.smp else aT[:, c, k:k + GROUP]
                        out = G.bl(y[:, c, 0:G.n])
                        if k == 0:
                            dve.tensor_scalar(out, src, dw[:, c, 0:1], conv_b[:, c:c + 1], ALU.mult, ALU.add).then_inc(s["conv"], 1)
                        else:
                            G.wait(dve, "conv", CONV_OPS, m)
                            dve.scalar_tensor_tensor(out, src, dw[:, c, k:k + 1], out, ALU.mult, ALU.add).then_inc(s["conv"], 1)

                def tail(G):
                    taps(G, TAPS_OWN, CONV_OPS)
                    stats(G)
                    normalise(G)

                def group(G, before):
                    it, n, nt, rows = G.it, G.n, G.tiles, G.rows
                    if before:
                        taps(before, TAPS_OWN, CONV_OPS)
                        before.wait(dve, "conv", CONV_OPS, CONV_OPS)
                        dve.tensor_copy(aT[:, :, 0:CONV_HIST], aT[:, :, GROUP:]).then_inc(s["a_free"], 1)
                    ran = [0]

                    def run(count):
                        taps(G, ran[0], min(ran[0] + count, TAPS_OWN))
                        ran[0] = min(ran[0] + count, TAPS_OWN)

                    G.wait(dve, "rq", 1, 1)
                    for j in range(nt):
                        G.wait(dve, "z", TILES, j + 1)
                        lat = zt[0:rows, j, 0:Q_RANK]
                        dve.tensor_scalar(lat, lat, rq[0:rows, j:j + 1], None, ALU.mult).then_inc(s["nrm"], 1)
                        lat = zt[0:rows, j, Q_RANK:Q_RANK + KV_RANK]
                        dve.scalar_tensor_tensor(lat, lat, rq[0:rows, TILES + j:TILES + j + 1], g_kv[0:rows, :], ALU.mult, ALU.mult).then_inc(s["nrm"], 1)
                    G.wait(dve, "rb", 1, 1)
                    G.wait(dve, "a_free", 1, 1)
                    G.wait(dve, "krt_out", 16, 16)
                    for c in range(CC):
                        bank = mm.wait_done(dve, it, T0 + 2 * c)
                        if c:
                            G.wait(dve, "glu", CC, 1)
                        dve.tensor_tensor(sg[:, 0:n], bank[:, 0:n], rb[:, 0:n], ALU.mult).then_inc(s["sgate"], 1)
                        G.wait(dve, "sgate", CC, c + 1)
                        dve.sem_inc(mm.free[(T0 + 2 * c) % mm.n], 1)
                        if before and c:
                            normalise(before)
                        run(4 * c)
                        bank = mm.wait_done(dve, it, T0 + 2 * c + 1)
                        dst = aS[:, c, :, CONV_HIST:] if G.smp else aT[:, c, CONV_HIST:]
                        dve.tensor_tensor(dst, G.bl(bank[:, 0:n]), G.bl(rb[:, 0:n]), ALU.mult).then_inc(s["aval"], 1)
                        G.wait(dve, "aval", CC, c + 1)
                        dve.sem_inc(mm.free[(T0 + 2 * c + 1) % mm.n], 1)
                        if before and c == 0:
                            stats(before)
                        run(4)
                    G.wait(dve, "u_free", 1, 1)
                    for c in range(CC):
                        bank = mm.wait_done(dve, it, T0 + 4 + c)
                        dst = uS[:, c, :, UH:] if G.smp else uT[:, c, UH:]
                        dve.tensor_tensor(dst, G.bl(bank[:, 0:n]), G.bl(rb[:, 0:n]), ALU.mult).then_inc(s["upool"], 1)
                        G.wait(dve, "upool", CC, c + 1)
                        dve.sem_inc(mm.free[(T0 + 4 + c) % mm.n], 1)
                        run(6 if c == 0 else 0)
                    for q in range(3):
                        G.wait(dve, "hi", 3, q + 1)
                        bank = tr.t[(T_CQ + q) % tr.n]
                        hi, lo = (cq[:, i, q, 0:n] if q < QC else ckv[:, i, 0:n] for i in range(2))
                        dve.tensor_tensor(lo, bank[:, 0:n], f32(hi), ALU.subtract).then_inc(s["pair"], 1)
                        G.wait(dve, "pair", 3, q + 1)
                        dve.sem_inc(tr.free[(T_CQ + q) % tr.n], 1)
                    G.wait(dve, "cs_ld", 16, 16)
                    for h in range(HEADS):
                        run(1)
                        bank = mm.wait_done(dve, it, Q0 + h)
                        G.wait(dve, q_out[h % 2], 16 * QST // 2, 16 * (h // 2 + 1))
                        dve.tensor_tensor(qst[:, h % 2, 0:n], bank[:, 0:n], cs[:, 0:n], ALU.mult).then_inc(s["qst"], 1)
                        G.wait(dve, "qst", HEADS, h + 1)
                        dve.sem_inc(mm.free[(Q0 + h) % mm.n], 1)
                    dve.sem_inc(s["cs_free"], 1)
                    run(TAPS_OWN)

                over_groups(dve, group, tail)

            @block.tensor
            def _(pe):
                pe.wait_ge(load, 32)

                def product(out, pairs):
                    for i, (w, x) in enumerate(pairs):
                        for q, (pw_, px) in enumerate(PASSES):
                            last = pe.matmul(out, w(pw_), x(px), start=(i == 0 and q == 0), stop=(i == len(pairs) - 1 and q == 2))
                    return last

                def pooled(G):
                    n = G.n
                    G.wait(pe, "d", CC, CC)
                    for c in range(CC):
                        bank = cv.wait_free(pe, G.it, PL + c)
                        if G.smp:
                            L = UH + DEC_SEQ
                            d = sA[:, :, :].rearrange("p c n -> p (c n)")[:, 0:CC * DEC_BATCH * L].rearrange("p (c b n) -> p c b n", c=CC, b=DEC_BATCH)[:, c, :, UH:]
                            out = bank[:, 0:n].rearrange("p (b l) -> p b l", l=DEC_SEQ)
                        else:
                            d, out = sA[:, c, UH:], bank[:, 0:n]
                        pe.matmul(out, plw[:, c, :], d, start=True, stop=True).then_inc(cv.done[(PL + c) % cv.n], 1)

                def to_tokens(G):
                    nt, rows = G.tiles, G.rows
                    G.wait(pe, "conv", CONV_OPS, CONV_OPS)
                    for q in range(2):
                        bank = cv.wait_free(pe, G.it, YF + q)
                        for j in (2 * q, 2 * q + 1):
                            for c in range(CC if j < nt else 0):
                                last = pe.transpose(bank[0:rows, (j % 2) * CONV_W + c * P:(j % 2) * CONV_W + (c + 1) * P],
                                                    y[:, c, j * P:j * P + rows], ident[:, :])
                        if 2 * q < nt:
                            last.then_inc(cv.done[(YF + q) % cv.n], 1)
                        else:
                            pe.sem_inc(cv.done[(YF + q) % cv.n], 1)

                def to_channels(G):
                    nt, rows = G.tiles, G.rows
                    G.wait(pe, "yn", 2 * TILES, 2 * nt)
                    for c in range(CC):
                        bank = cv.wait_free(pe, G.it, YB + c)
                        for j in range(nt):
                            last = pe.transpose(bank[:, j * P:j * P + rows], yn[0:rows, j, c * P:(c + 1) * P], ident[0:rows, 0:rows])
                        last.then_inc(cv.done[(YB + c) % cv.n], 1)

                def pointwise(G):
                    n = G.n
                    G.wait(pe, "act", CC, CC)
                    for c in range(CC):
                        bank = cv.wait_free(pe, G.it, CV + c)
                        for k in range(CC):
                            last = pe.matmul(bank[:, 0:n], pw[:, k, c * P:(c + 1) * P], ya[:, k, 0:n], start=(k == 0), stop=(k == CC - 1))
                        last.then_inc(cv.done[(CV + c) % cv.n], 1)

                def tail(G):
                    pooled(G)
                    to_tokens(G)
                    to_channels(G)
                    pointwise(G)

                def group(G, before):
                    it, n, nt, rows = G.it, G.n, G.tiles, G.rows
                    for j in range(nt):
                        bank = mm.wait_free(pe, it, TOK0 + j)
                        t0 = j * P
                        for k in range(KC):
                            if j == 0:
                                G.wait(pe, "split", KC, k + 1)
                                if not before:
                                    pe.wait_ge(w_lo, W_TOK + k + 1)
                            for q, (pw_, px) in enumerate(PASSES):
                                last = pe.matmul(bank[0:rows, 0:TOK_COLS], hT[:, pw_, k, t0:t0 + rows], w_in[:, px, k, 0:TOK_COLS],
                                                 start=(k == 0 and q == 0), stop=(k == KC - 1 and q == 2))
                        last.then_inc(mm.done[(TOK0 + j) % mm.n], 1)
                    for j in range(nt, TILES):
                        mm.wait_free(pe, it, TOK0 + j)
                        pe.sem_inc(mm.done[(TOK0 + j) % mm.n], 1)
                        pe.sem_inc(mm.free[(TOK0 + j) % mm.n], 1)
                    G.wait(pe, "rx", 1, 1)
                    bank = tr.wait_free(pe, it, T_R)
                    for j in range(nt):
                        last = pe.transpose(bank[:, j * P:j * P + rows], rx[0:rows, j:j + 1].broadcast_to([rows, P]), ident[0:rows, 0:rows])
                    last.then_inc(tr.done[T_R], 1)
                    for b in range(6):
                        bank = mm.wait_free(pe, it, T0 + b)
                        for k in range(KC):
                            if b == 0 and not before:
                                pe.wait_ge(w_lo, W_T + k + 1)
                            c0 = TOK_COLS + b * P
                            for q, (pw_, px) in enumerate(PASSES):
                                last = pe.matmul(bank[:, 0:n], w_in[:, pw_, k, c0:c0 + P], hT[:, px, k, 0:n],
                                                 start=(k == 0 and q == 0), stop=(k == KC - 1 and q == 2))
                        last.then_inc(mm.done[(T0 + b) % mm.n], 1)
                        if before and b == 0:
                            pooled(before)
                        if before and b == 1:
                            to_tokens(before)
                        if before and b == 3:
                            to_channels(before)
                        if before and b == 4:
                            pointwise(before)
                    if not before:
                        pe.wait_ge(w_lo, W_ALL)
                        pe.wait_ge(s["const"], 96)
                    pe.wait_ge(mm.done[(T0 + 5) % mm.n], mm.count(it, T0 + 5))
                    pe.sem_inc(s["hT_free"], 1)
                    G.wait(pe, "nrm", 2 * TILES, 2 * nt)
                    for q in range(4):
                        if q == 3:
                            G.wait(pe, "kr", 1, 2)
                        bank = tr.wait_free(pe, it, T_CQ + q)
                        for j in range(nt):
                            src = zt[0:rows, j, q * P:(q + 1) * P] if q < 3 else krd[0:rows, j, :]
                            last = pe.transpose(bank[:, j * P:j * P + rows], src, ident[0:rows, 0:rows])
                        last.then_inc(tr.done[(T_CQ + q) % tr.n], 1)
                    pe.wait_ge(tr.done[T_KR % tr.n], tr.count(it, T_KR))
                    pe.sem_inc(s["zt_free"], 1)
                    pe.sem_inc(s["krd_free"], 1)
                    G.wait(pe, "pair", 3, 2)
                    for h in range(HEADS):
                        bank = mm.wait_free(pe, it, Q0 + h)
                        product(bank[:, 0:n], [(lambda i, k=k: w_uq[:, i, k, h * P:(h + 1) * P], lambda i, k=k: cq[:, i, k, 0:n])
                                               for k in range(QC)]).then_inc(mm.done[(Q0 + h) % mm.n], 1)
                    G.wait(pe, "pair", 3, 3)
                    for u, (kind, m) in enumerate(KV):
                        bank = mm.wait_free(pe, it, KV0 + u)
                        if kind == "k":
                            last = product(bank[:, 0:n], [(lambda i: w_uk[:, i, m * P:(m + 1) * P], lambda i: ckv[:, i, 0:n])])
                        else:
                            t0 = 0 if G.smp else m * P
                            last = product(bank[0:rows, :], [(lambda i: ckv[:, i, t0:t0 + rows], lambda i: w_uv[:, i, :])])
                        last.then_inc(mm.done[(KV0 + u) % mm.n], 1)
                    for banks, job in ((tr, T_SPARE), (mm, SPARE0), (mm, SPARE0 + 1)):
                        banks.wait_free(pe, it, job)
                        pe.sem_inc(banks.done[job % banks.n], 1)
                        pe.sem_inc(banks.free[job % banks.n], 1)

                over_groups(pe, group, tail)


def stage2(nc, a, keep):
    ctx = ExitStack()
    with ctx:
        def sb(name, shape, dt=F32):
            return ctx.enter_context(nc.sbuf_tensor(name, shape, dt))

        def sem(name):
            return ctx.enter_context(nc.semaphore("s2_" + name))

        ident, rden = keep["ident"], keep["rden"]
        NT = SEQ // P
        qraw, kraw, vraw = sb("qraw", [P, SEQ]), sb("kraw", [P, SEQ]), sb("vraw", [P, NT, VDIM])
        q2, k2 = sb("q2", [P, 2, 2, SEQ], F32R), sb("k2", [P, 2, 2, SEQ], F32R)
        v2 = sb("v2", [P, 2, NT, 2 * VDIM], F32R)
        prob = sb("prob", [P, 2, SEQ])
        pT = sb("pT", [P, 2, NT, GROUP], F32R)
        mx, nm = sb("mx", [P, 4, 4]), sb("nm", [P, 4])
        dsum = sb("dsum", [P, 2, NT, 4])
        den = sb("den", [P, 2, NT])
        zero = sb("zero2", [P, 1])
        olo, ost = sb("olo", [VDIM, GROUP]), sb("ost", [VDIM, 2, GROUP])
        ident_b, mask_b, mask_f = sb("ident_b", [P, P], BF16), sb("mask_b", [P, P], BF16), sb("mask_f", [P, P])
        head_jobs = [(t, c, min(GROUP, (t + 1) * P - c * GROUP), c == t // 4) for t in range(NT) for c in range(t // 4 + 1)]
        JH = len(head_jobs)
        jobs = [(hf, *j) for hf in range(2) for j in head_jobs]
        J = len(jobs)
        sc = Banks(sem, "sc", [ctx.enter_context(nc.psum_tensor(f"sc{i}", [P, GROUP], F32)) for i in range(5)], J)
        tr = Banks(sem, "tr", [ctx.enter_context(nc.psum_tensor(f"tp{i}", [P, GROUP], F32)) for i in range(2)], J)
        pv = ctx.enter_context(nc.psum_tensor("pv", [P, GROUP], F32))
        s = {n: sem(n) for n in ("const", "raw", "split", "head_done", "mx", "nm", "pT_hi", "pv_done", "pv_free", "olo", "ost",
                                 "den", "init", "masks", "table", "gather", "first_hi", "first_lo")}
        assert HEADS == DEC_BATCH
        n_phys = a["cache_ckv"].shape[0]
        table = sb("table", [1, DEC_BATCH * N_PAGES], I32)
        o_out = [sem(f"o_out{i}") for i in range(2)]
        SP_N = 6
        ends = {n: (hf, t // 4) for n, (hf, t, c, w, last) in enumerate(jobs) if last and t % 4 == 3}
        tile_no = [hf * NT + t for hf, t, *_ in jobs]
        slice_at = {}
        for n, (_, g) in ends.items():
            for c in range(g + 1):
                slice_at.setdefault(n - g + c + 1, []).append((n, c))
        SLICES = 1 + 2 + 3 + 4

        def slices(i, n, c):
            hf, g = ends[n]
            return (i * 2 + hf) * SLICES + g * (g + 1) // 2 + c + 1

        LEAD = 4

        first = [(lambda i: q2[:, 0, i, :], qraw[:, :]), (lambda i: k2[0:NOPE, 0, i, :], kraw[0:NOPE, :]),
                 (lambda i: v2[:, 0, :, i * VDIM:(i + 1) * VDIM], vraw[:, :, :])]
        first = [(lambda i, b=b: k2[NOPE:P, b, i, :], kraw[NOPE:P, :]) for b in range(2)] + first

        with nc.Block() as block:
            @block.sync
            def _(sp):
                sp.dma_start(mask_f[:, :], a["causal"]).then_inc(s["const"], 16)
                sp.dma_start(kraw[NOPE:P, :], a["KRT"][:, 0:SEQ]).then_inc(s["const"], 16)


                def gather(b, pages):
                    for pg in pages:
                        page = sp.value_load(table[0:1, bass.ds(b * N_PAGES + pg, 1)], min_val=0, max_val=n_phys - 1)
                        sp.dma_start(a["LAT"][bass.ds(b, 1), pg, :, :].rearrange("o p n -> (o p) n"),
                                     a["cache_ckv"][bass.ds(page, 1), :, :].rearrange("o p n -> (o p) n")).then_inc(s["gather"], 16)
                        sp.dma_start(a["KR"][bass.ds(b, 1), pg, :, :].rearrange("o p n -> (o p) n"),
                                     a["cache_krope"][bass.ds(page, 1), :, :].rearrange("o p n -> (o p) n")).then_inc(s["gather"], 16)

                def load(h):
                    sp.dma_start(qraw[:, :], a["QT"][bass.ds(h * P, P), 0:SEQ]).then_inc(s["raw"], 16)
                    sp.dma_start(kraw[0:NOPE, :], a["KT"][bass.ds(h * NOPE, NOPE), 0:SEQ]).then_inc(s["raw"], 16)
                    sp.dma_start(vraw[:, :, :], a["V"][0:SEQ, bass.ds(h * VDIM, VDIM)].rearrange("(k p) d -> p k d", p=P)).then_inc(s["raw"], 16)

                load(0)
                sp.dma_start(table[:, :], a["page_table"]).then_inc(s["table"], 16)
                sp.wait_ge(s["table"], 16)
                sp.wait_ge(s["first_lo"], 5)
                load(1)
                with sp.Fori(0, HEADS // 2) as i:
                    for hf in range(2):
                        sp.wait_ge(s["split"], i * 2 * SP_N + (2 + hf) * SP_N)
                        load((i * 2 + 2 + hf) % HEADS)
                        for g in range(4):
                            gather(i * 2 + hf, range(g * N_PAGES // 4, (g + 1) * N_PAGES // 4))
                            sp.wait_ge(s["ost"], i * 8 + hf * 4 + g + 1)
                            sp.dma_start(a["Y"][bass.ds((i * 2 + hf) * VDIM, VDIM), g * GROUP:(g + 1) * GROUP],
                                         ost[:, g % 2, :]).then_inc(o_out[g % 2], 16)
                sp.wait_ge(s["raw"], 48 * (HEADS + 2))
                sp.wait_ge(s["gather"], 32 * DEC_BATCH * N_PAGES)
                for b in range(2):
                    sp.wait_ge(o_out[b], 16 * (2 * HEADS + 1))

            @block.gpsimd
            def _(pool):
                for b in (*sc.free, *tr.free):
                    pool.sem_inc(b, 1)
                for b in o_out:
                    pool.sem_inc(b, 16)
                pool.sem_inc(s["head_done"], 1)
                pool.sem_inc(s["pv_free"], 1)
                pool.memset(zero[:, :], 0.0).then_inc(s["init"], 1)
                pool.wait_ge(s["init"], 1)

                def copy(dst, src):
                    return pool.tensor_tensor(dst, src, spread(zero[0:dst.shape[0], :], dst), ALU.add)

                def split(b, before):
                    for q, (dst, src) in enumerate(((lambda i: q2[:, b, i, :], qraw[:, :]), (lambda i: k2[0:NOPE, b, i, :], kraw[0:NOPE, :]),
                                                    (lambda i: v2[:, b, :, i * VDIM:(i + 1) * VDIM], vraw[:, :, :]))):
                        copy(dst(0), src).then_inc(s["split"], 1)
                        pool.wait_ge(s["split"], before + 2 * q + 1)
                        pool.tensor_tensor(dst(1), src, f32(dst(0)), ALU.subtract).then_inc(s["split"], 1)
                    pool.wait_ge(s["split"], before + SP_N)

                pool.wait_ge(s["first_lo"], 5)
                pool.sem_inc(s["split"], SP_N)
                with pool.Fori(0, HEADS // 2) as i:
                    for hf in range(2):
                        pool.wait_ge(s["raw"], i * 96 + (2 + hf) * 48)
                        pool.wait_ge(s["head_done"], i * 2 + 1 + hf)
                        split(1 - hf, i * 2 * SP_N + (1 + hf) * SP_N)

            @block.tensor
            def _(pe):
                pe.wait_ge(s["first_lo"], 5)
                pe.wait_ge(s["masks"], 2)

                def scores(i, n):
                    hf, t, c, w, last = jobs[n]
                    if n % JH == 0:
                        pe.wait_ge(s["split"], i * 2 * SP_N + (1 + hf) * SP_N)
                    bank = sc.wait_free(pe, i, n)
                    for q, (pw_, px) in enumerate(PASSES):
                        ins = pe.matmul(bank[:, 0:w], q2[:, hf, pw_, t * P:(t + 1) * P], k2[:, hf, px, c * GROUP:c * GROUP + w],
                                        start=(q == 0), stop=(q == 2 and not last))
                    if last:
                        ins = pe.matmul(bank[:, w - P:w], ident_b[:, :], mask_b[:, :], start=False, stop=True)
                    ins.then_inc(sc.done[n % sc.n], 1)

                def transposes(i, n):
                    hf, t, c, w, last = jobs[n]
                    pe.wait_ge(sc.free[n % sc.n], sc.count(i, n) + 1)
                    bank = tr.wait_free(pe, i, n)
                    for k in range(w // P):
                        ins = pe.transpose(bank[:, k * P:(k + 1) * P], prob[:, t % 2, c * GROUP + k * P:c * GROUP + (k + 1) * P], ident[:, :])
                    ins.then_inc(tr.done[n % tr.n], 1)

                def values(i, n, c):
                    hf, g = ends[n]
                    m = n - g + c
                    pe.wait_ge(tr.free[m % tr.n], tr.count(i, m) + 1)
                    if c == 0:
                        pe.wait_ge(s["pv_free"], i * 8 + hf * 4 + g + 1)
                    for k in range(4 * c, 4 * c + 4):
                        c0 = max(0, k - 4 * g) * P
                        for part in range(2):
                            ins = pe.matmul(pv[:, c0:], v2[:, hf, k, :], pT[:, part, k, c0:], start=(k == 0 and part == 0),
                                            stop=(k == 4 * g + 3 and part == 1))
                    ins.then_inc(s["pv_done"], 1)
                    if g == 3 and c == 3:
                        pe.wait_ge(s["pv_done"], (i * 2 + hf + 1) * SLICES)
                        pe.sem_inc(s["head_done"], 1)

                with pe.Fori(0, HEADS // 2) as i:
                    for n in range(LEAD):
                        scores(i, n)
                    for n in range(J):
                        if n + LEAD < J:
                            scores(i, n + LEAD)
                        transposes(i, n)
                        for e, c in slice_at.get(n, ()):
                            values(i, e, c)
                    for e, c in slice_at[J]:
                        values(i, e, c)

            @block.scalar
            def _(act):
                act.wait_ge(s["const"], 32)
                act.activation(ident_b[:, :], ident[:, :], ACT.Copy).then_inc(s["masks"], 1)
                act.activation(mask_b[:, :], mask_f[:, :], ACT.Copy).then_inc(s["masks"], 1)

                def exps(i, n):
                    hf, t, c, w, last = jobs[n]
                    bank = sc.t[n % sc.n]
                    act.wait_ge(s["nm"], i * 2 * NT + tile_no[n] + 1)
                    act.activation(prob[:, t % 2, c * GROUP:c * GROUP + w], bank[:, 0:w], ACT.Exp, bias=nm[:, t % 4:t % 4 + 1],
                                   accum_out=dsum[:, hf, t, c:c + 1]).then_inc(sc.free[n % sc.n], 1)

                def hi(i, n):
                    hf, t, c, w, last = jobs[n]
                    bank = tr.wait_done(act, i, n)
                    if t % 4 == 0:
                        before = [e for e in ends if e < n]
                        if before and c <= ends[before[-1]][1]:
                            act.wait_ge(s["pv_done"], slices(i, before[-1], c))
                    act.activation(pT[:, 0, 4 * c:4 * c + w // P, (t % 4) * P:(t % 4 + 1) * P],
                                   bank[:, 0:w].rearrange("p (k q) -> p k q", q=P), ACT.Copy).then_inc(s["pT_hi"], 1)

                def values(i, n):
                    hf, g = ends[n]
                    act.wait_ge(s["pv_done"], slices(i, n, g))
                    act.activation(olo[:, :], pv[VDIM:P, :], ACT.Copy).then_inc(s["olo"], 1)

                for n, (dst, src) in enumerate(first):
                    if n == 2:
                        act.wait_ge(s["raw"], 48)
                    act.activation(dst(0), src, ACT.Copy).then_inc(s["first_hi"], 1)

                with act.Fori(0, HEADS // 2) as i:
                    exps(i, 0)
                    for n in range(J):
                        new_tile = n + 1 < J and jobs[n + 1][2] == 0
                        if n + 1 < J and not new_tile:
                            exps(i, n + 1)
                        hi(i, n)
                        if new_tile:
                            exps(i, n + 1)
                        if n - 1 in ends:
                            values(i, n - 1)
                    values(i, J - 1)

            @block.vector
            def _(dve):
                dve.memset(dsum[:, :, :, :], 0.0).then_inc(s["den"], 1)
                dve.memset(rden[:, :, NT:NT + 1], 1.0)
                dve.wait_ge(s["den"], 1)
                for n, (dst, src) in enumerate(first):
                    dve.wait_ge(s["first_hi"], n + 1)
                    dve.tensor_tensor(dst(1), src, f32(dst(0)), ALU.subtract).then_inc(s["first_lo"], 1)
                DN = 2 * 2

                def maxima(i, n):
                    hf, t, c, w, last = jobs[n]
                    bank = sc.wait_done(dve, i, n)
                    if last and c == 0:
                        dve.reduce_max(nm[:, t % 4:t % 4 + 1], bank[:, 0:w], AXX, negate=True).then_inc(s["nm"], 1)
                        return
                    dve.reduce_max(mx[:, t % 4, c:c + 1], bank[:, 0:w], AXX).then_inc(s["mx"], 1)
                    if last:
                        dve.wait_ge(s["mx"], i * MXN + mxc[n])
                        dve.reduce_max(nm[:, t % 4:t % 4 + 1], mx[:, t % 4, 0:c + 1], AXX, negate=True).then_inc(s["nm"], 1)

                mxc, count = [], 0
                for hf, t, c, w, last in jobs:
                    count += t >= 4
                    mxc.append(count)
                MXN = count

                def lo(i, n):
                    hf, t, c, w, last = jobs[n]
                    bank = tr.t[n % tr.n]
                    dve.wait_ge(s["pT_hi"], i * J + n + 1)
                    cut = lambda part: pT[:, part, 4 * c:4 * c + w // P, (t % 4) * P:(t % 4 + 1) * P]
                    dve.tensor_tensor(cut(1), bank[:, 0:w].rearrange("p (k q) -> p k q", q=P), f32(cut(0)), ALU.subtract)\
                       .then_inc(tr.free[n % tr.n], 1)

                def values(i, n):
                    hf, g = ends[n]
                    dve.wait_ge(s["olo"], i * 8 + hf * 4 + g + 1)
                    dve.wait_ge(o_out[g % 2], i * 64 + hf * 32 + (g // 2) * 16 + 16)
                    dve.tensor_tensor(ost[:, g % 2, :], pv[0:VDIM, :], olo[:, :], ALU.add).then_inc(s["ost"], 1)
                    dve.wait_ge(s["ost"], i * 8 + hf * 4 + g + 1)
                    dve.sem_inc(s["pv_free"], 1)
                    if g == 3:
                        dve.reduce_sum(den[:, hf, :], dsum[:, hf, :, :], AXX).then_inc(s["den"], 1)
                        dve.wait_ge(s["den"], i * DN + 2 + 2 * hf)
                        dve.reciprocal(rden[:, bass.ds(i * 2 + hf, 1), 0:NT].rearrange("p o t -> p (o t)"), den[:, hf, :]).then_inc(s["den"], 1)

                with dve.Fori(0, HEADS // 2) as i:
                    for n in range(LEAD):
                        maxima(i, n)
                    for n in range(J):
                        if n + LEAD < J:
                            maxima(i, n + LEAD)
                        lo(i, n)
                        if n - 1 in ends:
                            values(i, n - 1)
                    values(i, J - 1)


def stage3(nc, a, keep):
    ctx = ExitStack()
    with ctx:
        def sb(name, shape, dt=F32):
            return ctx.enter_context(nc.sbuf_tensor(name, shape, dt))

        def ps(name):
            return ctx.enter_context(nc.psum_tensor(name, [P, GROUP], F32))

        def sem(name):
            return ctx.enter_context(nc.semaphore("s3_" + name))

        ident = keep["ident"]
        B4 = 4
        PAST = N_PAGES * PAGE
        CH = PAST // GROUP
        PC = GROUP // PAGE
        w_gate = keep["w_gate"]
        stage, g_pre, zero = sb("stage3", [P, 2, D_MIX]), sb("g_pre3", [P, KC]), sb("zero3", [P, 1])
        qs = sb("qs", [NOPE, HEADS, SAMPLES])
        qra, qrb = sb("qra", [P, HEADS, SAMPLES]), sb("qrb", [P, HEADS, SAMPLES])
        q_abs = sb("q_abs", [P, HEADS, SAMPLES])
        q_rope = sb("q_rope", [P, PC, HEADS, SAMPLES])
        w_ukT = sb("w_ukT", [NOPE, HEADS, KV_RANK])
        w_uv = sb("w_uv3", [P, ATT_W])
        mask4 = sb("mask4", [P, DEC_SEQ])
        new_lat = sb("new_lat", [DEC_SEQ, DEC_BATCH, KV_RANK])
        new_tok = sb("new_tok", [SAMPLES, KV_RANK])
        new_latT = sb("new_latT", [P, SAMPLES])
        new_krT = sb("new_krT", [P, SAMPLES])
        lat = sb("lat", [P, B4, N_PAGES, KV_RANK])
        kr = sb("kr", [P, B4, N_PAGES, ROPE])
        qb = sb("qb", [P, B4, 1 + PC, HEADS * DEC_SEQ])
        now_latT, now_krT = sb("now_latT", [P, B4 * DEC_SEQ]), sb("now_krT", [P, B4 * DEC_SEQ])
        now_lat = sb("now_lat", [DEC_SEQ, B4, KV_RANK])
        latT = sb("latT", [P, 2, PAST])
        krT = sb("krT", [P, 2, CH, PAGE])
        prob = sb("prob3", [P, PAST + P])
        probT = sb("probT", [P, N_PAGES + 1, P])
        snew = sb("snew", [P, DEC_SEQ])
        mx, nm, dsum, den = sb("mx3", [P, CH + 1]), sb("nm3", [P, 2]), sb("dsum3", [P, CH + 1]), sb("den3", [P, 2])
        o_lat, o_latT = sb("o_lat", [P, KV_RANK]), sb("o_latT", [P, P])
        o_att = sb("o_att", [VDIM, HEADS, B4 * DEC_SEQ])
        sc = [ps(f"s3sc{i}") for i in range(CH)]
        sn = ps("s3new")
        tp = [ps(f"s3tp{i}") for i in range(2)]
        acc = ps("s3acc")
        s = {n: sem(n) for n in ("const", "lat_free", "prep", "prepd", "qabs", "latT", "tdone", "t_free", "krT", "sdone", "snew", "mx", "nm",
                                 "exp", "den", "pT", "pTd", "pv", "olat", "olT", "olTd", "att", "oatt", "out", "zero", "sfree", "w", "g_pre")}
        w_ld = [sem(f"w_ld{i}") for i in range(2)]
        NQ = B4 * 2 + 3
        NC_ = 15 * 16
        ld = [sem(f"ld{i}") for i in range(B4)]
        NTR = B4 * (CH + 1)
        NPT = (N_PAGES + 1 + 3) // 4
        TB = NTR + NPT + 1
        assert TB % 2 == 0
        kdims = (HEADS, SAMPLES)

        with nc.Block() as block:
            @block.sync
            def _(sp):
                def pages(i, b):
                    sample = bass.ds(i * B4 + b, 1)
                    for g in range(2):
                        k = slice(g * N_PAGES // 2, (g + 1) * N_PAGES // 2)
                        sp.dma_start(lat[:, b, k, :], a["LAT"][sample, k, :, :].rearrange("o k p n -> p (o k) n")).then_inc(ld[b], 16)
                    sp.dma_start(kr[:, b, :, :], a["KR"][sample, :, :, :].rearrange("o k p n -> p (o k) n")).then_inc(ld[b], 16)

                pages(0, 0)
                q_s = a["QT"][0:HEADS * P, SEQ:SEQ + SAMPLES].rearrange("(h p) n -> p h n", p=P)
                sp.dma_start(qs[:, :, :], q_s[0:NOPE, :, :]).then_inc(s["const"], 16)
                for rows, dst in ((q_s[NOPE:NOPE + ROPE, :, :], qra), (q_s[NOPE + ROPE:, :, :], qrb)):
                    for j in range(PC):
                        sp.dma_start(dst[j * ROPE:(j + 1) * ROPE, :, :], rows).then_inc(s["const"], 16)
                sp.dma_start(w_ukT[:, :, :], a["w_ukT"]).then_inc(s["const"], 16)
                sp.dma_start(w_uv[:, :], a["w_uv"]).then_inc(s["const"], 16)
                sp.dma_start(mask4[:, :], a["causal4"]).then_inc(s["const"], 16)
                sp.dma_start(new_tok[:, :], a["ckv_s"]).then_inc(s["const"], 16)
                sp.dma_start(new_lat[:, :, :], a["ckv_s"].rearrange("(b l) n -> l b n", l=DEC_SEQ)).then_inc(s["const"], 16)
                sp.wait_ge(s["zero"], 2)
                sp.dma_start(new_krT[0:ROPE, :], a["KRT"][0:ROPE, SEQ:SEQ + SAMPLES]).then_inc(s["const"], 16)
                for i in range(2):
                    for b in range(B4):
                        if i == 0 and b == 0:
                            continue
                        if i:
                            sp.wait_ge(s["lat_free"], b + 1)
                        pages(i, b)
                    sp.wait_ge(s["oatt"], i + 1)
                    sp.dma_start(a["Y"][0:ATT_W, bass.ds(i * (B4 * DEC_SEQ) + SEQ, B4 * DEC_SEQ)].rearrange("(h d) n -> d h n", d=VDIM),
                                 o_att[:, :, :]).then_inc(s["out"], 16)
                sp.wait_ge(s["out"], 48)

            @block.gpsimd
            def _(pool):
                pool.memset(q_rope[:, :, :, :], 0.0).then_inc(s["zero"], 1)
                pool.memset(new_krT[:, :], 0.0).then_inc(s["zero"], 1)
                pool.memset(prob[:, PAST:], 0.0).then_inc(s["zero"], 1)
                pool.sem_inc(s["t_free"], 2)
                pool.sem_inc(s["sfree"], 1)
                pool.sem_inc(s["out"], 16)
                pool.memset(zero[:, :], 0.0).then_inc(s["w"], 1)
                pool.dma_start(g_pre[:, :], a["norm_pre_c"]).then_inc(s["g_pre"], 16)

                def load_w(k):
                    pool.dma_start(stage[:, k % 2, :], a["w_gate"][k * P:(k + 1) * P, :]).then_inc(w_ld[k % 2], 16)

                load_w(0)
                load_w(1)
                pool.wait_ge(s["g_pre"], 16)
                pool.wait_ge(s["w"], 1)
                for k in range(KC):
                    raw = stage[:, k % 2, :]
                    pool.wait_ge(w_ld[k % 2], 16 * (k // 2) + 16)
                    pool.tensor_tensor(raw, raw, spread(g_pre[:, k:k + 1], raw), ALU.mult).then_inc(s["w"], 1)
                    pool.wait_ge(s["w"], 3 * k + 2)
                    pool.tensor_tensor(w_gate[:, 0, k, :], raw, spread(zero[:, :], raw), ALU.add).then_inc(s["w"], 1)
                    pool.wait_ge(s["w"], 3 * k + 3)
                    pool.tensor_tensor(w_gate[:, 1, k, :], raw, f32(w_gate[:, 0, k, :]), ALU.subtract).then_inc(s["w"], 1)
                    if k + 2 < KC:
                        pool.wait_ge(s["w"], 3 * k + 4)
                        load_w(k + 2)
                pool.wait_ge(s["w"], 3 * KC + 1)

            @block.tensor
            def _(pe):
                pe.wait_ge(s["const"], NC_)
                for h in range(HEADS):
                    last = pe.matmul(acc[:, h * SAMPLES:(h + 1) * SAMPLES], w_ukT[:, h, :], qs[:, h, :], start=True, stop=True)
                last.then_inc(s["prep"], 1)
                pe.transpose(sn[:, 0:SAMPLES], new_tok[:, :], ident[0:SAMPLES, 0:SAMPLES]).then_inc(s["prep"], 1)
                pe.wait_ge(s["prepd"], PC + 2)

                with pe.Fori(0, 2) as i:
                    use = [0]

                    def t_bank():
                        u = use[0]
                        use[0] += 1
                        pe.wait_ge(s["t_free"], i * TB + u + 1)
                        return tp[u % 2]

                    for b in range(B4):
                        pe.wait_ge(ld[b], i * 48 + 48)
                        for c in range(CH):
                            bank = t_bank()
                            for k in range(PC):
                                last = pe.transpose(bank[:, k * P:(k + 1) * P], lat[:, b, c * PC + k, :], ident[:, :])
                            last.then_inc(s["tdone"], 1)
                        bank = t_bank()
                        for c in range(CH):
                            last = pe.transpose(bank[:, c * P:(c + 1) * P], kr[:, b, c * PC:(c + 1) * PC, :].rearrange("p k r -> p (k r)"), ident[:, :])
                        last.then_inc(s["tdone"], 1)
                        if b == 0:
                            pe.wait_ge(s["qabs"], i * NQ + NQ)
                            pe.wait_ge(s["sfree"], i + 1)
                        row = slice(b * SAMPLES, (b + 1) * SAMPLES)
                        pe.wait_ge(s["latT"], i * NTR + (b + 1) * (CH + 1))
                        tok = slice(b * DEC_SEQ, (b + 1) * DEC_SEQ)
                        for c in range(CH):
                            pe.matmul(sc[c][row, :], qb[:, b, 0, :], latT[:, b % 2, c * GROUP:(c + 1) * GROUP], start=True, stop=False)
                            for j in range(PC):
                                last = pe.matmul(sc[c][row, j * P:(j + 1) * P], qb[:, b, 1 + j, :], krT[:, b % 2, c, :], start=False, stop=(j == PC - 1))
                            last.then_inc(s["sdone"], 1)
                        pe.matmul(sn[row, 0:DEC_SEQ], qb[:, b, 0, :], now_latT[:, tok], start=True, stop=False)
                        pe.matmul(sn[row, 0:DEC_SEQ], qb[:, b, 1, :], now_krT[:, tok], start=False, stop=True).then_inc(s["sdone"], 1)
                    pe.wait_ge(s["exp"], i * (CH + 1) + CH + 1)
                    for g in range(NPT):
                        bank = t_bank()
                        for k in range(4 * g, min(4 * g + 4, N_PAGES + 1)):
                            last = pe.transpose(bank[:, (k % 4) * P:(k % 4 + 1) * P], prob[:, k * P:(k + 1) * P], ident[:, :])
                        last.then_inc(s["tdone"], 1)
                    pe.wait_ge(s["pT"], i * NPT + NPT)
                    for b in range(B4):
                        row = slice(b * SAMPLES, (b + 1) * SAMPLES)
                        for pg in range(N_PAGES):
                            pe.matmul(acc[row, 0:KV_RANK], probT[:, pg, row], lat[:, b, pg, :], start=(pg == 0), stop=False)
                        pe.matmul(acc[row, 0:KV_RANK], probT[0:DEC_SEQ, N_PAGES, row],
                                  now_lat[:, b, :], start=False, stop=True).then_inc(s["lat_free"], 1)
                    pe.wait_ge(s["olat"], i + 1)
                    bank = t_bank()
                    pe.transpose(bank[:, 0:P], o_lat[:, :], ident[:, :]).then_inc(s["tdone"], 1)
                    pe.wait_ge(s["olT"], i + 1)
                    oT = o_latT[:, :].rearrange("p (b h l) -> p b h l", b=B4, h=HEADS)
                    for h in range(HEADS):
                        last = pe.matmul(acc[0:VDIM, GROUP // 2 + h * 16:GROUP // 2 + (h + 1) * 16].rearrange("p (b l) -> p b l", l=DEC_SEQ), w_uv[:, h * VDIM:(h + 1) * VDIM],
                                         oT[:, :, h, :], start=True, stop=True)
                    last.then_inc(s["att"], 1)
                    assert use[0] == TB, (use, TB)

            @block.scalar
            def _(act):
                act.wait_ge(s["zero"], 3)
                with act.Fori(0, 2) as i:
                    for c in range(CH + 1):
                        if c == 0:
                            act.wait_ge(s["nm"], i + 1)
                        src = sc[c][:, :] if c < CH else snew[:, :]
                        dst = prob[:, c * GROUP:(c + 1) * GROUP] if c < CH else prob[:, PAST:PAST + DEC_SEQ]
                        act.activation(dst, src, ACT.Exp, bias=nm[:, 1:2], accum_out=dsum[:, c:c + 1]).then_inc(s["exp"], 1)

            @block.vector
            def _(dve):
                dve.wait_ge(s["prep"], 2)
                dve.wait_ge(s["zero"], 3)
                dve.tensor_copy(q_abs[:, :, :], acc[:, 0:HEADS * SAMPLES].rearrange("p (h n) -> p h n", h=HEADS)).then_inc(s["prepd"], 1)
                dve.tensor_copy(new_latT[:, :], sn[:, 0:SAMPLES]).then_inc(s["prepd"], 1)
                dve.wait_ge(s["const"], NC_)
                for j in range(PC):
                    r = slice(j * ROPE, (j + 1) * ROPE)
                    dve.tensor_tensor(q_rope[r, j, :, :], qra[r, :, :], qrb[r, :, :], ALU.add).then_inc(s["prepd"], 1)
                dve.wait_ge(s["prepd"], PC + 2)
                with dve.Fori(0, 2) as i:
                    for b in range(B4):
                        tok = bass.ds(i * (B4 * DEC_SEQ) + b * DEC_SEQ, DEC_SEQ)
                        dve.tensor_copy(qb[:, b, 0, :].rearrange("p (h l) -> p h l", l=DEC_SEQ), q_abs[:, :, tok]).then_inc(s["qabs"], 1)
                        dve.tensor_copy(qb[:, b, 1:, :].rearrange("p j (h l) -> p j h l", l=DEC_SEQ), q_rope[:, :, :, tok]).then_inc(s["qabs"], 1)
                    now = bass.ds(i * (B4 * DEC_SEQ), B4 * DEC_SEQ)
                    dve.tensor_copy(now_latT[:, :], new_latT[:, now]).then_inc(s["qabs"], 1)
                    dve.tensor_copy(now_krT[:, :], new_krT[:, now]).then_inc(s["qabs"], 1)
                    dve.tensor_copy(now_lat[:, :, :], new_lat[:, bass.ds(i * B4, B4), :]).then_inc(s["qabs"], 1)
                    use = [0]

                    def from_bank(out, cols_, done):
                        u = use[0]
                        use[0] += 1
                        dve.wait_ge(s["tdone"], i * TB + u + 1)
                        dve.tensor_copy(out, tp[u % 2][:, 0:cols_]).then_inc(s[done], 1)
                        return u

                    def release(name, value):
                        dve.wait_ge(s[name], value)
                        dve.sem_inc(s["t_free"], 1)

                    for b in range(B4):
                        if b >= 2:
                            dve.wait_ge(s["sdone"], i * (B4 * (CH + 1)) + (b - 1) * (CH + 1))
                        for c in range(CH):
                            from_bank(latT[:, b % 2, c * GROUP:(c + 1) * GROUP], GROUP, "latT")
                            release("latT", i * NTR + b * (CH + 1) + c + 1)
                        from_bank(krT[:, b % 2, :, :].rearrange("p c n -> p (c n)"), GROUP, "latT")
                        release("latT", i * NTR + (b + 1) * (CH + 1))
                    dve.wait_ge(s["sdone"], (i + 1) * (B4 * (CH + 1)))
                    dve.tensor_tensor(snew[:, :], sn[:, 0:DEC_SEQ], mask4[:, :], ALU.add).then_inc(s["snew"], 1)
                    for c in range(CH):
                        dve.reduce_max(mx[:, c:c + 1], sc[c][:, :], AXX).then_inc(s["mx"], 1)
                    dve.wait_ge(s["snew"], i + 1)
                    dve.reduce_max(mx[:, CH:CH + 1], snew[:, :], AXX).then_inc(s["mx"], 1)
                    dve.wait_ge(s["mx"], i * (CH + 2) + CH + 1)
                    dve.reduce_max(nm[:, 0:1], mx[:, :], AXX).then_inc(s["mx"], 1)
                    dve.wait_ge(s["mx"], (i + 1) * (CH + 2))
                    dve.tensor_scalar(nm[:, 1:2], nm[:, 0:1], -1.0, None, ALU.mult).then_inc(s["nm"], 1)
                    dve.wait_ge(s["exp"], (i + 1) * (CH + 1))
                    dve.sem_inc(s["sfree"], 1)
                    dve.reduce_sum(den[:, 0:1], dsum[:, :], AXX).then_inc(s["den"], 1)
                    dve.wait_ge(s["den"], i * 2 + 1)
                    dve.reciprocal(den[:, 1:2], den[:, 0:1]).then_inc(s["den"], 1)
                    for g in range(NPT):
                        k0, k1 = 4 * g, min(4 * g + 4, N_PAGES + 1)
                        from_bank(probT[:, k0:k1, :].rearrange("p k n -> p (k n)"), (k1 - k0) * P, "pT")
                        release("pT", i * NPT + g + 1)
                    dve.wait_ge(s["lat_free"], (i + 1) * B4)
                    dve.wait_ge(s["den"], i * 2 + 2)
                    dve.tensor_scalar(o_lat[:, :], acc[:, 0:KV_RANK], den[:, 1:2], None, ALU.mult).then_inc(s["olat"], 1)
                    from_bank(o_latT[:, :], P, "olT")
                    release("olT", i + 1)
                    dve.wait_ge(s["att"], i + 1)
                    dve.wait_ge(s["out"], i * 16 + 16)
                    dve.tensor_copy(o_att[:, :, :], acc[0:VDIM, GROUP // 2:GROUP // 2 + HEADS * 16].rearrange("p (h n) -> p h n", h=HEADS)).then_inc(s["oatt"], 1)


def stage4(nc, a, keep):
    ctx = ExitStack()
    with ctx:
        def sb(name, shape, dt=F32):
            return ctx.enter_context(nc.sbuf_tensor(name, shape, dt))

        def sem(name):
            return ctx.enter_context(nc.semaphore("s4_" + name))

        ident, rstd_all, rden = keep["ident"], keep["rstd_all"], keep["rden"]
        NT = SEQ // P
        MC = D_MIX // P
        WB = 2
        w_gate = keep["w_gate"]
        w_out = sb("w_out", [P, 2, MC, D_MODEL], F32R)
        g_post = sb("g_post", [P, D_MODEL])
        half, eps = sb("half4", [P, 1]), sb("eps4", [P, 1])
        stage = sb("stage4", [P, WB, D_MODEL])
        xraw = sb("xraw", [P, 2, KC, P])
        hT = sb("hT4", [P, 2, 2, KC, P], F32R)
        gate = sb("gate", [P, D_MIX])
        yt = sb("yt", [P, 2, MC, P])
        mf = sb("mf", [P, MC, P])
        m2 = sb("m2", [P, 2, MC, P], F32R)
        xt = sb("xt", [P, 2, D_MODEL])
        ot = sb("ot", [P, 2, D_MODEL])
        junk = sb("junk4", [P, GROUP], BF16)
        rs = sb("rs", [P, 2])
        sq, rq = sb("sq4", [P, 2, 2]), sb("rq4", [P, 2, 2])
        mm = [ctx.enter_context(nc.psum_tensor(f"m4_{i}", [P, GROUP], F32)) for i in range(4)]
        tp = [ctx.enter_context(nc.psum_tensor(f"t4_{i}", [P, GROUP], F32)) for i in range(2)]
        s = {n: sem(n) for n in ("xT_free", "split", "cols", "gates", "silu", "tr", "yr", "mix", "hi", "pair", "outs",
                                 "square", "rms", "mid", "final", "o_done", "gate_free", "out_free", "mixed", "g_post", "init", "x_hi", "w_hi", "w_lo")}
        staged = [sem(f"staged{i}") for i in range(WB)]
        x_ld, xt_ld, y_ld, stored = ([sem(f"{n}{i}") for i in range(2)] for n in ("x_ld", "xt_ld", "y_ld", "stored"))

        class Tile:

            def __init__(self, i, hf, smp=False):
                self.t, self.b, self.smp = i * 2 + hf, hf, smp
                self.i = i
                self.rows = SAMPLES if smp else P

        def over_tiles(eng, f):
            with eng.Fori(0, NT // 2) as i:
                for hf in range(2):
                    f(Tile(i, hf))
            f(Tile(NT // 2, 0, True))

        with nc.Block() as block:
            @block.sync
            def _(sp):
                def load_x(t, b, wait=True):
                    if wait:
                        sp.wait_ge(s["xT_free"], t - 1)
                    sp.dma_start(xraw[:, b, :, :], a["xT"][:, bass.ds(t * P, P)].rearrange("(k p) n -> p k n", p=P)).then_inc(x_ld[b], 16)

                def store(t, n, b):
                    sp.wait_ge(s["o_done"], t + 1)
                    sp.dma_start(a["y"][bass.ds(t * P, n), :], ot[0:n, b, :]).then_inc(stored[b], 16)

                def tile(T, ahead=True, back=True):
                    n = T.rows
                    if ahead:
                        load_x(T.t + 2, T.b)
                    if back:
                        sp.wait_ge(s["mixed"], T.t - 1)
                    sp.dma_start(yt[:, T.b, :, 0:n], a["Y"][:, bass.ds(T.t * P, n)].rearrange("(k p) n -> p k n", p=P)).then_inc(y_ld[T.b], 16)
                    if back:
                        store(T.t - 2, P, T.b)
                    sp.dma_start(xt[0:n, T.b, :], a["x"][bass.ds(T.t * P, n), :]).then_inc(xt_ld[T.b], 16)

                load_x(0, 0, False)
                load_x(1, 1, False)
                sp.dma_start(g_post[:, :], a["norm_post"].broadcast_to([P, D_MODEL])).then_inc(s["g_post"], 16)
                for k in range(MC):
                    if k >= WB:
                        sp.wait_ge(s["w_lo"], k - WB + 1)
                    sp.dma_start(stage[:, k % WB, :], a["w_out"][k * P:(k + 1) * P, :]).then_inc(staged[k % WB], 16)
                    if k == WB - 1:
                        tile(Tile(0, 0), back=False)
                        tile(Tile(0, 1), back=False)
                with sp.Fori(1, NT // 2 - 1) as i:
                    for hf in range(2):
                        tile(Tile(i, hf))
                tile(Tile(NT // 2 - 1, 0))
                tile(Tile(NT // 2 - 1, 1), ahead=False)
                tile(Tile(NT // 2, 0, True), ahead=False)
                store(NT - 1, P, 1)
                store(NT, SAMPLES, 0)
                sp.wait_ge(stored[0], 16 * (NT // 2 + 2))
                sp.wait_ge(stored[1], 16 * (NT // 2 + 1))

            @block.gpsimd
            def _(pool):
                pool.memset(half[:, :], -0.5).then_inc(s["init"], 1)
                pool.wait_ge(s["init"], 1)
                pool.memset(eps[:, :], EPS).then_inc(s["init"], 1)
                pool.wait_ge(s["init"], 2)
                pool.sem_inc(s["gate_free"], 2)
                pool.sem_inc(s["out_free"], 2)
                for b in stored:
                    pool.sem_inc(b, 16)

                def split(t, b):
                    pool.wait_ge(s["x_hi"], t + 1)
                    pool.tensor_tensor(hT[:, b, 1, :, :], xraw[:, b, :, :], f32(hT[:, b, 0, :, :]), ALU.subtract).then_inc(s["split"], 1)
                    pool.wait_ge(s["split"], t + 1)
                    pool.sem_inc(s["xT_free"], 1)

                def post(T):
                    n, b = T.rows, T.b
                    pool.wait_ge(s["square"], T.t * 2 + 2)
                    pool.tensor_tensor(rq[0:n, b, 0:1], sq[0:n, b, 0:1], sq[0:n, b, 1:2], ALU.add).then_inc(s["mid"], 1)
                    pool.wait_ge(s["mid"], T.t * 2 + 1)
                    pool.tensor_tensor(rq[0:n, b, 0:1], rq[0:n, b, 0:1], eps[0:n, :], ALU.add).then_inc(s["mid"], 1)
                    pool.wait_ge(s["mid"], T.t * 2 + 2)
                    pool.tensor_tensor(rq[0:n, b, 1:2], rq[0:n, b, 0:1], half[0:n, :], ALU.pow).then_inc(s["rms"], 1)
                    pool.wait_ge(s["final"], T.t * 2 + 2)
                    pool.wait_ge(xt_ld[b], T.i * 16 + 16)
                    pool.tensor_tensor(ot[0:n, b, :], ot[0:n, b, :], xt[0:n, b, :], ALU.add).then_inc(s["o_done"], 1)

                split(0, 0)
                split(1, 1)
                with pool.Fori(0, NT // 2 - 1) as i:
                    for hf in range(2):
                        T = Tile(i, hf)
                        split(T.t + 2, hf)
                        post(T)
                split(NT, 0)
                post(Tile(NT // 2 - 1, 0))
                post(Tile(NT // 2 - 1, 1))
                post(Tile(NT // 2, 0, True))

            @block.tensor
            def _(pe):
                def passes(out, w, x, n):
                    for k in range(n):
                        for q, (pw_, px) in enumerate(PASSES):
                            last = pe.matmul(out, w(pw_, k), x(px, k), start=(k == 0 and q == 0), stop=(k == n - 1 and q == 2))
                    return last

                def gates(t, b):
                    pe.wait_ge(s["split"], t + 1)
                    pe.wait_ge(s["gate_free"], t * 2 + 2)
                    for c in range(2):
                        ins = passes(mm[c][:, :], lambda i, k: hT[:, b, i, k, :], lambda i, k: w_gate[:, i, k, c * GROUP:(c + 1) * GROUP], KC)
                        ins.then_inc(s["gates"], 1)

                def transposes(T):
                    n, b = T.rows, T.b
                    for c in (1, 0):
                        if c:
                            pe.wait_ge(s["silu"], T.t * 2 + 2)
                        else:
                            pe.wait_ge(s["yr"], T.t + 1)
                        for k in range(4):
                            ins = pe.transpose(tp[c][:, k * P:k * P + n], gate[0:n, (4 * c + k) * P:(4 * c + k + 1) * P], ident[0:n, 0:n])
                        ins.then_inc(s["tr"], 1)

                def outs(T):
                    n = T.rows
                    pe.wait_ge(s["w_lo"], MC)
                    pe.wait_ge(s["pair"], T.t * 2 + 2)
                    pe.wait_ge(s["out_free"], T.t * 2 + 2)
                    for c in range(2):
                        ins = passes(mm[2 + c][0:n, :], lambda i, k: m2[:, i, k, 0:n], lambda i, k: w_out[:, i, k, c * GROUP:(c + 1) * GROUP], MC)
                        ins.then_inc(s["outs"], 1)

                gates(0, 0)
                with pe.Fori(0, NT // 2) as i:
                    for hf in range(2):
                        T = Tile(i, hf)
                        transposes(T)
                        gates(T.t + 1, 1 - hf)
                        outs(T)
                T = Tile(NT // 2, 0, True)
                transposes(T)
                outs(T)

            @block.scalar
            def _(act):
                def silu(t, b):
                    for c in range(2):
                        act.wait_ge(s["gates"], t * 2 + c + 1)
                        act.activation(gate[:, c * GROUP:(c + 1) * GROUP], mm[c][:, :], ACT.Silu, scale=rs[:, b:b + 1]).then_inc(s["silu"], 1)
                    act.wait_ge(s["silu"], t * 2 + 2)
                    act.sem_inc(s["gate_free"], 2)

                def x_hi(T2, i, b):
                    act.activation(rs[:, b:b + 1], rstd_all[:, bass.ds(T2, 1)], ACT.Copy).then_inc(s["cols"], 1)
                    act.wait_ge(x_ld[b], i * 16 + 16)
                    act.activation(hT[:, b, 0, :, :], xraw[:, b, :, :], ACT.Copy).then_inc(s["x_hi"], 1)
                    act.wait_ge(s["x_hi"], T2 + 1)

                def hi(T):
                    for q, c in enumerate((1, 0)):
                        act.wait_ge(s["mix"], T.t * 2 + q + 1)
                        act.activation(m2[:, 0, 4 * c:4 * c + 4, 0:T.rows], mf[:, 4 * c:4 * c + 4, 0:T.rows], ACT.Copy).then_inc(s["hi"], 1)

                def squares(T):
                    n = T.rows
                    for c in range(2):
                        act.wait_ge(s["outs"], T.t * 2 + c + 1)
                        act.activation(junk[0:n, :], mm[2 + c][0:n, :], ACT.Square, scale=D_MODEL ** -0.5, accum_out=sq[0:n, T.b, c:c + 1]).then_inc(s["square"], 1)
                        act.wait_ge(s["square"], T.t * 2 + c + 1)

                x_hi(0, 0, 0)
                x_hi(1, 0, 1)
                for k in range(MC):
                    act.wait_ge(staged[k % WB], 16 * (k // WB) + 16)
                    act.activation(w_out[:, 0, k, :], stage[:, k % WB, :], ACT.Copy).then_inc(s["w_hi"], 1)
                silu(0, 0)

                def tile(T, ahead=True):
                    if ahead:
                        x_hi(T.t + 2, T.i + 1, T.b)
                    hi(T)
                    silu(T.t + 1, 1 - T.b)
                    squares(T)

                with act.Fori(0, NT // 2 - 1) as i:
                    for hf in range(2):
                        tile(Tile(i, hf))
                tile(Tile(NT // 2 - 1, 0))
                tile(Tile(NT // 2 - 1, 1), ahead=False)
                T = Tile(NT // 2, 0, True)
                hi(T)
                squares(T)

            @block.vector
            def _(dve):
                def divide(t):
                    dve.wait_ge(s["silu"], t * 2 + 1)
                    g4 = gate[:, 0:ATT_W].rearrange("p (h d) -> p h d", d=VDIM)
                    dve.tensor_tensor(g4, g4, rden[:, :, bass.ds(t, 1)].broadcast_to([P, HEADS, VDIM]), ALU.mult).then_inc(s["yr"], 1)

                def tile(T):
                    n, b = T.rows, T.b
                    dve.wait_ge(y_ld[b], T.i * 16 + 16)
                    for q, c in enumerate((1, 0)):
                        dve.wait_ge(s["tr"], T.t * 2 + 1 + q)
                        dve.tensor_tensor(mf[:, 4 * c:4 * c + 4, 0:n], tp[c][:, :].rearrange("p (k n) -> p k n", k=4)[:, :, 0:n],
                                          yt[:, b, 4 * c:4 * c + 4, 0:n], ALU.mult).then_inc(s["mix"], 1)
                    for q, c in enumerate((1, 0)):
                        dve.wait_ge(s["hi"], T.t * 2 + q + 1)
                        dve.tensor_tensor(m2[:, 1, 4 * c:4 * c + 4, 0:n], mf[:, 4 * c:4 * c + 4, 0:n], f32(m2[:, 0, 4 * c:4 * c + 4, 0:n]),
                                          ALU.subtract).then_inc(s["pair"], 1)
                    dve.wait_ge(s["mix"], T.t * 2 + 2)
                    dve.sem_inc(s["mixed"], 1)
                    if not T.smp:
                        divide(T.t + 1)
                    dve.wait_ge(s["rms"], T.t + 1)
                    dve.wait_ge(stored[b], T.i * 16 + 16)
                    for c in range(2):
                        dve.scalar_tensor_tensor(ot[0:n, b, c * GROUP:(c + 1) * GROUP], mm[2 + c][0:n, :], rq[0:n, b, 1:2],
                                                 g_post[0:n, c * GROUP:(c + 1) * GROUP], ALU.mult, ALU.mult).then_inc(s["final"], 1)
                    dve.wait_ge(s["final"], T.t * 2 + 2)
                    dve.sem_inc(s["out_free"], 2)

                for k in range(MC):
                    dve.wait_ge(s["w_hi"], k + 1)
                    dve.tensor_tensor(w_out[:, 1, k, :], stage[:, k % WB, :], f32(w_out[:, 0, k, :]), ALU.subtract).then_inc(s["w_lo"], 1)
                dve.wait_ge(s["g_post"], 16)
                divide(0)
                over_tiles(dve, tile)


def build(nc, a):
    with nc.sbuf_tensor("ident", [P, P], F32) as ident, nc.sbuf_tensor("rstd_all", [P, GROUPS * TILES + 1], F32) as rstd_all:
        keep = {"ident": ident, "rstd_all": rstd_all}
        stage1(nc, a, keep)
        nc.clear_and_free_semaphores(keep["stage1_sems"])
        nc.all_engine_barrier()
        with nc.sbuf_tensor("rden", [P, HEADS, GROUPS * TILES + 1], F32) as rden:
            keep["rden"] = rden
            stage2(nc, a, keep)
            with nc.sbuf_tensor("w_gate", [P, 2, KC, D_MIX], F32R) as w_gate:
                keep["w_gate"] = w_gate
                stage3(nc, a, keep)
                stage4(nc, a, keep)


def _columns(np, v, n):
    return np.ascontiguousarray(np.asarray(v).reshape(n, 128).T)


def _arrange(np, i):
    f = np.float32
    x = np.zeros((SEQ + GROUP, D_MODEL), f)
    x[:SEQ] = i["x_prompt"][0]
    x[SEQ:SEQ + SAMPLES] = i["x_sample"].reshape(SAMPLES, D_MODEL)
    w = i["w_in"][0]
    o_pool = TOK_COLS
    o_conv = o_pool + POOL_W
    o_gate = o_conv + 2 * CONV_W
    order = [w[:, :TOK_COLS]]
    for c in range(CC):
        order += [w[:, o_conv + CONV_W + c * P:o_conv + CONV_W + (c + 1) * P], w[:, o_conv + c * P:o_conv + (c + 1) * P]]
    order.append(w[:, o_pool:o_pool + POOL_W])
    uq = i["w_uq"][0].reshape(Q_RANK, HEADS, NOPE + ROPE)
    uq = np.concatenate([uq, uq[:, :, NOPE + HALF:], uq[:, :, NOPE:NOPE + HALF]], axis=2)
    gate_order = w[:, o_gate:]
    blocks = np.zeros((P, CC, P), f)
    for g in range(4):
        r = (g % 2) * 64
        blocks[r:r + 64, g // 2, r:r + 64] = i["pool_w"][0, g]
    dw = i["conv_dw"][0]
    windows = np.array([2, 4, 8, 16])
    win = np.repeat(windows, 64).reshape(CC, P).T
    cols = np.concatenate([
        _columns(np, i["norm_pre"][0], 8), _columns(np, i["q_norm"][0], 2), _columns(np, i["pool_scale"][0], 2),
        _columns(np, i["conv_ln_g"][0], 2), _columns(np, i["conv_ln_b"][0], 2), _columns(np, i["conv_b"][0], 2),
        (f(1) / win.astype(f)), dw.reshape(CONV_K, CC, P).transpose(2, 1, 0).reshape(P, CC * CONV_K)], axis=1)
    inv = (f(10000.0) ** (-np.arange(0, ROPE, 2, dtype=f) / f(ROPE))).astype(f)
    pos = np.arange(SEQ + SAMPLES)
    pos[SEQ:] = N_PAGES * PAGE + np.arange(SAMPLES) % DEC_SEQ
    ang = pos.astype(f)[:, None] * inv[None, :]
    cos, sin = np.cos(ang).astype(f), np.sin(ang).astype(f)
    scale = f((NOPE + ROPE) ** -0.5)
    cs_T = np.concatenate([np.full((SEQ + SAMPLES, NOPE), scale), cos * scale, cos * scale, -sin * scale, sin * scale], axis=1).T
    cs_tok = np.zeros(((GROUPS + 1) * GROUP, ROPE), f)
    cs_tok[:SEQ + SAMPLES] = np.concatenate([cos, sin], axis=1)
    cs_tok = cs_tok.reshape(GROUPS + 1, TILES, P, ROPE).transpose(0, 2, 1, 3)
    icnt = np.ones((GROUPS, UH)) * 1.0
    t = np.arange(GROUPS)[:, None] * GROUP + np.arange(UH)[None, :]
    icnt = 1.0 / np.minimum(t[None, :, None, :] + 1, win[:, None, :, None])
    return {
        "x": x, "xT": x.T, "w_in": np.concatenate(order, axis=1), "w_uq": uq.reshape(Q_RANK, HEADS * P),
        "w_uk": i["w_uk"][0].reshape(KV_RANK, HEADS * NOPE), "w_uv": i["w_uv"][0].reshape(KV_RANK, HEADS * VDIM),
        "cols": cols.astype(f), "kv_norm": i["kv_norm"][0].reshape(1, KV_RANK), "ident": np.eye(P, dtype=f),
        "cs_T": cs_T.astype(f), "cs_tok": cs_tok, "icnt": icnt.astype(f), "conv_pw": i["conv_pw"][0], "pool_w": blocks,
        "state_conv": i["state_conv"][0].reshape(DEC_BATCH, CONV_HIST, CC, P).transpose(3, 2, 0, 1),
        "state_pool": i["state_pool"][0].reshape(DEC_BATCH, POOL_HIST, CC, P).transpose(3, 2, 0, 1),
        "w_gate": gate_order, "w_out": i["w_out"][0], "norm_post": i["norm_post"][0].reshape(1, D_MODEL),
        "cache_ckv": i["cache_ckv"][0], "cache_krope": i["cache_krope"][0],
        "page_table": np.asarray(i["page_table"]).astype(np.int32).reshape(1, DEC_BATCH * N_PAGES),
        "w_ukT": i["w_uk"][0].transpose(2, 1, 0),
        "norm_pre_c": _columns(np, i["norm_pre"][0], 8),
        "causal": np.where(np.arange(P)[None, :] <= np.arange(P)[:, None], 0.0, -1e30).astype(f),
        "causal4": np.where(np.arange(DEC_SEQ)[None, :] <= (np.arange(P) % DEC_SEQ)[:, None], 0.0, -1e30).astype(f),
    }


_OUT = {"y": (SEQ + SAMPLES, D_MODEL), "ckv_p": (SEQ, KV_RANK), "krope_p": (SEQ, ROPE), "pool_p": (POOL_W, POOL_HIST),
        "conv_p": (CONV_W, CONV_HIST), "ckv_s": (SAMPLES, KV_RANK), "krope_s": (SAMPLES, ROPE),
        "pool_s": (P, CC, DEC_BATCH, POOL_HIST), "conv_s": (P, CC, DEC_BATCH, CONV_HIST)}
_SCRATCH = {"QT": (HEADS * P, SEQ + SAMPLES), "KT": (HEADS * NOPE, SEQ + SAMPLES), "KRT": (P - NOPE, SEQ + SAMPLES),
            "V": (SEQ + 4 * SAMPLES, ATT_W), "Y": (D_MIX, SEQ + SAMPLES), 
            "LAT": (DEC_BATCH, N_PAGES, PAGE, KV_RANK), "KR": (DEC_BATCH, N_PAGES, PAGE, ROPE)}


def program(nc, arrays, scratch_kind="Internal"):
    a = {n: nc.dram_tensor("in_" + n, v.shape, mybir.dt.from_np(v.dtype), kind="ExternalInput").ap() for n, v in arrays.items()}
    a |= {n: nc.dram_tensor("out_" + n, shape, F32, kind="ExternalOutput").ap() for n, shape in _OUT.items()}
    a |= {n: nc.dram_tensor(n, shape, F32, kind=scratch_kind).ap() for n, shape in _SCRATCH.items()}
    build(nc, a)


def kernel(**inputs):
    import concourse.bacc as bacc
    import numpy as np
    from concourse.bass_utils import run_bass_kernel_spmd

    inputs = {n: np.asarray(v) for n, v in inputs.items()}
    arrays = {n: np.ascontiguousarray(v) for n, v in _arrange(np, inputs).items()}
    nc = bacc.Bacc("TRN2", target_bir_lowering=False, num_devices=1)
    program(nc, arrays)
    r = run_bass_kernel_spmd(nc, [{"in_" + n: v for n, v in arrays.items()}], core_ids=[0]).results[0]
    o = {n: np.asarray(r["out_" + n]) for n in _OUT}

    def state(v):
        return np.ascontiguousarray(v.transpose(2, 3, 1, 0)).reshape(1, DEC_BATCH, v.shape[3], CC * P)

    return (o["y"][:SEQ].reshape(1, SEQ, D_MODEL), o["y"][SEQ:].reshape(DEC_BATCH, DEC_SEQ, D_MODEL),
            o["ckv_p"].reshape(1, 1, SEQ, KV_RANK), o["krope_p"].reshape(1, 1, SEQ, ROPE),
            np.ascontiguousarray(o["pool_p"].T)[None, None], np.ascontiguousarray(o["conv_p"].T)[None, None],
            o["ckv_s"].reshape(1, DEC_BATCH, DEC_SEQ, KV_RANK), o["krope_s"].reshape(1, DEC_BATCH, DEC_SEQ, ROPE),
            state(o["pool_s"]), state(o["conv_s"]))
```
